# Optimizing a Trainium2 kernel written in Bass

```python
import math
import jax
import jax.numpy as jnp
from jax import lax
import numpy as np

D_MODEL = 1024
BATCH = 1
SEQ = 512
DEPTH = 2

HEAD_DIM = 128
MIX = D_MODEL // 2
GM_CHUNK = 128
GM_HEADS = MIX // HEAD_DIM
S5_GROUP = 16
S5_GROUPS = MIX // S5_GROUP
S5_STATE = 64
S5_DT_MIN = 1e-3
S5_DT_MAX = 1e-1
ML_HEADS = MIX // HEAD_DIM
ML_CHUNK = 128
CONV_W = 4
MB_HEADS = MIX // HEAD_DIM
MB_BLOCK = 256
MB_TOPK = 3
MB_QBLOCK = 16
ROPE_THETA = 10000.0
N_MEM = 256
XA_HEADS = 4
XA_HEAD_DIM = D_MODEL // XA_HEADS
XA_DIM = XA_HEADS * XA_HEAD_DIM
N_GROUPS = 4
EXP_PER_GROUP = 4
N_EXPERTS = N_GROUPS * EXP_PER_GROUP
EXP_FF = D_MODEL // 4
EXP_TOPK = 2
EPS = 1e-6
N_EVEN = (DEPTH + 1) // 2
N_ODD = DEPTH // 2
EVEN_IN = 3 * MIX
ODD_IN = 7 * MIX + 2 * ML_HEADS

kernel_name = 'hybrid_gmlp_s5_mlstm_moba_hmoe'

def rmsnorm(x, g):
    xf = x.astype(jnp.float32)
    y = xf * lax.rsqrt(jnp.mean(xf * xf, axis=-1, keepdims=True) + EPS)
    return (y * g.astype(jnp.float32)).astype(x.dtype)

def layernorm(x, g):
    xf = x.astype(jnp.float32)
    xc = xf - jnp.mean(xf, axis=-1, keepdims=True)
    y = xc * lax.rsqrt(jnp.mean(xc * xc, axis=-1, keepdims=True) + EPS)
    return (y * g.astype(jnp.float32)).astype(x.dtype)

def split_heads(t, n_heads):
    b, s, w = t.shape
    return t.reshape(b, s, n_heads, w // n_heads).transpose(0, 2, 1, 3)

def merge_heads(t):
    b, h, s, d = t.shape
    return t.transpose(0, 2, 1, 3).reshape(b, s, h * d)

def rope(x):
    s, d = x.shape[-2], x.shape[-1]
    half = d // 2
    inv_freq = ROPE_THETA ** (-jnp.arange(half, dtype=jnp.float32) / half)
    ang = jnp.arange(s, dtype=jnp.float32)[:, None] * inv_freq[None, :]
    cos, sin = jnp.cos(ang), jnp.sin(ang)
    xf = x.astype(jnp.float32)
    x1, x2 = xf[..., :half], xf[..., half:]
    return jnp.concatenate([x1 * cos - x2 * sin, x1 * sin + x2 * cos], axis=-1).astype(x.dtype)

def gmlp_mixer(u, v, ws, bs, ln_g):
    b, s, _ = u.shape
    nc = s // GM_CHUNK
    vh = layernorm(v.reshape(b, s, GM_HEADS, HEAD_DIM), ln_g.reshape(GM_HEADS, HEAD_DIM))
    vh = vh.reshape(b, nc, GM_CHUNK, GM_HEADS, HEAD_DIM)
    causal = jnp.tril(jnp.ones((GM_CHUNK, GM_CHUNK), dtype=bool))
    w = jnp.where(causal[None], ws, jnp.zeros_like(ws))
    mixed = jnp.einsum('hts,bcshd->bcthd', w, vh) + bs.T[None, None, :, :, None]
    return u * mixed.reshape(b, s, MIX).astype(u.dtype)

def _linear_combine(e1, e2):
    a1, b1 = e1
    a2, b2 = e2
    return a1 * a2, a2 * b1 + b2

def s5_mixer(u, lam_re, lam_im, b_re, b_im, c_re, c_im, d_skip, log_step, w_glu, b_glu):
    f32 = jnp.float32
    bsz, s, _ = u.shape
    uf = u.astype(f32).reshape(bsz, s, S5_GROUPS, S5_GROUP)
    lam = lax.complex(lam_re.astype(f32), lam_im.astype(f32))
    step = jnp.exp(log_step.astype(f32))[:, None]
    lam_bar = jnp.exp(lam * step)
    b_mat = lax.complex(b_re.astype(f32), b_im.astype(f32))
    b_bar = ((lam_bar - 1.0) / lam)[..., None] * b_mat
    bu = jnp.einsum('bsgi,gpi->bsgp', uf.astype(jnp.complex64), b_bar)
    a = jnp.broadcast_to(lam_bar, bu.shape)
    _, states = lax.associative_scan(_linear_combine, (a, bu), axis=1)
    c_mat = lax.complex(c_re.astype(f32), c_im.astype(f32))
    y = jnp.einsum('bsgp,gip->bsgi', states, c_mat).real
    y = y + d_skip.astype(f32).reshape(S5_GROUPS, S5_GROUP) * uf
    y = jax.nn.gelu(y.reshape(bsz, s, MIX))
    return (y * jax.nn.sigmoid(y @ w_glu.astype(f32) + b_glu.astype(f32))).astype(u.dtype)

def causal_conv(x, w, b):
    c = x.shape[-1]
    y = lax.conv_general_dilated(x, w[:, None, :].astype(x.dtype), window_strides=(1,),
                                 padding=[(CONV_W - 1, 0)],
                                 dimension_numbers=('NWC', 'WIO', 'NWC'),
                                 feature_group_count=c)
    return y + b.astype(x.dtype)

def mlstm_chunkwise(q, k, v, ig, fg):
    bsz, h, s, d = q.shape
    L = ML_CHUNK
    nc = s // L
    q = q.reshape(bsz, h, nc, L, d)
    k = k.reshape(bsz, h, nc, L, d)
    v = v.reshape(bsz, h, nc, L, d)
    ii = ig.reshape(bsz, h, nc, L)
    bcum = jnp.cumsum(jax.nn.log_sigmoid(fg).reshape(bsz, h, nc, L), axis=-1)
    g = bcum[..., -1]
    a = g[..., None] - bcum + ii

    def step(carry, xs):
        c_st, n_st, m_st = carry
        kc, vc, ac, gc = xs
        m_new = jnp.maximum(gc + m_st, jnp.max(ac, axis=-1))
        w = jnp.exp(ac - m_new[..., None])
        decay = jnp.exp(gc + m_st - m_new)
        kw = kc * w[..., None]
        c_new = decay[..., None, None] * c_st + jnp.einsum('bhld,bhle->bhde', kw, vc)
        n_new = decay[..., None] * n_st + jnp.sum(kw, axis=2)
        return (c_new, n_new, m_new), (c_st, n_st, m_st)

    init = (jnp.zeros((bsz, h, d, d), jnp.float32), jnp.zeros((bsz, h, d), jnp.float32),
            jnp.zeros((bsz, h), jnp.float32))
    xs = (jnp.moveaxis(k, 2, 0), jnp.moveaxis(v, 2, 0), jnp.moveaxis(a, 2, 0), jnp.moveaxis(g, 2, 0))
    _, (cs, ns, ms) = lax.scan(step, init, xs)
    cs = jnp.moveaxis(cs, 0, 2)
    ns = jnp.moveaxis(ns, 0, 2)
    ms = jnp.moveaxis(ms, 0, 2)

    causal = jnp.tril(jnp.ones((L, L), dtype=bool))
    dlog = jnp.where(causal, bcum[..., :, None] - bcum[..., None, :] + ii[..., None, :], -jnp.inf)
    inter_log = bcum + ms[..., None]
    m_t = jnp.maximum(inter_log, jnp.max(dlog, axis=-1))
    dw = jnp.exp(dlog - m_t[..., None])
    inter_w = jnp.exp(inter_log - m_t)
    sc = jnp.einsum('bhctd,bhcsd->bhcts', q, k) * dw
    num = inter_w[..., None] * jnp.einsum('bhctd,bhcde->bhcte', q, cs) + jnp.einsum('bhcts,bhcse->bhcte', sc, v)
    den = inter_w * jnp.einsum('bhctd,bhcd->bhct', q, ns) + jnp.sum(sc, axis=-1)
    out = num / jnp.maximum(jnp.abs(den), jnp.exp(-m_t))[..., None]
    return out.reshape(bsz, h, s, d)

def mlstm_mixer(c_qk, c_v, c_o, c_if, conv_w, conv_b, hn_g):
    f32 = jnp.float32
    qk = jax.nn.silu(causal_conv(c_qk, conv_w, conv_b))
    q = split_heads(qk[..., :MIX], ML_HEADS).astype(f32)
    k = split_heads(qk[..., MIX:], ML_HEADS).astype(f32) * (HEAD_DIM ** -0.5)
    v = split_heads(c_v, ML_HEADS).astype(f32)
    ig = c_if[..., :ML_HEADS].astype(f32).transpose(0, 2, 1)
    fg = c_if[..., ML_HEADS:].astype(f32).transpose(0, 2, 1)
    hh = mlstm_chunkwise(q, k, v, ig, fg)
    hh = rmsnorm(hh, hn_g.reshape(ML_HEADS, 1, HEAD_DIM))
    return (merge_heads(hh) * jax.nn.sigmoid(c_o.astype(f32))).astype(c_v.dtype)

_gather_blocks = jax.vmap(jax.vmap(lambda blocks, ids: blocks[ids]))

def moba_attention(q, k, v):
    bsz, h, s, d = q.shape
    nb = -(-s // MB_BLOCK)
    pad = nb * MB_BLOCK - s
    kb = jnp.pad(k, ((0, 0), (0, 0), (0, pad), (0, 0))).reshape(bsz, h, nb, MB_BLOCK, d)
    vb = jnp.pad(v, ((0, 0), (0, 0), (0, pad), (0, 0))).reshape(bsz, h, nb, MB_BLOCK, d)
    kmean = jnp.mean(kb.astype(jnp.float32), axis=3)
    n_sel = min(MB_TOPK, nb - 1)
    scale = HEAD_DIM ** -0.5

    def q_block(i):
        start = i * MB_QBLOCK
        qb = lax.dynamic_slice_in_dim(q, start, MB_QBLOCK, axis=2).astype(jnp.float32)
        qpos = start + jnp.arange(MB_QBLOCK)
        own = start // MB_BLOCK
        k_own = lax.dynamic_index_in_dim(kb, own, axis=2, keepdims=False)
        v_own = lax.dynamic_index_in_dim(vb, own, axis=2, keepdims=False)
        kpos = own * MB_BLOCK + jnp.arange(MB_BLOCK)
        s_own = jnp.einsum('bhqd,bhkd->bhqk', qb, k_own) * scale
        s_own = jnp.where(kpos[None, :] <= qpos[:, None], s_own, -jnp.inf)
        if n_sel == 0:
            p = jax.nn.softmax(s_own, axis=-1)
            return jnp.einsum('bhqk,bhkd->bhqd', p, v_own)
        gate = jnp.einsum('bhqd,bhnd->bhqn', qb, kmean)
        gate = jnp.where(jnp.arange(nb) < own, gate, -jnp.inf)
        _, idx = lax.top_k(gate, n_sel)
        valid = idx < own
        k_sel = _gather_blocks(kb, idx)
        v_sel = _gather_blocks(vb, idx)
        s_sel = jnp.einsum('bhqd,bhqnkd->bhqnk', qb, k_sel) * scale
        s_sel = jnp.where(valid[..., None], s_sel, -jnp.inf)
        s_all = jnp.concatenate([s_own, s_sel.reshape(bsz, h, MB_QBLOCK, n_sel * MB_BLOCK)], axis=-1)
        p = jax.nn.softmax(s_all, axis=-1)
        p_own = p[..., :MB_BLOCK]
        p_sel = p[..., MB_BLOCK:].reshape(bsz, h, MB_QBLOCK, n_sel, MB_BLOCK)
        return (jnp.einsum('bhqk,bhkd->bhqd', p_own, v_own)
                + jnp.einsum('bhqnk,bhqnkd->bhqd', p_sel, v_sel))

    outs = lax.map(q_block, jnp.arange(s // MB_QBLOCK))
    return outs.transpose(1, 2, 0, 3, 4).reshape(bsz, h, s, d)

def moba_mixer(d_qkv, qn_g, kn_g):
    q = rope(rmsnorm(split_heads(d_qkv[..., :MIX], MB_HEADS), qn_g))
    k = rope(rmsnorm(split_heads(d_qkv[..., MIX:2 * MIX], MB_HEADS), kn_g))
    v = split_heads(d_qkv[..., 2 * MIX:], MB_HEADS)
    return merge_heads(moba_attention(q, k, v)).astype(d_qkv.dtype)

def even_mixer(xn, w_in, w_out, gm_ws, gm_bs, gm_ln_g, lam_re, lam_im, b_re, b_im, c_re, c_im,
               d_skip, log_step, w_glu, b_glu):
    z = xn @ w_in
    uv = jax.nn.gelu(z[..., :2 * MIX])
    ya = gmlp_mixer(uv[..., :MIX], uv[..., MIX:], gm_ws, gm_bs, gm_ln_g)
    yb = s5_mixer(z[..., 2 * MIX:], lam_re, lam_im, b_re, b_im, c_re, c_im, d_skip, log_step, w_glu, b_glu)
    return (jnp.concatenate([ya, yb], axis=-1) @ w_out).astype(xn.dtype)

def odd_mixer(xn, w_in, w_out, conv_w, conv_b, b_if, hn_g, qn_g, kn_g):
    z = xn @ w_in
    c_qk = z[..., :2 * MIX]
    c_v = z[..., 2 * MIX:3 * MIX]
    c_o = z[..., 3 * MIX:4 * MIX]
    c_if = z[..., 4 * MIX:4 * MIX + 2 * ML_HEADS] + b_if
    d_qkv = z[..., 4 * MIX + 2 * ML_HEADS:]
    yc = mlstm_mixer(c_qk, c_v, c_o, c_if, conv_w, conv_b, hn_g)
    yd = moba_mixer(d_qkv, qn_g, kn_g)
    return (jnp.concatenate([yc, yd], axis=-1) @ w_out).astype(xn.dtype)

def cross_attn(xn, mem_k, mem_v, wq, wo, qn_g, kn_g):
    q = rmsnorm(split_heads(xn @ wq, XA_HEADS), qn_g)
    k = rmsnorm(mem_k, kn_g)
    s = jnp.einsum('bhsd,bhmd->bhsm', q, k).astype(jnp.float32) * (XA_HEAD_DIM ** -0.5)
    p = jax.nn.softmax(s, axis=-1).astype(xn.dtype)
    o = jnp.einsum('bhsm,bhmd->bhsd', p, mem_v)
    return (merge_heads(o) @ wo).astype(xn.dtype)

def hier_moe(xn, w_grp, b_grp, w_exp, b_exp, w1, w3, w2):
    bsz, s, dm = xn.shape
    t = xn.reshape(-1, dm)
    grp_logits = (t @ w_grp + b_grp).astype(jnp.float32)
    grp_p = jax.nn.softmax(grp_logits, axis=-1)
    grp = jnp.argmax(grp_logits, axis=-1)
    exp_logits = (t @ w_exp + b_exp).astype(jnp.float32).reshape(-1, N_GROUPS, EXP_PER_GROUP)
    sel = jnp.take_along_axis(exp_logits, grp[:, None, None], axis=1)[:, 0]
    top_v, top_i = lax.top_k(sel, EXP_TOPK)
    w_tok = jax.nn.softmax(top_v, axis=-1) * jnp.take_along_axis(grp_p, grp[:, None], axis=1)
    eid = grp[:, None] * EXP_PER_GROUP + top_i
    gate = jnp.sum(jax.nn.one_hot(eid, N_EXPERTS, dtype=jnp.float32) * w_tok[..., None], axis=1)
    hid = jax.nn.silu(jnp.einsum('td,edf->tef', t, w1)) * jnp.einsum('td,edf->tef', t, w3)
    hid = hid * gate[..., None].astype(hid.dtype)
    y = hid.reshape(t.shape[0], N_EXPERTS * EXP_FF) @ w2.reshape(N_EXPERTS * EXP_FF, dm)
    return y.reshape(bsz, s, dm).astype(xn.dtype)

def setup_inputs(seed: int = 0) -> dict:
    key = jax.random.key(seed)
    it = iter(jax.random.split(key, 48))
    f32 = jnp.float32

    def nrm(shape, fan_in):
        return jax.random.normal(next(it), shape, f32) * (fan_in ** -0.5)

    def gain(shape):
        return 1.0 + 0.05 * jax.random.normal(next(it), shape, f32)

    def small(shape, sc=0.01):
        return sc * jax.random.normal(next(it), shape, f32)

    L, NE, NO = DEPTH, N_EVEN, N_ODD
    x = jax.random.normal(next(it), (BATCH, SEQ, D_MODEL), f32)
    mem = jax.random.normal(next(it), (BATCH, N_MEM, D_MODEL), f32)
    mem_norm_g = gain((D_MODEL,))
    w_mem_kv = nrm((D_MODEL, 2 * XA_DIM), D_MODEL)
    norm_mix_g = gain((L, D_MODEL))
    norm_xa_g = gain((L, D_MODEL))
    norm_ffn_g = gain((L, D_MODEL))
    xa_wq = nrm((L, D_MODEL, XA_DIM), D_MODEL)
    xa_wo = nrm((L, XA_DIM, D_MODEL), XA_DIM)
    xa_qn_g = gain((L, XA_HEAD_DIM))
    xa_kn_g = gain((L, XA_HEAD_DIM))
    moe_w_grp = nrm((L, D_MODEL, N_GROUPS), D_MODEL)
    moe_b_grp = small((L, N_GROUPS))
    moe_w_exp = nrm((L, D_MODEL, N_EXPERTS), D_MODEL)
    moe_b_exp = small((L, N_EXPERTS))
    moe_w1 = nrm((L, N_EXPERTS, D_MODEL, EXP_FF), D_MODEL)
    moe_w3 = nrm((L, N_EXPERTS, D_MODEL, EXP_FF), D_MODEL)
    moe_w2 = nrm((L, N_EXPERTS, EXP_FF, D_MODEL), EXP_FF)
    ev_w_in = nrm((NE, D_MODEL, EVEN_IN), D_MODEL)
    ev_w_out = nrm((NE, 2 * MIX, D_MODEL), 2 * MIX)
    gm_ws = nrm((NE, GM_HEADS, GM_CHUNK, GM_CHUNK), GM_CHUNK)
    gm_bs = 1.0 + small((NE, GM_HEADS, GM_CHUNK), 0.05)
    gm_ln_g = gain((NE, MIX))
    s5_lam_re = -0.5 + small((NE, S5_GROUPS, S5_STATE))
    s5_lam_im = (jnp.pi * jnp.arange(S5_STATE, dtype=f32))[None, None, :] + small((NE, S5_GROUPS, S5_STATE))
    s5_b_re = nrm((NE, S5_GROUPS, S5_STATE, S5_GROUP), 2 * S5_GROUP)
    s5_b_im = nrm((NE, S5_GROUPS, S5_STATE, S5_GROUP), 2 * S5_GROUP)
    s5_c_re = nrm((NE, S5_GROUPS, S5_GROUP, S5_STATE), 2 * S5_STATE)
    s5_c_im = nrm((NE, S5_GROUPS, S5_GROUP, S5_STATE), 2 * S5_STATE)
    s5_d = jax.random.normal(next(it), (NE, MIX), f32)
    s5_log_step = jax.random.uniform(next(it), (NE, S5_GROUPS), f32,
                                     minval=math.log(S5_DT_MIN), maxval=math.log(S5_DT_MAX))
    s5_w_glu = nrm((NE, MIX, MIX), MIX)
    s5_b_glu = small((NE, MIX))
    od_w_in = nrm((NO, D_MODEL, ODD_IN), D_MODEL)
    od_w_out = nrm((NO, 2 * MIX, D_MODEL), 2 * MIX)
    ml_conv_w = nrm((NO, CONV_W, 2 * MIX), CONV_W)
    ml_conv_b = small((NO, 2 * MIX))
    ml_b_if = jnp.concatenate([small((NO, ML_HEADS), 0.1),
                               jnp.linspace(3.0, 6.0, ML_HEADS, dtype=f32)[None, :] + small((NO, ML_HEADS))], axis=-1)
    ml_hn_g = gain((NO, MIX))
    mb_qn_g = gain((NO, HEAD_DIM))
    mb_kn_g = gain((NO, HEAD_DIM))
    return {'x': x, 'mem': mem, 'mem_norm_g': mem_norm_g, 'w_mem_kv': w_mem_kv,
            'norm_mix_g': norm_mix_g, 'norm_xa_g': norm_xa_g, 'norm_ffn_g': norm_ffn_g,
            'xa_wq': xa_wq, 'xa_wo': xa_wo, 'xa_qn_g': xa_qn_g, 'xa_kn_g': xa_kn_g,
            'moe_w_grp': moe_w_grp, 'moe_b_grp': moe_b_grp, 'moe_w_exp': moe_w_exp, 'moe_b_exp': moe_b_exp,
            'moe_w1': moe_w1, 'moe_w3': moe_w3, 'moe_w2': moe_w2,
            'ev_w_in': ev_w_in, 'ev_w_out': ev_w_out, 'gm_ws': gm_ws, 'gm_bs': gm_bs, 'gm_ln_g': gm_ln_g,
            's5_lam_re': s5_lam_re, 's5_lam_im': s5_lam_im, 's5_b_re': s5_b_re, 's5_b_im': s5_b_im,
            's5_c_re': s5_c_re, 's5_c_im': s5_c_im, 's5_d': s5_d, 's5_log_step': s5_log_step,
            's5_w_glu': s5_w_glu, 's5_b_glu': s5_b_glu,
            'od_w_in': od_w_in, 'od_w_out': od_w_out, 'ml_conv_w': ml_conv_w, 'ml_conv_b': ml_conv_b,
            'ml_b_if': ml_b_if, 'ml_hn_g': ml_hn_g, 'mb_qn_g': mb_qn_g, 'mb_kn_g': mb_kn_g}

def reference(x, mem, mem_norm_g, w_mem_kv, norm_mix_g, norm_xa_g, norm_ffn_g, xa_wq, xa_wo, xa_qn_g,
              xa_kn_g, moe_w_grp, moe_b_grp, moe_w_exp, moe_b_exp, moe_w1, moe_w3, moe_w2, ev_w_in,
              ev_w_out, gm_ws, gm_bs, gm_ln_g, s5_lam_re, s5_lam_im, s5_b_re, s5_b_im, s5_c_re, s5_c_im,
              s5_d, s5_log_step, s5_w_glu, s5_b_glu, od_w_in, od_w_out, ml_conv_w, ml_conv_b, ml_b_if,
              ml_hn_g, mb_qn_g, mb_kn_g):
    mkv = rmsnorm(mem, mem_norm_g) @ w_mem_kv
    mem_k = split_heads(mkv[..., :XA_DIM], XA_HEADS)
    mem_v = split_heads(mkv[..., XA_DIM:], XA_HEADS)
    h = x
    for layer in range(DEPTH):
        j = layer // 2
        xn = rmsnorm(h, norm_mix_g[layer])
        if layer % 2 == 0:
            mix = even_mixer(xn, ev_w_in[j], ev_w_out[j], gm_ws[j], gm_bs[j], gm_ln_g[j],
                             s5_lam_re[j], s5_lam_im[j], s5_b_re[j], s5_b_im[j], s5_c_re[j], s5_c_im[j],
                             s5_d[j], s5_log_step[j], s5_w_glu[j], s5_b_glu[j])
        else:
            mix = odd_mixer(xn, od_w_in[j], od_w_out[j], ml_conv_w[j], ml_conv_b[j], ml_b_if[j],
                            ml_hn_g[j], mb_qn_g[j], mb_kn_g[j])
        h = h + mix
        h = h + cross_attn(rmsnorm(h, norm_xa_g[layer]), mem_k, mem_v, xa_wq[layer], xa_wo[layer],
                           xa_qn_g[layer], xa_kn_g[layer])
        h = h + hier_moe(rmsnorm(h, norm_ffn_g[layer]), moe_w_grp[layer], moe_b_grp[layer],
                         moe_w_exp[layer], moe_b_exp[layer], moe_w1[layer], moe_w3[layer], moe_w2[layer])
    return h


_drawn_inputs = setup_inputs


def setup_inputs(seed=0):
    import zlib

    import numpy as np

    out = dict(_drawn_inputs(seed))
    spreads = {}
    factors = {'xa_qn_g': 2.716,
     'xa_kn_g': 3.865,
     'moe_b_grp': 2.989,
     'moe_b_exp': 3.644,
     's5_lam_re': 8.0,
     's5_b_re': 2.695,
     's5_b_glu': 8.0,
     'ml_conv_b': 8.0,
     'mb_qn_g': 6.854,
     'mb_kn_g': 5.609}
    for name, (base, spread) in spreads.items():
        noise = np.random.default_rng([zlib.crc32(name.encode()), seed]).standard_normal(out[name].shape)
        drawn = base * np.exp(spread * noise) if base else spread * noise
        out[name] = jnp.asarray(drawn.astype(out[name].dtype))
    for name, factor in factors.items():
        out[name] = (out[name] * factor).astype(out[name].dtype)
    return out
```

```python
from contextlib import ExitStack

import concourse.bass as bass
import numpy as np
from concourse import mybir

F32 = mybir.dt.float32
F32R = mybir.dt.float32r
I32 = mybir.dt.int32
U32 = mybir.dt.uint32
ACT = mybir.ActivationFunctionType
ALU = mybir.AluOpType
AX = mybir.AxisListType

P = 128
BIG = 1.0e30
TWO_PI = 6.283185
ROUND = 1.5 * 2.0 ** 23
EPS = 1e-6
UPTO = "all"
STAGES = ["mix0", "xa0", "moe0", "mix1", "xa1", "all"]


def uses_of_banks(layers):
    steps = [("cols", 1), ("memT", 4), ("ct", 2), ("kv", 8), ("bT", 8), ("w", 8), ("memKT", 4)]

    def attention(l):
        return [(f"xa_norm{l}", 8), (f"q{l}", 8), (f"qT{l}", 8), (f"sc{l}", 8), (f"pT{l}", 8), (f"o{l}", 8),
                (f"wo{l}", 8)]

    def moe(l):
        return [(f"ffn_norm{l}", 8), (f"route{l}", 1), (f"rank{l}", 1), (f"idx{l}", 1)]

    steps += [("mix_norm0", 8), ("uv", 8), ("s5u", 4), ("ws", 1), ("mixed", 4), ("yaT", 4), ("uj", 8), ("ucT", 4), ("V", 4),
              ("Vsw", 4), ("Xp", 4), ("y", 8), ("yT", 4), ("glu", 4), ("out0", 8)]
    steps += attention(0) + moe(0)
    steps += [("mix_norm1", 8), ("dq", 4), ("dk", 4), ("qk", 8), ("v", 4), ("og", 4), ("if", 1), ("dv", 4),
              ("dT", 8), ("ifT", 2), ("col", 1), ("mlh0", 5), ("mlh1", 5), ("num0", 4), ("mlh2", 5), ("mlh3", 5),
              ("num1", 4), ("ms0", 4), ("ms1", 4), ("mp0", 4), ("ms2", 4), ("mp1", 4), ("ms3", 4), ("mp2", 4),
              ("mp3", 4), ("ycT", 4), ("out1", 8)]
    steps += attention(1) + moe(1)
    first, n = {}, 0
    for name, k in steps:
        first[name] = n
        n += k
    return first


def program(nc, A, out):
    T, D = A["x"].shape[1:]
    MIX = D // 2
    TT, KT = T // P, D // P
    NM = A["mem"].shape[1]
    MT = NM // P
    H, HD = 4, 128
    XD = D // 4
    G, GI, NS = A["s5_b_re"].shape[1], A["s5_b_re"].shape[3], A["s5_b_re"].shape[2]
    LC = P // GI
    NC = T // LC
    NE, FF = A["moe_w1"].shape[1], A["moe_w1"].shape[3]
    NX = T // P - 1
    NI = NE + 2 * T // P
    XA_SCALE = float(XD) ** -0.5
    HD_SCALE = float(HD) ** -0.5
    first = uses_of_banks(2)
    RING = 4

    ctx = ExitStack()
    with ctx:
        def sb(name, shape, dt=F32):
            return ctx.enter_context(nc.sbuf_tensor(name, shape, dt))

        def sem(name):
            return ctx.enter_context(nc.semaphore(name))

        banks = [ctx.enter_context(nc.psum_tensor(f"bank{i}", [P, 512], F32)) for i in range(8)]
        filled = [sem(f"filled{i}") for i in range(8)]
        evacuated = [sem(f"evacuated{i}") for i in range(8)]

        with ExitStack() as shared:
            xTr, E0r, E1r, E2r, E4r, E5r = [
                shared.enter_context(nc.sbuf_tensor(f"{n}r", [P, w], F32R))
                for n, w in (("xT", KT * T), ("E0", 4096), ("E1", 4096), ("E2", 4096), ("E4", 4096), ("E5", G * (LC + 1) * GI))]
        xT = sb("xT", [P, KT, T])
        E = {i: sb(f"E{i}", [P, 4096]) for i in (0, 1, 2, 4)}
        E5 = sb("E5", [P, G * (LC + 1) * GI])
        E[3] = sb("E3", [P, 4096])
        h = sb("h", [P, TT, D])
        W = [sb(f"W{i}", [P, KT, 512]) for i in range(2)]
        whi = [sb(f"whi{i}", [P, 512], F32R) for i in range(RING)]
        wlo = [sb(f"wlo{i}", [P, 512], F32R) for i in range(RING)]
        memKT = sb("memKT", [P, KT, NM])
        memV = sb("memV", [P, MT, D])
        ident = sb("ident", [P, P])
        perm = sb("perm", [P, P])
        after = sb("after", [P, P])
        before = sb("before", [P, P])
        strict = sb("strict", [P, P])
        ones = sb("ones", [P, P])
        wsT = sb("wsT", [P, 4 * P])
        sgn = sb("sgn", [P, 1])
        nsgn = sb("nsgn", [P, 1])
        halfpi = sb("halfpi", [P, 1])
        cols = sb("cols", [P, P])
        spare = sb("spare", [P, 1])
        ssq = sb("ssq", [P, 7, 4])
        std = sb("std", [P, 7, 4])
        rstd = sb("rstd", [P, 7, 4])
        rw = sb("rw", [P, 2, KT, 20])
        rbias = sb("rbias", [P, 2, 20])
        ifw = sb("ifw", [P, KT, 8])
        ifb = sb("ifb", [P, 8])
        gbs = sb("gbs", [P, 4])
        sm = sb("sm", [P, 640])
        st = sb("st", [P, 256])
        junk = sb("junk", [P, 256])
        rows = junk[:, 0:P]
        iot = sb("iot", [P, P], I32)
        iof = sb("iof", [P, P])
        tab = sb("tab", [P, 64], I32)
        toki = sb("toki", [P, 2 * TT], I32)
        tokf = sb("tokf", [P, 2 * TT])
        pos = sb("pos", [P, 2, 4], U32)
        itemi = sb("itemi", [P, 8], U32)
        gate = sb("gate", [P, 2, 4])
        slots = sb("slots", [P, NI], U32)
        idx = sb("idx", [P, 2], U32)

        xs = [nc.dram_tensor(f"xs{l}", [T, D], F32).ap() for l in range(2)]
        ybuf = [nc.dram_tensor(f"ybuf{l}", [NI * P, D], F32).ap() for l in range(2)]

        names = """x_in small_in s5_in consts_ready wide_in rope_in mem_in panel0 panel1 x_hi w_hi w_lo w_used
        stat_ready hmean_ready hstd_ready mean_ready std_ready xn_ready s5_args s5_exp s5_sin s5_bb s5_pp s5_w s5_t memk_norm
        ln_mean ln_sq vh_ready ws_masked s5_scan s5_x ya_ready q_norm hd_sq max_ready probs mo_probs
        a_step d_step p_step qk_ready d_norm ml_args ml_act ml_rows diag_ready dt_ready conv_in hh_ready rows_ready
        spare_rows final""".split()
        S = {n: sem(n) for n in names}
        per_layer = """xs_stored onehots_ready slots_ready table_ready gate_args gate_exp pos_ready msum_ready w13a w13b w2a w2b
        idx_ready pool_waited xg_in0 xg_in1 xt_filled xt_ready hid_filled silu_ready hid_ready ht_filled ht_ready
        y_filled0 y_filled1 y_ready0 y_ready1 y_stored0 y_stored1 y_gathered0 y_gathered1 y_gathered2 y_gathered3
        h_half h_combined""".split()
        M = [{n: sem(f"{n}_{l}") for n in per_layer} for l in range(2)]

        block = ctx.enter_context(nc.Block())

        def bank(u):
            return banks[u % 8]

        def claim(pe, u):
            if u >= 8:
                pe.wait_ge(evacuated[u % 8], u // 8)

        def fill(ins, u):
            ins.then_inc(filled[u % 8], 1)

        def await_filled(eng, u):
            eng.wait_ge(filled[u % 8], u // 8 + 1)

        def evac(ins, u):
            ins.then_inc(evacuated[u % 8], 1)

        def taken(eng, u):
            eng.wait_ge(evacuated[u % 8], u // 8 + 1)

        def taken_all(eng, name, n):
            for u in range(first[name] + max(0, n - 8), first[name] + n):
                taken(eng, u)

        class Chain:

            def __init__(self, eng, own):
                self.eng, self.own, self.n = eng, own, {}

            def __call__(self, ins, s=None):
                s = s or self.own
                self.n[s] = self.n.get(s, 0) + 1
                ins.then_inc(S[s], 1)
                self.eng.wait_ge(S[s], self.n[s])

        vec, at = {}, 0
        for name, n in (("mem_norm_g", 8), ("norm_mix_g", 16), ("norm_xa_g", 16), ("norm_ffn_g", 16),
                        ("xa_qn_g", 4), ("xa_kn_g", 4), ("ml_conv_w", 32), ("ml_conv_b", 8), ("s5_b_glu", 4)):
            vec[name] = (at, n)
            at += n
        NROWS = at

        def col(name, i):
            return cols[:, vec[name][0] + i:vec[name][0] + i + 1]

        w_kv = A["w_mem_kv"].rearrange("(k p) n -> p k n", p=P)
        w_ev = A["ev_w_in"][0].rearrange("(k p) n -> p k n", p=P)
        w_evo = A["ev_w_out"][0].rearrange("(k p) n -> p k n", p=P)
        w_glu = A["s5_w_glu"][0].rearrange("(k p) n -> p k n", p=P)
        w_od = A["od_w_in"][0].rearrange("(k p) n -> p k n", p=P)
        w_odo = A["od_w_out"][0].rearrange("(k p) n -> p k n", p=P)
        w_q = [A["xa_wq"][l].rearrange("(k p) n -> p k n", p=P) for l in range(2)]
        w_o = [A["xa_wo"][l].rearrange("(k p) n -> p k n", p=P) for l in range(2)]
        panels, pnum = [], {}

        def panel(name, src, last):
            pnum[name] = len(panels)
            panels.append((src, last))

        for n in range(4):
            panel(f"kv{n}", w_kv[:, :, n * 512:(n + 1) * 512], first["kv"] + 2 * n + 1)
        for n, (s, k) in enumerate((("uv", 3), ("uv", 7), ("s5u", 3))):
            panel(f"ev{n}", w_ev[:, :, n * 512:(n + 1) * 512], first[s] + k)
        panel("glu", w_glu, first["glu"] + 3)
        for n in range(2):
            panel(f"out0{n}", w_evo[:, :, n * 512:(n + 1) * 512], first["out0"] + 4 * n + 3)
        for l in range(2):
            if l == 1:
                q0 = 4 * MIX + 8
                for n, (s, k, c) in enumerate((("dq", 3, q0), ("dk", 3, q0 + 512), ("qk", 3, 0), ("qk", 7, 512),
                                               ("v", 3, 1024), ("og", 3, 1536), ("dv", 3, q0 + 1024))):
                    panel(f"od{n}", w_od[:, :, c:c + 512], first[s] + k)
                for n in range(2):
                    panel(f"out1{n}", w_odo[:, :, n * 512:(n + 1) * 512], first["out1"] + 4 * n + 3)
            for n in range(2):
                panel(f"wq{l}{n}", w_q[l][:, :, n * 512:(n + 1) * 512], first[f"q{l}"] + 4 * n + 3)
            for n in range(2):
                panel(f"wo{l}{n}", w_o[l][:, :, n * 512:(n + 1) * 512], first[f"wo{l}"] + 4 * n + 3)
        first_of_layer1 = pnum["od0"]
        landed = [S["panel0"], S["panel1"]]

        def slot(name):
            return W[pnum[name] % 2]

        def panel_in(pe, name):
            p = pnum[name]
            pe.wait_ge(landed[p % 2], 16 * (p // 2 + 1))

        split_panels = [f"{w}0{n}" for w in ("wq", "wo") for n in range(2)] + [f"od{n}" for n in range(7)] + \
                       [f"{w}1{n}" for w in ("out", "wq", "wo") for n in range(2)]

        def step(name, k):
            return split_panels.index(name) * KT + k

        def await_ring(eng, s_):
            i, k = divmod(s_ - RING, KT)
            if i >= 0:
                if k < KT - 1:
                    eng.wait_ge(S["w_used"], (KT - 1) * i + k + 1)
                else:
                    await_filled(eng, panels[pnum[split_panels[i]]][1])

        two_parts = [first["xa_norm0"] + k for k in range(8)] + [first["o0"] + k for k in range(8)] + \
                    [first["mix_norm1"] + k for k in range(8)] + [first[f"mp{n}"] + 3 for n in range(4)] + \
                    [first["ycT"] + k for k in range(4)] + [first["xa_norm1"] + k for k in range(8)] + \
                    [first["o1"] + k for k in range(8)]

        rope_c = A["rope_cos"].rearrange("(a p) d -> p a d", p=P)
        rope_s = A["rope_sin"].rearrange("(a p) d -> p a d", p=P)
        w1 = A["moe_w1"].rearrange("l e (k p) f -> (l e) p k f", p=P)
        w3 = A["moe_w3"].rearrange("l e (k p) f -> (l e) p k f", p=P)
        w2 = A["moe_w2"].rearrange("l e (k p) d -> (l e) p k d", p=P)

        def v3(buf, a, lo=0, hi=None):
            hi = buf.shape[1] if hi is None else hi
            return buf[:, lo:hi].rearrange("p (a b) -> p a b", a=a)

        xn = v3(E[0], 4)
        s5T = v3(E[0], G)
        s5Q = v3(E[1], G)
        s5cos = v3(E[2], G, 0, G * NC)
        s5sin = v3(E[2], G, G * NC, 2 * G * NC)
        s5PP = E5[:, :].rearrange("p (g k i) -> p g k i", g=G, k=LC + 1)
        s5Qn = E[3][:, :].rearrange("p (g j i) -> p g j i", g=G, j=LC)
        s5Wst = v3(E[3], G)
        xnE = v3(E[3], 4)
        Gu = v3(E[3], 4, 0, 2048)
        Gv = v3(E[3], 4, 2048, 4096)
        U = E[4][0:NC, :].rearrange("c (g j i) -> c g j i", g=G, j=LC)
        Uc = v3(E[3], G, 2048, 4096)
        Vc = v3(E[3], G, 0, 2048)
        Vs = v3(E[4], G, 0, 2048)
        Sc = v3(E[4], G, 2048, 4096)
        Y = E[2][0:NC, :].rearrange("c (j n) -> c j n", j=LC)
        uT = xT[:, 4:8, :]
        yT = v3(E[4], 4, 0, 2048)
        sg = v3(E[3], 4, 0, 2048)
        QKT = v3(E[0], 8)
        VML = E5[:, 0:16 * 129].rearrange("p (t h d) -> p t h d", t=4, h=4)
        SO = v3(E5, 4, 2112, 2112 + 2048)
        Dq = v3(E[1], 4, 0, 2048)
        Dk = v3(E[1], 4, 2048, 4096)
        qdT = v3(E[2], 4, 0, 2048)
        kdT = v3(E[2], 4, 2048, 4096)
        Dv = v3(E[3], 4, 0, 2048)
        Rt = E[3][:, 2048:4096]
        hh = v3(E[1], 4, 0, 2048)
        hsq = v3(E[1], 4, 2048, 4096)

        WOFF = [0, 512, 896, 1152]

        def wts(hh_, s):
            o = (hh_ % 2) * 1280 + WOFF[s]
            return E[4][:, o:o + T - P * s]

        def dts(n):
            return E[4][:, 2560 + 512 * (n % 2):3072 + 512 * (n % 2)]

        sdiag = E[4][:, 3584:4096]
        POFF = [0, 128, 384, 768]

        def pm(hh_, t):
            o = (hh_ % 2) * 1280 + POFF[t]
            return E[0][:, o:o + P * (t + 1)]

        TOFF = [0, 512, 1024, 896]

        def ptm(hh_, k):
            o = (hh_ % 2) * 1280 + TOFF[k]
            return E[4][:, o:o + T - P * k]

        def row(name):
            return rows[vec[name][0]:vec[name][0] + vec[name][1], :]

        small = [(row("mem_norm_g"), A["mem_norm_g"].rearrange("(r c) -> r c", c=P))]
        for name in ("norm_mix_g", "norm_xa_g", "norm_ffn_g", "xa_qn_g", "xa_kn_g"):
            small.append((row(name), A[name].rearrange("l (r c) -> (l r) c", c=P)))
        small += [(row("ml_conv_w"), A["ml_conv_w"][0].rearrange("w (r c) -> (w r) c", c=P)),
                  (row("ml_conv_b"), A["ml_conv_b"][0].rearrange("(r c) -> r c", c=P)),
                  (row("s5_b_glu"), A["s5_b_glu"][0].rearrange("(r c) -> r c", c=P))]
        for l in range(2):
            small += [(rw[:, l, :, 0:4], A["moe_w_grp"][l].rearrange("(k p) n -> p k n", p=P)),
                      (rw[:, l, :, 4:20], A["moe_w_exp"][l].rearrange("(k p) n -> p k n", p=P)),
                      (rbias[:, l, 0:4], A["moe_b_grp"][l].partition_broadcast(P)),
                      (rbias[:, l, 4:20], A["moe_b_exp"][l].partition_broadcast(P))]
        small += [(ifw[:, :, :], w_od[:, :, 4 * MIX:4 * MIX + 8]),
                  (ifb[:, :], A["ml_b_if"][0].partition_broadcast(P)),
                  (gbs[:, :], A["gm_bs"][0].rearrange("h t -> t h"))]
        lamr, lami, lstep = sm[:, 0:32], sm[:, 32:64], sm[:, 64:96]
        dT = sm[0:GI, 96:128]
        Cst1, Cst2 = v3(E[4], 4, 0, 512), v3(E[4], 4, 512, 1024)
        B1, B2, BB1, BB2, C1, C2 = [v3(E[4], G, 1024 + 512 * n, 1536 + 512 * n) for n in range(6)]
        s5_loads = [(lstep, A["s5_log_step"][0].partition_broadcast(P)),
                    (dT, A["s5_d"][0].rearrange("(g i) -> i g", i=GI))]
        for lo, b1, b2, c1, c2 in ((0, "s5_b_re", "s5_b_im", "s5_c_re", "s5_c_im"),
                                   (NS, "s5_b_im", "s5_b_re", "s5_c_im", "s5_c_re")):
            s5_loads += [(lamr[lo:lo + NS, :], A["s5_lam_re"][0].rearrange("g p -> p g")),
                         (lami[lo:lo + NS, :], A["s5_lam_im"][0].rearrange("g p -> p g")),
                         (B1[lo:lo + NS], A[b1][0].rearrange("g p i -> p g i")),
                         (B2[lo:lo + NS], A[b2][0].rearrange("g p i -> p g i")),
                         (Cst1[:, :, lo:lo + NS], A[c1][0].rearrange("(a g) i p -> (g i) a p", a=4)),
                         (Cst2[:, :, lo:lo + NS], A[c2][0].rearrange("(a g) i p -> (g i) a p", a=4))]
        xTf = xT[:, :, :].rearrange("p a b -> p (a b)")
        memtok = v3(xTf, 2, 2048, 4096)
        memnT = v3(xTf, 8, 0, 2048)
        headsel = wsT[0:4, :].rearrange("p (h m) -> p h m", h=4)
        xg = [E[1][:, 1024 * n:1024 * n + 1024] for n in range(2)]
        xgT = [v3(E[1], KT, 2048 + 1024 * n, 3072 + 1024 * n) for n in range(2)]
        yo = [E[2][:, 1024 * n:1024 * n + 1024] for n in range(2)]
        silu = [E[2][:, 2048 + FF * n:2048 + FF * n + FF] for n in range(2)]
        hid = [E[2][:, 2560 + FF * n:2560 + FF * n + FF] for n in range(2)]
        hT = [E[2][:, 3072 + FF * n:3072 + FF * n + FF] for n in range(2)]
        w2s = [v3(E[3], 2, 2048 * n, 2048 * n + 2048) for n in range(2)]
        Yg = [v3(E[3 + n], TT) for n in range(2)]
        qtok = v3(E[1], TT)
        qT = v3(E[2], KT)
        prob = E[3][:, :].rearrange("p (t h m) -> p t h m", t=TT, h=4)
        pT = E[4][:, :].rearrange("p (h k q) -> p h k q", h=4, k=2)
        oT = v3(E[0], KT)
        xlo = {"q": v3(E4r, KT), "o": v3(E1r, KT), "od": v3(E2r, KT), "out1": v3(E5r, KT, 0, KT * T)}
        xhi, ohi = v3(xTr, KT), v3(E0r, KT)
        xmx, xnm, xsum, xrec = st[:, 0:16], st[:, 16:32], st[:, 32:48], st[:, 48:64]
        stage = STAGES.index(UPTO)
        wsN = v3(wsT, 4)
        Irow, Frow, lrow, erow, Brow, arow, Mrow, enrow = [E[4][0:4, 512 * n:512 * n + 512] for n in range(8)]
        Irow = E[3][0:4, 2816:3328]
        nMrow = Irow
        ifg = st[:, 64:96].rearrange("p (t n) -> p t n", t=4)
        mlc = st[:, 96:128]
        g2 = st[:, 128:132]
        msum = v3(sm, 4, 512, 576)
        lngain, hngain = E[4][:, 3584:4096], sm[:, 0:512]
        ropec, ropes = v3(E[3], 4, 2048, 2304), v3(E[3], 4, 2304, 2560)
        rope_loads = [(ropec, rope_c), (ropes, rope_s), (E[3][:, 2560:2688], A["mb_qn_g"][0].partition_broadcast(P)),
                      (E[3][:, 2688:2816], A["mb_kn_g"][0].partition_broadcast(P))]
        dsq, dstd, drec = st[:, 132:164], st[:, 164:196], st[:, 196:228]
        step_, are, th, turn, t8, rho8, Fr, Fi, nr, n1, n2 = [sm[:, 128 + 32 * n:160 + 32 * n] for n in range(11)]
        mag, Lr, Li, Lt = [v3(E[1], G, 288 * n, 288 * n + 288) for n in range(4)]
        def t4(lo, k):
            return sm[:, lo:lo + 4 * k].rearrange("p (t k) -> p t k", t=4)

        lg, gsub, gexp, gmax, gs, gp, geq, gf = (t4(0, 20), t4(80, 4), t4(96, 4), sm[:, 112:116], sm[:, 116:120],
                                                 sm[:, 120:124], t4(124, 4), t4(140, 4))
        sel16, sel, m1, m2, f1, f2 = t4(160, 16), t4(224, 4), sm[:, 240:244], sm[:, 244:248], t4(248, 4), t4(264, 4)
        sel2, dsub, dexp, tmp4, RB = t4(280, 4), sm[:, 296:300], sm[:, 300:304], t4(304, 4), t4(448, 16)
        M12 = [t4(320, 16), t4(384, 16)]
        posf, rev4 = sm[:, 576:584], sm[:, 584:588]
        def c3(ap):
            return ap.rearrange("p (e j) -> p e j", e=NE)

        E4 = E[4]
        rank, full, more, cum, zero, base, xbase, slotf, itemf = [
            E4[:, lo:lo + n] for lo, n in ((0, 5 * NE), (80, NX), (96, NE * NX), (144, NE * NX), (192, NE * NX),
                                           (240, NE), (256, NE), (272, 8), (280, 8))]
        slot1h, item1h = v3(E4, 8, 512, 512 + 8 * P), v3(E4, 8, 1536, 1536 + 8 * NI)
        epx, nth, tabf, half_, big1, big2 = [
            E4[0:1, lo:lo + n] for lo, n in ((1792, NE * NX), (1840, 8), (1856, 64), (1920, 4), (2048, 8 * NE * NX),
                                             (2048 + 8 * NE * NX, 8 * NE * NX))]
        dgain = [E[3][:, 2560:2688], E[3][:, 2688:2816]]

        @block.sync
        def _(sp):
            def load_panel(p):
                src, _ = panels[p]
                if p >= 2:
                    await_filled(sp, panels[p - 2][1])
                sp.dma_start(W[p % 2][:, 0:src.shape[1], :], src).then_inc(landed[p % 2], 16)

            def experts(l):
                m = M[l]
                for p in range(first_of_layer1 if l == 0 else len(panels))[-2:]:
                    await_filled(sp, panels[p][1])
                await_filled(sp, first[f"pT{l}"] + 7)

                def load_up(e, par):
                    for n, w in enumerate((w1, w3)):
                        sp.dma_start(W[par][:, :, n * FF:(n + 1) * FF], w[e]).then_inc(m["w13a" if par == 0 else "w13b"], 16)

                def load_down(e, par):
                    sp.dma_start(w2s[par], w2[e])\
                      .then_inc(m["w2a" if par == 0 else "w2b"], 16)

                def store(q, par):
                    for half in range(2):
                        sp.wait_ge(m[f"y_ready{half}"], q * 2 + (par + 1))
                    sp.dma_start(ybuf[l][bass.ds(q * (2 * P) + par * P, P), :], yo[par]).then_inc(m[f"y_stored{par}"], 16)

                sp.wait_ge(S["spare_rows"], 16 * 2 * (NI - NE) * P // NM)
                for par in range(2):
                    load_up(NE * l + par, par)
                    load_down(NE * l + par, par)
                sp.wait_ge(m["table_ready"], 1)
                last_pair = sp.value_load(tab[0:1, 60:61], min_val=NE // 2 - 1, max_val=NI // 2 - 1)
                with sp.Fori(1, last_pair + 1) as q:
                    for par in range(2):
                        e = sp.value_load(tab[0:1, bass.ds(q * 2 + par, 1)], min_val=0, max_val=NE - 1)
                        sp.wait_ge(m["hid_filled"], q * 2 + (par - 1))
                        load_up(e + NE * l, par)
                        sp.wait_ge(m["y_filled1"], q * 2 + (par - 1))
                        load_down(e + NE * l, par)
                        store(q - 1, par)
                for par in range(2):
                    store(last_pair, par)

            for k in range(TT):
                sp.dma_start(h[:, k, :], A["x"][0, k * P:(k + 1) * P, :]).then_inc(S["x_in"], 16)
            for p in range(len(panels)):
                if p == first_of_layer1:
                    experts(0)
                load_after_moe = first_of_layer1 <= p < first_of_layer1 + 2
                if p == first_of_layer1:
                    sp.wait_ge(M[0]["y_gathered2"], 32)
                if load_after_moe:
                    src, _ = panels[p]
                    sp.dma_start(W[p % 2][:, 0:src.shape[1], :], src).then_inc(landed[p % 2], 16)
                else:
                    load_panel(p)
                if p + 1 == {0: pnum["out01"] + 1, 1: pnum["wo01"] + 1, 3: pnum["out11"] + 1, 4: pnum["wo11"] + 1}.get(stage):
                    break
                if stage == 2 and p + 1 == first_of_layer1:
                    experts(0)
                    break
            else:
                experts(1)
            sp.wait_ge(S["final"], 4)
            for k in range(TT):
                sp.dma_start(out[0, k * P:(k + 1) * P, :], h[:, k, :]).then_inc(S["x_in"], 16)
            sp.wait_ge(S["x_in"], 2 * 16 * TT)

        @block.gpsimd
        def _(pool):
            p_ = Chain(pool, "p_step")
            def select(t, base, pattern, mult, op, fill):
                p_(pool.affine_select(out=t, in_=t, compare_op=op, fill=fill, base=base, pattern=pattern,
                                      channel_multiplier=mult))

            for t, value in ((ident, 0.0), (perm, 0.0), (after, 0.0), (before, 0.0), (strict, 1.0), (ones, 1.0),
                             (halfpi, TWO_PI / 4), (sgn, 1.0), (nsgn, -1.0)):
                p_(pool.memset(t[:], value))
            select(ident[:], 0, [[-1, P]], 1, ALU.not_equal, 1.0)
            select(perm[:], -NS, [[-1, P]], 1, ALU.not_equal, 1.0)
            select(perm[:], NS, [[-1, P]], 1, ALU.not_equal, -1.0)
            select(after[:], 0, [[1, P]], -1, ALU.is_ge, -BIG)
            select(before[:], 0, [[-1, P]], 1, ALU.is_ge, -BIG)
            select(strict[:], 0, [[1, P]], -1, ALU.is_gt, 0.0)
            select(sgn[:], NS - 1, [[0, 1]], -1, ALU.is_ge, -1.0)
            select(nsgn[:], NS - 1, [[0, 1]], -1, ALU.is_ge, 1.0)
            p_(pool.iota(iot[:], pattern=[[1, P]], base=0, channel_multiplier=0))
            p_(pool.iota(toki[:], pattern=[[0, 2], [P, TT]], base=0, channel_multiplier=1))
            p_(pool.tensor_copy(tokf[:], toki[:]))
            p_(pool.tensor_copy(iof[:], iot[:]))
            pool.memset(E[0][:], 0.0).then_inc(S["consts_ready"], 1)

            taken(pool, first["ws"])
            wsv = v3(wsT, 4)
            p_(pool.affine_select(out=wsv, in_=wsv, compare_op=ALU.is_ge, fill=0.0, base=0, pattern=[[0, 4], [1, P]],
                                  channel_multiplier=-1), "ws_masked")
            await_filled(pool, first["mixed"] + 3)
            p_(pool.memset(headsel, 0.0))
            p_(pool.affine_select(out=headsel, in_=headsel, compare_op=ALU.not_equal, fill=1.0, base=0,
                                  pattern=[[-1, 4], [0, P]], channel_multiplier=1), "ws_masked")

            def experts(l):
                m = M[l]

                def wait_alone(semaphore, value):
                    pool.wait_ge(semaphore, value)
                    pool.sem_inc(m["pool_waited"], 1)

                def gather(q, par):
                    if not isinstance(q, int):
                        wait_alone(m["xt_filled"], q * 4 + (2 * par - 2))
                    pool.tensor_copy(idx[:, par:par + 1], slots[:, bass.ds(q * 2 + par, 1)]).then_inc(m["idx_ready"], 1)
                    wait_alone(m["idx_ready"], q * 2 + (par + 1))
                    pool.indirect_dma_start(xg[par], None, xs[l],
                                            bass.IndirectOffsetOnAxis(ap=idx[:, par:par + 1], axis=0))\
                        .then_inc(m[f"xg_in{par}"], 16)

                pool.wait_ge(m["slots_ready"], 1)
                pool.wait_ge(m["xs_stored"], 16 * TT)
                gather(0, 0)
                gather(0, 1)
                pool.wait_ge(m["table_ready"], 1)
                last_pair = pool.value_load(tab[0:1, 60:61], min_val=NE // 2 - 1, max_val=NI // 2 - 1)
                with pool.Fori(1, last_pair + 1) as q:
                    gather(q, 0)
                    gather(q, 1)
                pool.wait_ge(m["pos_ready"], 1)
                for par in range(2):
                    wait_alone(m[f"y_stored{par}"], last_pair * 16 + 16)
                for t in range(TT):
                    for j in range(2):
                        pool.indirect_dma_start(Yg[j][:, t, :], None, ybuf[l],
                                                bass.IndirectOffsetOnAxis(ap=pos[:, j, t:t + 1], axis=0))\
                            .then_inc(m[f"y_gathered{t}"], 16)
            taken_all(pool, "kv", 8)
            for l in range(2):
                for n in range(NE * P // NM, NI * P // NM):
                    pool.dma_start(ybuf[l][n * NM:(n + 1) * NM, :].rearrange("(k p) d -> p k d", p=P), memV[:, :, :])\
                        .then_inc(S["spare_rows"], 16)
            def low_parts(*names):
                for name in names:
                    for k in range(KT):
                        s_ = step(name, k)
                        pool.wait_ge(S["w_hi"], s_ + 1)
                        pool.tensor_tensor(wlo[s_ % RING][:, :], slot(name)[:, k, :], whi[s_ % RING][:, :].bitcast(F32),
                                           ALU.subtract).then_inc(S["w_lo"], 1)

            if stage >= 1:
                low_parts("wq00", "wq01", "wo00", "wo01")
            if stage >= 2:
                experts(0)
            if stage >= 3:
                low_parts(*[f"od{n}" for n in range(7)], "out10", "out11")
            if stage >= 4:
                low_parts("wq10", "wq11", "wo10", "wo11")
            if stage >= 5:
                experts(1)

        NORMS = {"mem": 0, "mix_norm0": 1, "xa_norm0": 2, "ffn_norm0": 3, "mix_norm1": 4, "xa_norm1": 5, "ffn_norm1": 6}

        @block.tensor
        def _(pe):
            def transpose_gain_norm(name):
                u0 = first[name]
                src = xnE if name == "mix_norm0" else xn
                n = NORMS[name]
                for k in range(KT):
                    claim(pe, u0 + k)
                    for t in range(TT):
                        if k == 0:
                            pe.wait_ge(S["xn_ready"], 2 + 4 * (n - 1) + t + 1)
                        ins = pe.transpose(bank(u0 + k)[:, t * P:(t + 1) * P], src[:, t, k * P:(k + 1) * P], ident[:])
                    fill(ins, u0 + k)

            def tokens_gemm(name, panel_names, lhsT, kt, order=None):
                u = first[name]
                for pn in panel_names:
                    panel_in(pe, pn)
                    for t in range(TT):
                        claim(pe, u)
                        for k in range(kt):
                            ins = pe.matmul(bank(u)[:, :], lhsT(k, t), slot(pn)[:, k, :], start=(k == 0),
                                            stop=(k == kt - 1))
                        fill(ins, u)
                        u += 1

            def split_gemm(u, panel_name, hi, lo, x_ready=None, weights_first=False):
                for t in range(TT):
                    claim(pe, u + t)
                for k in range(KT):
                    s_ = step(panel_name, k)
                    if x_ready:
                        taken(pe, x_ready(k))
                    pe.wait_ge(S["w_lo"], s_ + 1)
                    wh, wl = whi[s_ % RING], wlo[s_ % RING]
                    xh, xl = hi[:, k, :], lo[:, k, :]
                    for t in range(TT):
                        c = slice(t * P, (t + 1) * P)
                        if weights_first:
                            passes = ((wh[:, c], xh), (wh[:, c], xl), (wl[:, c], xh))
                        else:
                            passes = ((xh[:, c], wh[:, :]), (xh[:, c], wl[:, :]), (xl[:, c], wh[:, :]))
                        for n, (a, b) in enumerate(passes):
                            ins = pe.matmul(bank(u + t)[:, :], a, b, start=(k == 0 and n == 0),
                                            stop=(k == KT - 1 and n == 2))
                        if k == KT - 1:
                            fill(ins, u + t)
                    if k < KT - 1:
                        ins.then_inc(S["w_used"], 1)

            def plain(buf):
                return lambda k, t: buf[:, k, t * P:(t + 1) * P]

            pe.wait_ge(S["consts_ready"], 1)
            u = first["cols"]
            pe.wait_ge(S["small_in"], 16 * len(small))
            fill(pe.transpose(bank(u)[:, 0:NROWS], rows[0:NROWS, :], ident[0:NROWS, 0:NROWS]), u)
            u = first["memT"]
            for t in range(MT):
                pe.wait_ge(S["xn_ready"], t + 1)
            for k in range(0, KT, 2):
                for kk in range(2):
                    for t in range(MT):
                        ins = pe.transpose(bank(u)[:, kk * NM + t * P:kk * NM + (t + 1) * P],
                                           memtok[:, t, (k + kk) * P:(k + kk + 1) * P], ident[:])
                fill(ins, u)
                u += 1
            taken_all(pe, "memT", 4)
            pe.wait_ge(S["s5_in"], 16 * len(s5_loads))
            for n, c in enumerate((Cst1, Cst2)):
                u = first["ct"] + n
                claim(pe, u)
                for a in range(4):
                    ins = pe.transpose(bank(u)[:, a * P:(a + 1) * P], c[:, a, :], ident[:])
                fill(ins, u)
            u = first["kv"]
            for n in range(4):
                panel_in(pe, f"kv{n}")
                for t in range(MT):
                    claim(pe, u)
                    for k in range(KT):
                        ins = pe.matmul(bank(u)[:, :], memnT[:, k, t * P:(t + 1) * P], slot(f"kv{n}")[:, k, :],
                                        start=(k == 0), stop=(k == KT - 1))
                    fill(ins, u)
                    u += 1
            pe.wait_ge(S["s5_bb"], 1)
            for n in range(8):
                u = first["bT"] + n
                claim(pe, u)
                for g in range(4 * n, 4 * n + 4):
                    ins = pe.transpose(bank(u)[:, (g % 4) * P:(g % 4 + 1) * P],
                                       s5Qn[:, g].rearrange("p j i -> p (j i)"), ident[:])
                fill(ins, u)
            pe.wait_ge(S["s5_pp"], 1)
            for n in range(8):
                u = first["w"] + n
                claim(pe, u)
                for g in range(4 * n, 4 * n + 4):
                    ins = pe.matmul(bank(u)[0:GI, (g % 4) * P:(g % 4 + 1) * P], BB1[:, g, :], s5PP[:, g, 0:LC, :]
                                    .rearrange("p k i -> p (k i)"), start=(g % 4 == 0), stop=(g % 4 == 3),
                                    skip_group_check=True)
                fill(ins, u)
            u = first["memKT"]
            pe.wait_ge(S["memk_norm"], 1)
            for k in range(0, KT, 2):
                claim(pe, u)
                for kk in range(2):
                    for t in range(MT):
                        ins = pe.transpose(bank(u)[:, kk * NM + t * P:kk * NM + (t + 1) * P],
                                           memtok[:, t, (k + kk) * P:(k + kk + 1) * P], ident[:])
                fill(ins, u)
                u += 1

            transpose_gain_norm("mix_norm0")
            taken_all(pe, "mix_norm0", 8)
            tokens_gemm("uv", ["ev0", "ev1"], plain(xT), KT)
            panel_in(pe, "ev2")
            for n in range(4):
                u = first["s5u"] + n
                claim(pe, u)
                for k in range(KT):
                    ins = pe.matmul(bank(u)[:, :], slot("ev2")[:, k, n * P:(n + 1) * P], xT[:, k, :], start=(k == 0),
                                    stop=(k == KT - 1))
                fill(ins, u)
            u = first["ws"]
            claim(pe, u)
            pe.wait_ge(S["wide_in"], 16)
            for n in range(H):
                ins = pe.transpose(bank(u)[:, n * P:(n + 1) * P], wsN[:, n, :], ident[:])
            fill(ins, u)
            pe.wait_ge(S["ws_masked"], 1)
            pe.wait_ge(S["vh_ready"], 1)
            for n in range(H):
                u = first["mixed"] + n
                claim(pe, u)
                fill(pe.matmul(bank(u)[:, :], wsT[:, n * P:(n + 1) * P], Gv[:, :, n * P:(n + 1) * P], start=True,
                               stop=True), u)
            taken_all(pe, "mixed", 4)
            for n in range(4):
                u = first["yaT"] + n
                claim(pe, u)
                for t in range(TT):
                    ins = pe.transpose(bank(u)[:, t * P:(t + 1) * P], Gu[:, t, n * P:(n + 1) * P], ident[:])
                fill(ins, u)
            taken_all(pe, "s5u", 4)
            for j in range(LC):
                u = first["uj"] + j
                claim(pe, u)
                for n in range(4):
                    ins = pe.transpose(bank(u)[0:NC, n * P:(n + 1) * P],
                                       uT[:, n, :].rearrange("p (c j) -> p j c", j=LC)[:, j, :], ident[:])
                fill(ins, u)
            taken_all(pe, "uj", 8)
            for n in range(4):
                u = first["ucT"] + n
                claim(pe, u)
                for g in range(8):
                    ins = pe.transpose(bank(u)[:, g * NC:(g + 1) * NC], U[:, 8 * n + g].rearrange("c j i -> c (j i)"),
                                       ident[0:NC, 0:NC])
                fill(ins, u)
            taken_all(pe, "ucT", 4)
            taken_all(pe, "bT", 8)
            for n in range(4):
                u = first["V"] + n
                claim(pe, u)
                for g in range(8):
                    ins = pe.matmul(bank(u)[:, g * NC:(g + 1) * NC], s5Q[:, 8 * n + g, :], Uc[:, 8 * n + g, :],
                                    start=(g == 0), stop=(g == 7), skip_group_check=True)
                fill(ins, u)
            for n in range(4):
                u = first["Vsw"] + n
                claim(pe, u)
                taken(pe, first["V"] + n)
                fill(pe.matmul(bank(u)[:, :], perm[:], Vc[:, 8 * n:8 * n + 8, :].rearrange("p g c -> p (g c)"),
                               start=True, stop=True), u)
            pe.wait_ge(S["s5_scan"], 1)
            for n in range(4):
                u = first["Xp"] + n
                claim(pe, u)
                fill(pe.matmul(bank(u)[:, :], perm[:], Vs[:, 8 * n:8 * n + 8, :].rearrange("p g c -> p (g c)"),
                               start=True, stop=True), u)
            pe.wait_ge(S["s5_x"], 1)
            pe.wait_ge(S["s5_t"], 16 * LC)
            for n in range(8):
                u = first["y"] + n
                claim(pe, u)
                for g in range(4 * n, 4 * n + 4):
                    o = bank(u)[0:NC, (g % 4) * P:(g % 4 + 1) * P]
                    pe.matmul(o, Uc[:, g, :], s5T[:, g, :], start=(g % 4 == 0), stop=False, skip_group_check=True)
                    ins = pe.matmul(o, Sc[:, g, :], s5PP[:, g, 1:LC + 1, :].rearrange("p k i -> p (k i)"),
                                    start=False, stop=(g % 4 == 3), skip_group_check=True)
                fill(ins, u)
            taken_all(pe, "y", 8)
            for n in range(4):
                u = first["yT"] + n
                claim(pe, u)
                for j in range(LC):
                    ins = pe.transpose(bank(u)[:, j * NC:(j + 1) * NC], Y[:, j, n * P:(n + 1) * P],
                                       ident[0:NC, 0:NC])
                fill(ins, u)
            taken_all(pe, "yT", 4)
            panel_in(pe, "glu")
            for n in range(4):
                u = first["glu"] + n
                claim(pe, u)
                for k in range(4):
                    ins = pe.matmul(bank(u)[:, :], slot("glu")[:, k, n * P:(n + 1) * P], yT[:, k, :], start=(k == 0),
                                    stop=(k == 3))
                fill(ins, u)
            pe.wait_ge(S["ya_ready"], 4)
            tokens_gemm("out0", ["out00", "out01"], plain(xT), KT)
            if stage == 0:
                return

            def attention(l):
                transpose_gain_norm(f"xa_norm{l}")
                for n in range(2):
                    split_gemm(first[f"q{l}"] + 4 * n, f"wq{l}{n}", xhi, xlo["q"], lambda k: first[f"xa_norm{l}"] + k)
                for t in range(TT):
                    pe.wait_ge(S["q_norm"], 4 * l + t + 1)
                for k in range(KT):
                    u = first[f"qT{l}"] + k
                    claim(pe, u)
                    for t in range(TT):
                        ins = pe.transpose(bank(u)[:, t * P:(t + 1) * P], qtok[:, t, k * P:(k + 1) * P], ident[:])
                    fill(ins, u)
                taken_all(pe, f"qT{l}", 8)
                for t in range(TT):
                    for hp in range(2):
                        u = first[f"sc{l}"] + 2 * t + hp
                        claim(pe, u)
                        for n in range(2):
                            for kk in range(2):
                                k = 2 * (2 * hp + n) + kk
                                ins = pe.matmul(bank(u)[:, n * NM:(n + 1) * NM], qT[:, k, t * P:(t + 1) * P],
                                                memKT[:, k, :], start=(kk == 0), stop=(kk == 1))
                        fill(ins, u)
                for n in range(4):
                    for k in range(2):
                        u = first[f"pT{l}"] + 2 * n + k
                        claim(pe, u)
                        for t in range(TT):
                            if n == 0 and k == 0 and t == 0:
                                pe.wait_ge(S["probs"], 8 * l + 8)
                            ins = pe.transpose(bank(u)[:, t * P:(t + 1) * P], prob[:, t, n, k * P:(k + 1) * P], ident[:])
                        fill(ins, u)
                for n in range(4):
                    for d in range(2):
                        u = first[f"o{l}"] + 2 * n + d
                        claim(pe, u)
                        for k in range(2):
                            taken(pe, first[f"pT{l}"] + 2 * n + k)
                            ins = pe.matmul(bank(u)[:, :], memV[:, k, n * XD + d * P:n * XD + (d + 1) * P],
                                            pT[:, n, k, :], start=(k == 0), stop=(k == 1))
                        fill(ins, u)
                for n in range(2):
                    split_gemm(first[f"wo{l}"] + 4 * n, f"wo{l}{n}", ohi, xlo["o"], lambda k: first[f"o{l}"] + k)

            def experts(l):
                m = M[l]
                transpose_gain_norm(f"ffn_norm{l}")
                taken_all(pe, f"ffn_norm{l}", 8)
                u = first[f"route{l}"]
                claim(pe, u)
                for t in range(TT):
                    for k in range(KT):
                        ins = pe.matmul(bank(u)[:, 20 * t:20 * t + 20], xT[:, k, t * P:(t + 1) * P], rw[:, l, k, :],
                                        start=(k == 0), stop=(k == KT - 1), skip_group_check=True)
                fill(ins, u)
                u = first[f"rank{l}"]
                claim(pe, u)
                pe.wait_ge(m["msum_ready"], 1)
                for t in range(TT + 1):
                    for s_ in range(min(t + 1, TT)):
                        ins = pe.matmul(bank(u)[:, NE * t:NE * (t + 1)], strict[:] if s_ == t else ones[:],
                                        msum[:, s_, :], start=(s_ == 0), stop=(s_ == min(t, TT - 1)),
                                        skip_group_check=True)
                fill(ins, u)
                u = first[f"idx{l}"]
                claim(pe, u)
                pe.wait_ge(m["onehots_ready"], 1)
                for n in range(2 * TT):
                    ins = pe.matmul(bank(u)[:, 0:NI], slot1h[:, n, :], item1h[:, n, :], start=(n == 0),
                                    stop=(n == 2 * TT - 1))
                fill(ins, u)
                for v in range(u - 7, u + 1):
                    taken(pe, v)

                def later(semaphore, value):
                    if not isinstance(value, int) or value > 0:
                        pe.wait_ge(semaphore, value)

                def turn(q, par):
                    pe.wait_ge(m[f"xg_in{par}"], q * 16 + 16)
                    later(m["xt_ready"], q * 4 + 2 * par)
                    for b in range(2):
                        for k in range(4):
                            ins = pe.transpose(banks[b][:, k * P:(k + 1) * P],
                                               xg[par][:, (4 * b + k) * P:(4 * b + k + 1) * P], ident[:])
                        ins.then_inc(m["xt_filled"], 1)

                def up(q, par):
                    pe.wait_ge(m["xt_ready"], q * 4 + (2 * par + 2))
                    pe.wait_ge(m["w13a" if par == 0 else "w13b"], q * 32 + 32)
                    later(m["hid_ready"], q * 2 + (par - 1))
                    for k in range(KT):
                        ins = pe.matmul(banks[2 + par][:, :], xgT[par][:, k, :], W[par][:, k, :], start=(k == 0),
                                        stop=(k == KT - 1))
                    ins.then_inc(m["hid_filled"], 1)

                def turn_hidden(q, par):
                    pe.wait_ge(m["hid_ready"], q * 2 + (par + 1))
                    later(m["ht_ready"], q * 2 + par)
                    for k in range(2):
                        ins = pe.transpose(banks[4][:, k * P:(k + 1) * P], hid[par][:, k * P:(k + 1) * P], ident[:])
                    ins.then_inc(m["ht_filled"], 1)

                def down(q, par):
                    pe.wait_ge(m["ht_ready"], q * 2 + (par + 1))
                    pe.wait_ge(m["w2a" if par == 0 else "w2b"], q * 16 + 16)
                    w = w2s[par]
                    for half in range(2):
                        later(m[f"y_ready{half}"], q * 2 + par)
                        for k in range(2):
                            ins = pe.matmul(banks[5 + half][:, :], hT[par][:, k * P:(k + 1) * P],
                                            w[:, k, half * 512:(half + 1) * 512], start=(k == 0), stop=(k == 1))
                        ins.then_inc(m[f"y_filled{half}"], 1)

                def pair(q):
                    up(q, 1)
                    turn_hidden(q, 0)
                    turn(q + 1, 0)
                    down(q, 0)
                    up(q + 1, 0)
                    turn_hidden(q, 1)
                    turn(q + 1, 1)
                    down(q, 1)

                turn(0, 0)
                up(0, 0)
                turn(0, 1)
                pe.wait_ge(m["table_ready"], 1)
                last_pair = pe.value_load(tab[0:1, 60:61], min_val=NE // 2 - 1, max_val=NI // 2 - 1)
                pair(0)
                with pe.Fori(1, last_pair) as q:
                    pair(q)
                up(last_pair, 1)
                turn_hidden(last_pair, 0)
                down(last_pair, 0)
                turn_hidden(last_pair, 1)
                down(last_pair, 1)

            attention(0)
            if stage == 1:
                return
            experts(0)
            if stage == 2:
                return
            transpose_gain_norm("mix_norm1")
            split_gemm(first["dq"], "od0", xhi, xlo["od"], lambda k: first["mix_norm1"] + k)
            split_gemm(first["dk"], "od1", xhi, xlo["od"])
            for n in range(2):
                split_gemm(first["qk"] + 4 * n, f"od{2 + n}", xhi, xlo["od"], weights_first=True)
            split_gemm(first["v"], "od4", xhi, xlo["od"])
            split_gemm(first["og"], "od5", xhi, xlo["od"])
            u = first["if"]
            claim(pe, u)
            for t in range(TT):
                for n, x_ in enumerate((xhi, xlo["od"])):
                    for k in range(KT):
                        ins = pe.matmul(bank(u)[:, 8 * t:8 * t + 8], x_[:, k, t * P:(t + 1) * P].bitcast(F32), ifw[:, k, :],
                                        start=(k == 0 and n == 0), stop=(k == KT - 1 and n == 1), skip_group_check=True)
            fill(ins, u)
            split_gemm(first["dv"], "od6", xhi, xlo["od"])
            pe.wait_ge(S["d_norm"], 1)
            for n in range(8):
                u = first["dT"] + n
                claim(pe, u)
                src = Dq if n < 4 else Dk
                for t in range(TT):
                    ins = pe.transpose(bank(u)[:, t * P:(t + 1) * P], src[:, t, (n % 4) * P:(n % 4 + 1) * P], ident[:])
                fill(ins, u)
            taken(pe, first["if"])
            for n in range(2):
                u = first["ifT"] + n
                claim(pe, u)
                for t in range(TT):
                    ins = pe.transpose(bank(u)[0:4, t * P:(t + 1) * P], ifg[:, t, 4 * n:4 * n + 4], ident[:])
                fill(ins, u)
            u = first["col"]
            claim(pe, u)
            pe.wait_ge(S["ml_rows"], 1)
            for n, r in enumerate((arow, enrow)):
                for t in range(TT):
                    ins = pe.transpose(bank(u)[:, 16 * n + 4 * t:16 * n + 4 * t + 4], r[:, t * P:(t + 1) * P],
                                       ident[0:4, 0:4])
            fill(ins, u)
            pe.wait_ge(S["ws_masked"], 2)
            pe.wait_ge(S["qk_ready"], 8)
            taken_all(pe, "v", 4)
            for n in range(H):
                u = first[f"mlh{n}"]
                claim(pe, u)
                fill(pe.matmul(bank(u)[:, :], headsel[:, n, :], nMrow, start=True, stop=True), u)
                for s_ in range(TT):
                    u = first[f"mlh{n}"] + 1 + s_
                    claim(pe, u)
                    fill(pe.matmul(bank(u)[:, 0:T - P * s_], QKT[:, 4 + n, s_ * P:(s_ + 1) * P],
                                   QKT[:, n, s_ * P:T], start=True, stop=True), u)
                if n % 2 == 0:
                    continue
                for t in range(TT):
                    u = first[f"num{n // 2}"] + t
                    claim(pe, u)
                    for n2 in (n - 1, n):
                        for s_ in range(t + 1):
                            taken(pe, first[f"mlh{n2}"] + 1 + s_)
                            ins = pe.matmul(bank(u)[:, 256 * (n2 % 2):256 * (n2 % 2) + 129],
                                            wts(n2, s_)[:, P * (t - s_):P * (t - s_ + 1)], VML[:, s_, n2, :],
                                            start=(s_ == 0), stop=(s_ == t))
                    fill(ins, u)
            taken_all(pe, "dT", 8)

            def moba_scores(n):
                for t in range(TT):
                    u = first[f"ms{n}"] + t
                    claim(pe, u)
                    fill(pe.matmul(bank(u)[:, 0:P * (t + 1)], qdT[:, n, t * P:(t + 1) * P],
                                   kdT[:, n, 0:P * (t + 1)], start=True, stop=True), u)

            def moba_out(n):
                pe.wait_ge(S["mo_probs"], 4 * (n + 1))
                for b, ks in enumerate(((0,), (1, 3), (2,))):
                    u = first[f"mp{n}"] + b
                    claim(pe, u)
                    o = 0
                    for k in ks:
                        for t in range(k, TT):
                            ins = pe.transpose(bank(u)[:, o:o + P], pm(n, t)[:, k * P:(k + 1) * P], ident[:])
                            o += P
                    fill(ins, u)
                u = first[f"mp{n}"] + 3
                claim(pe, u)
                for b in range(3):
                    taken(pe, first[f"mp{n}"] + b)
                for k in range(TT):
                    ins = pe.matmul(bank(u)[:, k * P:T], Dv[:, k, n * P:(n + 1) * P], ptm(n, k), start=(k == 0),
                                    stop=(k == TT - 1), skip_group_check=True)
                fill(ins, u)

            moba_scores(0)
            for n in range(1, H):
                moba_scores(n)
                moba_out(n - 1)
            moba_out(H - 1)
            pe.wait_ge(S["hh_ready"], 1)
            for n in range(4):
                u = first["ycT"] + n
                claim(pe, u)
                for t in range(TT):
                    ins = pe.transpose(bank(u)[:, t * P:(t + 1) * P], hh[:, t, n * P:(n + 1) * P], ident[:])
                fill(ins, u)
            for n in range(2):
                split_gemm(first["out1"] + 4 * n, f"out1{n}", xhi, xlo["out1"],
                           lambda k: first["ycT"] + k if k < 4 else first[f"mp{k - 4}"] + 3)
            if stage == 3:
                return
            attention(1)
            if stage == 4:
                return
            experts(1)

        @block.scalar
        def _(act):
            a_ = Chain(act, "a_step")

            def h_is_ready(name, t):
                before_ = {"xa_norm0": "out0", "ffn_norm0": "wo0", "xa_norm1": "out1", "ffn_norm1": "wo1"}
                if name == "mix_norm0":
                    act.wait_ge(S["x_in"], 16 * TT)
                elif name == "mix_norm1":
                    act.wait_ge(M[0]["h_combined"], t + 1)
                else:
                    taken(act, first[before_[name]] + 4 + t)

            def high_part(u, dst, scale=1.0):
                await_filled(act, u)
                act.activation(dst, bank(u)[:, :], ACT.Copy, scale=scale).then_inc(S["x_hi"], 1)

            def weights(name, k0, k1):
                p = pnum[name]
                act.wait_ge(landed[p % 2], 16 * (p // 2 + 1))
                for k in range(k0, k1):
                    s_ = step(name, k)
                    await_ring(act, s_)
                    act.activation(whi[s_ % RING][:, :], slot(name)[:, k, :], ACT.Copy).then_inc(S["w_hi"], 1)

            def weights_between(a, b):
                weights(a, RING, KT)
                if b:
                    weights(b, 0, RING)

            def table(func):
                a_(act.activation(spare[:, 0:1], ones[:, 0:1], func))

            def norm(name, between=None):
                n = NORMS[name]
                dst = xnE if name == "mix_norm0" else v3(E[1], 4)
                table(ACT.Sqrt)
                for t in range(TT):
                    h_is_ready(name, t)
                    act.activation(dst[:, t, :], h[:, t, :], ACT.Square, accum_out=ssq[:, n, t:t + 1])\
                       .then_inc(S["stat_ready"], 1)
                if between:
                    between()
                act.wait_ge(S["mean_ready"], n + 1)
                act.activation(std[:, n, :], ssq[:, n, :], ACT.Sqrt).then_inc(S["std_ready"], 1)
                gain, lo = {"mix": ("norm_mix_g", 0), "xa_": ("norm_xa_g", 0), "ffn": ("norm_ffn_g", 0)}[name[0:3]]
                lo = 8 * int(name[-1])
                if first[name] in two_parts:
                    for k in range(KT):
                        high_part(first[name] + k, xhi[:, k, :], col(gain, lo + k))
                    return
                for k in range(0, KT, 2):
                    u = first[name] + k
                    await_filled(act, u)
                    evac(act.activation(xT[:, k, :], bank(u)[:, :], ACT.Copy, scale=col(gain, lo + k)), u)

            def copies(name, n0, n1, dst, step=1):
                for n in range(n0, n1, step):
                    u = first[name] + n
                    await_filled(act, u)
                    evac(act.activation(dst(n), bank(u)[:, :], ACT.Copy), u)

            act.dma_start(memtok, A["mem"][0].rearrange("(a p) d -> p a d", p=P)).then_inc(S["mem_in"], 16)
            for dst, src in small:
                act.dma_start(dst, src, allow_slow_non_contiguous=True).then_inc(S["small_in"], 16)
            for dst, src in s5_loads:
                act.dma_start(dst, src, allow_slow_non_contiguous=True).then_inc(S["s5_in"], 16)
            act.dma_start(wsN, A["gm_ws"][0].rearrange("h t s -> t h s")).then_inc(S["wide_in"], 16)
            act.wait_ge(S["mem_in"], 16)
            for t in range(MT):
                act.activation(memnT[:, 4 * t:4 * t + 4, :].rearrange("p a b -> p (a b)"), memtok[:, t, :], ACT.Square,
                               accum_out=ssq[:, 0, t:t + 1]).then_inc(S["stat_ready"], 1)
            act.wait_ge(S["mean_ready"], 1)
            act.activation(std[:, 0, 0:MT], ssq[:, 0, 0:MT], ACT.Sqrt).then_inc(S["std_ready"], 1)
            act.wait_ge(S["s5_in"], 16 * len(s5_loads))
            act.activation(step_, lstep, ACT.Exp).then_inc(S["s5_exp"], 1)
            act.wait_ge(S["s5_args"], 1)
            act.activation(mag, mag, ACT.Exp).then_inc(S["s5_exp"], 1)
            act.activation(rho8, are, ACT.Exp, scale=float(LC)).then_inc(S["s5_exp"], 1)
            act.wait_ge(S["s5_args"], 2)
            act.wait_ge(S["consts_ready"], 1)
            act.activation(Li, Li, ACT.Sin, scale=TWO_PI).then_inc(S["s5_sin"], 1)
            act.activation(Lr, Lr, ACT.Sin, bias=halfpi[:, 0:1], scale=-TWO_PI).then_inc(S["s5_sin"], 1)
            act.activation(s5sin, s5sin, ACT.Sin, scale=TWO_PI).then_inc(S["s5_sin"], 1)
            act.activation(s5cos, s5cos, ACT.Sin, bias=halfpi[:, 0:1], scale=-TWO_PI).then_inc(S["s5_sin"], 1)
            copies("kv", 0, 8, lambda n: (memtok if n < 4 else memV)[:, n % 2, (n // 2 % 2) * 512:(n // 2 % 2 + 1) * 512])
            taken(act, first["kv"] + 3)
            for t in range(MT):
                for n in range(4):
                    a_(act.activation(junk[:, 0:XD], memtok[:, t, n * XD:(n + 1) * XD], ACT.Square,
                                      accum_out=xmx[:, 4 * t + n:4 * t + n + 1]), "hd_sq")
            act.wait_ge(S["hmean_ready"], 1)
            act.activation(xnm[:, 0:8], xmx[:, 0:8], ACT.Sqrt).then_inc(S["hstd_ready"], 1)
            for n in range(8):
                u = first["bT"] + n
                await_filled(act, u)
                if n == 0:
                    act.wait_ge(S["s5_pp"], 1)
                evac(act.activation(E[1][:, 512 * n:512 * n + 512], bank(u)[:, :], ACT.Copy), u)
            for n in range(8):
                u = first["w"] + n
                await_filled(act, u)
                evac(act.activation(E[3][0:GI, 512 * n:512 * n + 512], bank(u)[0:GI, :], ACT.Copy), u)
            act.wait_ge(S["s5_w"], 1)
            act.dma_start(lngain, A["gm_ln_g"][0].partition_broadcast(P)).then_inc(S["wide_in"], 16)
            for j in range(LC):
                act.dma_start(s5T[GI * j:GI * (j + 1), :, GI * j:P], s5Wst[0:GI, :, 0:P - GI * j]).then_inc(S["s5_t"], 16)
            for n in range(4):
                u = first["memKT"] + n
                await_filled(act, u)
                evac(act.activation(memKT[:, 2 * n:2 * n + 2, :].rearrange("p a b -> p (a b)"), bank(u)[:, :], ACT.Copy), u)
            act.wait_ge(S["s5_t"], 16 * LC)
            norm("mix_norm0")
            for n in range(8):
                u = first["uv"] + n
                await_filled(act, u)
                dst = (Gu if n < 4 else Gv)[:, n % 4, :]
                evac(act.activation(dst, bank(u)[:, :], ACT.Gelu_apprx_tanh), u)
            act.wait_ge(S["ln_mean"], 1)
            for n in range(16):
                a_(act.activation(junk[:, 0:P], Gv[:, n // 4, (n % 4) * P:(n % 4 + 1) * P], ACT.Square,
                                  bias=xnm[:, n:n + 1], accum_out=xsum[:, n:n + 1]), "ln_sq")
            act.wait_ge(S["ln_mean"], 2)
            act.activation(xrec, xsum, ACT.Sqrt).then_inc(S["ln_sq"], 1)
            a_.n["ln_sq"] += 1
            await_filled(act, first["s5u"] + 3)
            copies("yaT", 0, 4, lambda n: xT[:, n, :])
            copies("ucT", 0, 4, lambda n: Uc[:, 8 * n:8 * n + 8, :].rearrange("p g c -> p (g c)"))
            copies("V", 0, 4, lambda n: Vc[:, 8 * n:8 * n + 8, :].rearrange("p g c -> p (g c)"))
            act.wait_ge(S["s5_x"], 1)
            for n in range(8):
                u = first["y"] + n
                await_filled(act, u)
                evac(act.activation(Y[:, :, 64 * n:64 * n + 64].rearrange("c j (g i) -> c g j i", g=4),
                                    bank(u)[0:NC, :].rearrange("c (g j i) -> c g j i", g=4, j=LC),
                                    ACT.Gelu_apprx_tanh), u)
            for n in range(4):
                u = first["yT"] + n
                await_filled(act, u)
                evac(act.activation(yT[:, n, :].rearrange("p (c j) -> p j c", j=LC),
                                    bank(u)[:, :].rearrange("p (j c) -> p j c", j=LC), ACT.Copy), u)
            for n in range(4):
                u = first["glu"] + n
                await_filled(act, u)
                evac(act.activation(sg[:, n, :], bank(u)[:, :], ACT.Sigmoid, bias=col("s5_b_glu", n)), u)
            if stage == 0:
                return

            def attention(l):
                norm(f"xa_norm{l}", lambda: weights(f"wq{l}0", 0, RING))
                weights_between(f"wq{l}0", f"wq{l}1")
                copies(f"q{l}", 0, 4, lambda n: qtok[:, n % 4, 0:512])
                weights_between(f"wq{l}1", f"wo{l}0")
                copies(f"q{l}", 4, 8, lambda n: qtok[:, n % 4, 512:1024])
                for n in range(16):
                    taken(act, first[f"q{l}"] + 4 * ((n % 4) // 2) + n // 4)
                    a_(act.activation(junk[:, 0:XD], qtok[:, n // 4, (n % 4) * XD:(n % 4 + 1) * XD], ACT.Square,
                                      accum_out=xmx[:, n:n + 1]), "hd_sq")
                act.wait_ge(S["hmean_ready"], (2, 5)[l])
                act.activation(xnm, xmx, ACT.Sqrt).then_inc(S["hstd_ready"], 1)
                for k in range(0, KT, 2):
                    u = first[f"qT{l}"] + k
                    await_filled(act, u)
                    evac(act.activation(qT[:, k, :], bank(u)[:, :], ACT.Copy, scale=g2[:, 2 * l:2 * l + 1]), u)
                table(ACT.Exp)
                for t in range(TT):
                    for hp in range(2):
                        u = first[f"sc{l}"] + 2 * t + hp
                        act.wait_ge(S["max_ready"], (0, 24)[l] + 2 * t + hp + 1)
                        for n in range(2):
                            c = 4 * t + 2 * hp + n
                            ins = act.activation(prob[:, t, 2 * hp + n, :], bank(u)[:, n * NM:(n + 1) * NM], ACT.Exp,
                                                 bias=xnm[:, c:c + 1], scale=XA_SCALE, accum_out=xsum[:, c:c + 1])
                        evac(ins, u)
                copies(f"pT{l}", 0, 8, lambda n: pT[:, n // 2, n % 2, :], 2)
                for n in range(8):
                    high_part(first[f"o{l}"] + n, ohi[:, n, :])
                weights_between(f"wo{l}0", f"wo{l}1")
                weights_between(f"wo{l}1", None)

            def experts(l):
                m = M[l]
                norm(f"ffn_norm{l}")
                for t in range(TT):
                    act.wait_ge(S["xn_ready"], 2 + 4 * (NORMS[f"ffn_norm{l}"] - 1) + t + 1)
                    act.dma_start(xs[l][t * P:(t + 1) * P, :], xn[:, t, :]).then_inc(m["xs_stored"], 16)
                act.wait_ge(m["gate_args"], 1)
                act.activation(gexp, gsub, ACT.Exp).then_inc(m["gate_exp"], 1)
                act.wait_ge(m["gate_args"], 2)
                act.activation(dexp, dsub, ACT.Exp).then_inc(m["gate_exp"], 1)

                def item(q, par):
                    act.wait_ge(m["hid_filled"], q * 2 + (par + 1))
                    act.activation(silu[par], banks[2 + par][:, 0:FF], ACT.Silu).then_inc(m["silu_ready"], 1)
                    act.wait_ge(m["ht_filled"], q * 2 + (par + 1))
                    act.activation(hT[par], banks[4][:, 0:2 * P], ACT.Copy).then_inc(m["ht_ready"], 1)
                    if not isinstance(q, int):
                        act.wait_ge(m[f"y_stored{par}"], q * 16)
                    act.wait_ge(m["y_filled1"], q * 2 + (par + 1))
                    act.activation(yo[par][:, 512:1024], banks[6][:, :], ACT.Copy).then_inc(m["y_ready1"], 1)

                item(0, 0)
                item(0, 1)
                act.wait_ge(m["table_ready"], 1)
                last_pair = act.value_load(tab[0:1, 60:61], min_val=NE // 2 - 1, max_val=NI // 2 - 1)
                with act.Fori(1, last_pair + 1) as q:
                    item(q, 0)
                    item(q, 1)

            attention(0)
            if stage == 1:
                return
            experts(0)
            if stage == 2:
                return
            norm("mix_norm1", lambda: weights("od0", 0, RING))
            act.dma_start(hngain, A["ml_hn_g"][0].partition_broadcast(P)).then_inc(S["wide_in"], 16)
            for dst, src in rope_loads:
                act.dma_start(dst, src).then_inc(S["rope_in"], 16)
            weights_between("od0", "od1")
            copies("dq", 0, 4, lambda n: Dq[:, n, :])
            weights_between("od1", "od2")
            copies("dk", 0, 4, lambda n: Dk[:, n, :])
            weights_between("od2", "od3")
            act.wait_ge(S["hmean_ready"], 3)
            act.activation(dstd, dsq, ACT.Sqrt).then_inc(S["hstd_ready"], 1)

            def taps(c0, c1):
                for ct in range(c0, c1):
                    u = first["qk"] + ct
                    await_filled(act, u)
                    act.activation(QKT[:, ct, :], bank(u)[:, :], ACT.Identity, bias=col("ml_conv_b", ct),
                                   scale=col("ml_conv_w", 24 + ct)).then_inc(S["conv_in"], 1)

            taps(0, 4)
            weights_between("od3", "od4")
            taps(4, 8)
            weights_between("od4", "od5")
            for ct in range(8):
                taken(act, first["qk"] + ct)
                act.activation(QKT[:, ct, :], QKT[:, ct, :], ACT.Silu).then_inc(S["qk_ready"], 1)
            for n in range(TT):
                u = first["v"] + n
                await_filled(act, u)
                evac(act.activation(VML[:, n, :, 0:P], bank(u)[:, :].rearrange("p (h d) -> p h d", h=4), ACT.Copy), u)
            weights_between("od5", "od6")
            for n in range(TT):
                u = first["og"] + n
                await_filled(act, u)
                evac(act.activation(SO[:, n, :], bank(u)[:, :], ACT.Sigmoid), u)
            weights_between("od6", "out10")
            copies("dv", 0, 4, lambda n: Dv[:, n, :])
            copies("dT", 0, 8, lambda n: (qdT if n < 4 else kdT)[:, n % 4, :], 2)
            act.wait_ge(S["ml_args"], 1)
            a_(act.activation(erow, lrow, ACT.Exp, scale=-1.0), "ml_act")
            a_(act.activation(lrow, erow, ACT.Ln, bias=ones[0:4, 0:1]), "ml_act")
            act.wait_ge(S["ml_args"], 2)
            act.activation(enrow, enrow, ACT.Exp, scale=-1.0).then_inc(S["ml_rows"], 1)
            taken(act, first["col"])
            for n in range(H):
                u = first[f"mlh{n}"]
                act.wait_ge(S["diag_ready"], n + 1)
                for s_ in range(TT):
                    i = 4 * n + s_
                    if i >= 2:
                        taken(act, first[f"mlh{(i - 2) // 4}"] + 1 + (i - 2) % 4)
                    d = dts(i)
                    bias = mlc[:, 4 * s_ + n:4 * s_ + n + 1]
                    if s_ < 3:
                        ins = act.activation(d[:, P:T - P * s_], bank(u)[:, P * (s_ + 1):T], ACT.Exp, bias=bias)
                        if s_ == 2:
                            evac(ins, u)
                    act.activation(d[:, 0:P], sdiag[:, P * s_:P * (s_ + 1)], ACT.Exp, bias=bias)\
                       .then_inc(S["dt_ready"], 1)
            act.wait_ge(S["hmean_ready"], 4)
            act.activation(dstd[:, 0:16], dsq[:, 0:16], ACT.Sqrt).then_inc(S["hstd_ready"], 1)

            def moba_exp(n):
                for t in range(TT):
                    u = first[f"ms{n}"] + t
                    act.wait_ge(S["max_ready"], 8 + 4 * n + t + 1)
                    if n >= 2:
                        for b in range(3):
                            await_filled(act, first[f"mp{n - 2}"] + b)
                    c = 4 * n + t
                    evac(act.activation(pm(n, t), bank(u)[:, 0:P * (t + 1)], ACT.Exp, bias=xnm[:, c:c + 1],
                                        scale=HD_SCALE, accum_out=xsum[:, c:c + 1]), u)

            def moba_turn(n):
                for b, o in ((0, 0), (2, 1024)):
                    u = first[f"mp{n}"] + b
                    w = (512, 512, 256)[b]
                    await_filled(act, u)
                    evac(act.activation(E[4][:, (n % 2) * 1280 + o:(n % 2) * 1280 + o + w], bank(u)[:, 0:w], ACT.Copy), u)
                high_part(first[f"mp{n}"] + 3, xhi[:, 4 + n, :])

            moba_exp(0)
            for n in range(1, H):
                moba_exp(n)
                moba_turn(n - 1)
            moba_turn(H - 1)
            for n in range(4):
                high_part(first["ycT"] + n, xhi[:, n, :])
            weights_between("out10", "out11")
            weights_between("out11", None)
            if stage == 3:
                return
            attention(1)
            if stage == 4:
                return
            experts(1)

        @block.vector
        def _(dve):
            v = Chain(dve, "d_step")
            tt, ts, stt = dve.tensor_tensor, dve.tensor_scalar, dve.scalar_tensor_tensor

            def bc(ap, shape):
                return ap.broadcast_to(shape)

            def last(ap, n):
                return ap.unsqueeze(len(ap.shape)).broadcast_to(list(ap.shape) + [n])

            def mid(ap, n):
                return ap.unsqueeze(1).broadcast_to([ap.shape[0], n] + list(ap.shape[1:]))

            def rstd_of(sq, std_, rec, width, s_in, s_out):
                v(ts(sq, sq, 1.0 / width, EPS, ALU.mult, ALU.add), s_in)
                dve.wait_ge(S[s_out], v.n[s_in])
                v(dve.reciprocal(rec, std_))

            def low_part(u, hi, lo, scale=1.0):
                dve.wait_ge(S["x_hi"], two_parts.index(u) + 1)
                evac(stt(lo, bank(u)[:, :], scale, hi.bitcast(F32), ALU.mult, ALU.subtract), u)

            def norm(name):
                n = NORMS[name]
                dst = xnE if name == "mix_norm0" else xn
                dve.wait_ge(S["stat_ready"], 2 + 4 * n)
                rstd_of(ssq[:, n, :], std[:, n, :], rstd[:, n, :], D, "mean_ready", "std_ready")
                for t in range(TT):
                    ts(dst[:, t, :], h[:, t, :], rstd[:, n, t:t + 1], None, ALU.mult).then_inc(S["xn_ready"], 1)
                gain = {"mix": "norm_mix_g", "xa_": "norm_xa_g", "ffn": "norm_ffn_g"}[name[0:3]]
                lo = 8 * int(name[-1])
                if first[name] in two_parts:
                    for k in range(KT):
                        low_part(first[name] + k, xhi[:, k, :], xlo["od" if name == "mix_norm1" else "q"][:, k, :],
                                 col(gain, lo + k))
                    return
                for k in range(1, KT, 2):
                    u = first[name] + k
                    await_filled(dve, u)
                    evac(ts(xT[:, k, :], bank(u)[:, :], col(gain, lo + k), None, ALU.mult), u)

            def copies(name, n0, n1, dst, step=1):
                for n in range(n0, n1, step):
                    u = first[name] + n
                    await_filled(dve, u)
                    evac(dve.tensor_copy(dst(n), bank(u)[:, :]), u)

            def add_to_h(name):
                for n in range(2):
                    for t in range(TT):
                        u = first[name] + 4 * n + t
                        await_filled(dve, u)
                        hs = h[:, t, n * 512:(n + 1) * 512]
                        evac(tt(hs, bank(u)[:, :], hs, ALU.add), u)

            dve.wait_ge(S["consts_ready"], 1)
            u = first["cols"]
            await_filled(dve, u)
            evac(dve.tensor_copy(cols[:, 0:NROWS], bank(u)[:, 0:NROWS]), u)
            dve.wait_ge(S["stat_ready"], 2)
            rstd_of(ssq[:, 0, 0:MT], std[:, 0, 0:MT], rstd[:, 0, 0:MT], D, "mean_ready", "std_ready")
            for t in range(MT):
                ts(memtok[:, t, :], memtok[:, t, :], rstd[:, 0, t:t + 1], None, ALU.mult).then_inc(S["xn_ready"], 1)
            taken(dve, u)
            for k in range(0, KT, 2):
                u = first["memT"] + k // 2
                await_filled(dve, u)
                v(ts(memnT[:, k, :], bank(u)[:, 0:NM], col("mem_norm_g", k), None, ALU.mult))
                evac(ts(memnT[:, k + 1, :], bank(u)[:, NM:2 * NM], col("mem_norm_g", k + 1), None, ALU.mult), u)
            for l in range(2):
                v(tt(g2[:, 2 * l:2 * l + 2], cols[:, vec["xa_qn_g"][0] + 2 * l:vec["xa_qn_g"][0] + 2 * l + 2],
                     cols[:, vec["xa_kn_g"][0] + 2 * l:vec["xa_kn_g"][0] + 2 * l + 2], ALU.mult))

            dve.wait_ge(S["s5_in"], 16 * len(s5_loads))
            dve.wait_ge(S["s5_exp"], 1)
            v(tt(are, lamr, step_, ALU.mult))
            v(tt(th, lami, step_, ALU.mult))
            v(ts(turn, th, 1.0 / (2.0 * np.pi), None, ALU.mult))

            def fraction(x, tmp):
                v(ts(tmp, x, ROUND, ROUND, ALU.add, ALU.subtract))
                v(tt(x, x, tmp, ALU.subtract))

            fraction(turn, n1)
            v(ts(t8, turn, float(LC), None, ALU.mult))
            fraction(t8, n1)
            K9 = mid(iof[:, 0:LC + 1], G)
            v(tt(mag, last(are, LC + 1), K9, ALU.mult), "s5_args")
            v(tt(Li, last(turn, LC + 1), K9, ALU.mult))
            fraction(Li, Lt)
            v(stt(Lr, Li, -1.0, Li, ALU.mult, ALU.max))
            v(tt(s5sin, last(t8, NC), mid(iof[:, 0:NC], G), ALU.mult))
            fraction(s5sin, s5cos)
            v(stt(s5cos, s5sin, -1.0, s5sin, ALU.mult, ALU.max), "s5_args")
            dve.wait_ge(S["s5_exp"], 3)
            dve.wait_ge(S["s5_sin"], 4)
            v(tt(Lr, Lr, mag, ALU.mult))
            v(tt(Li, Li, mag, ALU.mult))
            lr1, li1 = Lr[:, :, 1], Li[:, :, 1]
            v(ts(nr, lr1, -1.0, None, ALU.add))
            v(tt(n1, lamr, lamr, ALU.mult))
            v(tt(n2, lami, lami, ALU.mult))
            v(tt(n1, n1, n2, ALU.add))
            v(dve.reciprocal(th, n1))
            for dst, a, b, op in ((Fr, nr, li1, ALU.add), (Fi, li1, nr, ALU.subtract)):
                v(tt(n1, a, lamr, ALU.mult))
                v(tt(n2, b, lami, ALU.mult))
                v(tt(n1, n1, n2, op))
                v(tt(dst, n1, th, ALU.mult))
            v(ts(B2, B2, nsgn[:, 0:1], None, ALU.mult))
            for n, (c, sc) in enumerate(((C1, sgn[:, 0:1]), (C2, -1.0))):
                u = first["ct"] + n
                await_filled(dve, u)
                evac(ts(c, bank(u)[:, :].rearrange("p (g i) -> p g i", g=G), sc, None, ALU.mult), u)
                taken(dve, u)
            tA, tB = v3(E[4], G, 0, 512), v3(E[4], G, 512, 1024)

            def combine(dst, p, a, q, b, op=ALU.add):
                tt(tA, last(p, GI), a, ALU.mult)
                v(tt(tB, last(q, GI), b, ALU.mult))
                v(tt(dst, tA, tB, op))

            combine(BB1, Fr, B1, Fi, B2)
            combine(BB2, Fr, B2, Fi, B1, ALU.subtract)
            for j in range(LC):
                combine(s5Qn[:, :, j, :], Lr[:, :, LC - 1 - j], BB1, Li[:, :, LC - 1 - j], BB2)
            dve.nop().then_inc(S["s5_bb"], 1)
            for k in range(LC + 1):
                combine(s5PP[:, :, k, :], Lr[:, :, k], C1, Li[:, :, k], C2)
            dve.nop().then_inc(S["s5_pp"], 1)
            dve.wait_ge(S["hd_sq"], 8)
            rstd_of(xmx[:, 0:8], xnm[:, 0:8], xrec[:, 0:8], XD, "hmean_ready", "hstd_ready")
            for n in range(8):
                k = memtok[:, n // 4, (n % 4) * XD:(n % 4 + 1) * XD]
                ins = ts(k, k, xrec[:, n:n + 1], None, ALU.mult)
            ins.then_inc(S["memk_norm"], 1)
            taken_all(dve, "w", 8)
            dI = v3(E[4], G, 0, 512)[0:GI]
            v(tt(dI, mid(ident[0:GI, 0:GI], G), last(dT, GI), ALU.mult))
            W0 = s5Wst[0:GI, :, 0:GI]
            tt(W0, W0, dI, ALU.add).then_inc(S["s5_w"], 1)

            norm("mix_norm0")
            G16 = E[3][:, 2048:4096].rearrange("p (n d) -> p n d", n=16)
            taken_all(dve, "uv", 8)
            v(dve.tensor_reduce(xmx, G16, AX.X, ALU.add))
            v(ts(xnm, xmx, -1.0 / HD, None, ALU.mult), "ln_mean")
            dve.wait_ge(S["ln_sq"], 16)
            v(ts(xsum, xsum, 1.0 / HD, EPS, ALU.mult, ALU.add), "ln_mean")
            dve.wait_ge(S["ln_sq"], 17)
            v(dve.reciprocal(xmx, xrec))
            for n in range(16):
                ins = ts(G16[:, n, :], G16[:, n, :], xnm[:, n:n + 1], xmx[:, n:n + 1], ALU.add, ALU.mult)
            v(ins)
            dve.wait_ge(S["wide_in"], 32)
            tt(Gv, Gv, mid(lngain, 4), ALU.mult).then_inc(S["vh_ready"], 1)
            await_filled(dve, first["s5u"] + 3)
            copies("s5u", 0, 4, lambda n: uT[:, n, :])
            copies("ws", 0, 1, lambda n: wsT[:, :])
            dve.wait_ge(S["small_in"], 16 * len(small))
            for n in range(H):
                u = first["mixed"] + n
                await_filled(dve, u)
                g = Gu[:, :, n * P:(n + 1) * P]
                evac(stt(g, bank(u)[:, :].rearrange("p (c d) -> p c d", c=4), gbs[:, n:n + 1], g, ALU.add, ALU.mult), u)
            for j in range(LC):
                u = first["uj"] + j
                await_filled(dve, u)
                evac(dve.tensor_copy(U[:, :, j, :], bank(u)[0:NC, :].rearrange("c (g i) -> c g i", g=G)), u)
            for n in range(4):
                u = first["Vsw"] + n
                await_filled(dve, u)
                evac(tt(Vs[:, 8 * n:8 * n + 8, :], bank(u)[:, :].rearrange("p (g c) -> p g c", g=8),
                        s5sin[:, 8 * n:8 * n + 8, :], ALU.mult), u)
            taken_all(dve, "Vsw", 4)
            v(tt(Vc, Vc, s5cos, ALU.mult))
            v(tt(Vs, Vs, Vc, ALU.add))
            rho = v3(E[1], G, 0, 2048)
            v(dve.tensor_copy(rho, last(rho8, NC)))
            v(dve.memset(rho[:, :, 0:1], 0.0))
            v(dve.tensor_tensor_scan(E[4][:, 2048:4096], E[1][:, 0:2048], E[4][:, 0:2048], 0.0, ALU.mult, ALU.add))
            v(tt(Vs, Sc, s5sin, ALU.mult), "s5_scan")
            v(tt(Vc, Sc, s5cos, ALU.mult))
            v(dve.memset(Sc[:, :, 0:1], 0.0))
            for n in range(4):
                u = first["Xp"] + n
                await_filled(dve, u)
                r = slice(8 * n, 8 * n + 8)
                evac(tt(Sc[:, r, 1:NC], Vc[:, r, 0:NC - 1],
                        bank(u)[:, :].rearrange("p (g c) -> p g c", g=8)[:, :, 0:NC - 1], ALU.subtract), u)
            taken_all(dve, "Xp", 4)
            dve.nop().then_inc(S["s5_x"], 1)
            for n in range(4):
                taken(dve, first["glu"] + n)
                tt(xT[:, 4 + n, :], sg[:, n, :], yT[:, n, :], ALU.mult).then_inc(S["ya_ready"], 1)
            add_to_h("out0")

            def attention(l):
                norm(f"xa_norm{l}")
                dve.wait_ge(S["hd_sq"], 8 + 16 * l + 16)
                rstd_of(xmx, xnm, xrec, XD, "hmean_ready", "hstd_ready")
                for n in range(16):
                    q = qtok[:, n // 4, (n % 4) * XD:(n % 4 + 1) * XD]
                    ins = ts(q, q, xrec[:, n:n + 1], None, ALU.mult)
                    if n % 4 == 3:
                        v(ins, "q_norm")
                for k in range(1, KT, 2):
                    u = first[f"qT{l}"] + k
                    await_filled(dve, u)
                    evac(ts(qT[:, k, :], bank(u)[:, :], g2[:, 2 * l + 1:2 * l + 2], None, ALU.mult), u)

                def maxima(n):
                    u = first[f"sc{l}"] + n
                    await_filled(dve, u)
                    v(dve.tensor_reduce(xmx[:, 2 * n:2 * n + 2], bank(u)[:, :].rearrange("p (a m) -> p a m", a=2),
                                        AX.X, ALU.max))
                    v(ts(xnm[:, 2 * n:2 * n + 2], xmx[:, 2 * n:2 * n + 2], -XA_SCALE, None, ALU.mult), "max_ready")

                def normalise(n):
                    taken(dve, first[f"sc{l}"] + n)
                    v(dve.reciprocal(xrec[:, 2 * n:2 * n + 2], xsum[:, 2 * n:2 * n + 2]))
                    for a in range(2):
                        p_ = prob[:, n // 2, 2 * (n % 2) + a, :]
                        ins = ts(p_, p_, xrec[:, 2 * n + a:2 * n + a + 1], None, ALU.mult)
                    ins.then_inc(S["probs"], 1)

                maxima(0)
                for n in range(1, 8):
                    maxima(n)
                    normalise(n - 1)
                normalise(7)
                copies(f"pT{l}", 1, 8, lambda n: pT[:, n // 2, n % 2, :], 2)
                for n in range(8):
                    low_part(first[f"o{l}"] + n, ohi[:, n, :], xlo["o"][:, n, :])
                add_to_h(f"wo{l}")

            def first_max(x, mx, eq, onehot):
                v(dve.tensor_reduce(mx, x, AX.X, ALU.max))
                v(tt(eq, x, last(mx, 4), ALU.is_equal))
                v(tt(eq, eq, mid(rev4, 4), ALU.mult))
                v(dve.tensor_reduce(posf[:, 0:4], eq, AX.X, ALU.max))
                v(tt(onehot, eq, last(posf[:, 0:4], 4), ALU.is_equal))

            def experts(l):
                m = M[l]
                norm(f"ffn_norm{l}")
                v(ts(rev4, iof[:, 0:4], -1.0, 4.0, ALU.mult, ALU.add))
                v(ts(full, iof[:, 0:NX], float(P), float(P), ALU.mult, ALU.add))
                v(ts(base, iof[:, 0:NE], float(P), None, ALU.mult))
                v(dve.memset(zero, 0.0))
                u = first[f"route{l}"]
                await_filled(dve, u)
                dve.wait_ge(S["small_in"], 16 * len(small))
                evac(tt(lg, bank(u)[:, 0:80].rearrange("p (t n) -> p t n", t=4), mid(rbias[:, l, :], 4), ALU.add), u)
                taken(dve, u)
                gl = lg[:, :, 0:4]
                first_max(gl, gmax, geq, gf)
                v(tt(gsub, gl, last(gmax, 4), ALU.subtract))
                dve.nop().then_inc(m["gate_args"], 1)
                el = lg[:, :, 4:20].rearrange("p t (g e) -> p t g e", g=4)
                s16 = sel16.rearrange("p t (g e) -> p t g e", g=4)
                v(tt(s16, el, last(gf, 4), ALU.mult))
                v(dve.tensor_reduce(sel, sel16.rearrange("p t (g e) -> p t e g", g=4), AX.X, ALU.add))
                first_max(sel, m1, tmp4, f1)
                v(stt(sel2, f1, -BIG, sel, ALU.mult, ALU.add))
                first_max(sel2, m2, tmp4, f2)
                v(tt(dsub, m2, m1, ALU.subtract))
                dve.nop().then_inc(m["gate_args"], 1)
                for mm, f in zip(M12, (f1, f2)):
                    v(tt(mm.rearrange("p t (g e) -> p t g e", g=4), last(gf, 4),
                         f.unsqueeze(2).broadcast_to([P, 4, 4, 4]), ALU.mult))
                tt(msum, M12[0], M12[1], ALU.add).then_inc(m["msum_ready"], 1)
                dve.wait_ge(m["gate_exp"], 2)
                v(dve.tensor_reduce(gs, gexp, AX.X, ALU.add))
                v(dve.reciprocal(gp, gs))
                v(ts(gs, dexp, 1.0, None, ALU.add))
                v(dve.reciprocal(gmax, gs))
                v(tt(gate[:, 0, :], gmax, gp, ALU.mult))
                v(tt(gate[:, 1, :], gate[:, 0, :], dexp, ALU.mult))
                u = first[f"rank{l}"]
                await_filled(dve, u)
                evac(dve.tensor_copy(rank[:, :], bank(u)[:, 0:5 * NE]), u)
                taken(dve, u)
                R, cnt = rank[:, 0:4 * NE].rearrange("p (t e) -> p t e", t=4), rank[:, 4 * NE:5 * NE]
                v(tt(c3(more), last(cnt, NX), mid(full, NE), ALU.is_gt))
                v(dve.tensor_tensor_scan(cum, more, zero, 0.0, ALU.add, ALU.add))
                v(tt(xbase, c3(cum)[:, :, 0], c3(more)[:, :, 0], ALU.subtract))
                v(ts(xbase, xbase, float(P), float((NE - 1) * P), ALU.mult, ALU.add))
                v(tt(base, base, xbase, ALU.subtract))
                v(ts(RB, R, float(P), None, ALU.is_lt))
                v(tt(RB, RB, mid(base, 4), ALU.mult))
                v(tt(RB, RB, R, ALU.add))
                v(tt(RB, RB, mid(xbase, 4), ALU.add))
                for j in range(2):
                    v(tt(sel16, M12[j], RB, ALU.mult))
                    v(dve.tensor_reduce(posf[:, 4 * j:4 * j + 4], sel16, AX.X, ALU.add))
                v(dve.tensor_copy(pos[:, :, :], posf.rearrange("p (j t) -> p j t", j=2)))
                posw = pos[:, :, :].rearrange("p j t -> p (j t)")
                v(ts(itemi[:, :], posw, P.bit_length() - 1, None, ALU.logical_shift_right))
                v(dve.tensor_copy(itemf, itemi[:, :]))
                v(stt(slotf, itemf, -float(P), posf, ALU.mult, ALU.add))
                v(tt(slot1h, mid(iof[:, :], 8), last(slotf, P), ALU.is_equal))
                v(tt(item1h, mid(iof[:, 0:NI], 8), last(itemf, NI), ALU.is_equal))
                tt(item1h, item1h, last(tokf[:, :], NI), ALU.mult).then_inc(m["onehots_ready"], 1)
                v(dve.tensor_copy(c3(epx), last(iof[0:1, 0:NE], NX)))
                v(ts(nth, iof[0:1, 0:8], 1.0, None, ALU.add))
                b1, b2 = v3(big1, 8), v3(big2, 8)
                v(tt(b1, mid(cum[0:1, :], 8), last(nth, NE * NX), ALU.is_equal))
                v(tt(b1, b1, mid(more[0:1, :], 8), ALU.mult))
                v(tt(b2, b1, mid(epx, 8), ALU.mult))
                u = first[f"idx{l}"]
                await_filled(dve, u)
                evac(dve.tensor_copy(slots[:, :], bank(u)[:, 0:NI]), u)
                taken(dve, u)
                dve.nop().then_inc(m["slots_ready"], 1)
                dve.nop().then_inc(m["pos_ready"], 1)
                v(dve.memset(tabf, 0.0))
                v(dve.tensor_copy(tabf[:, 0:NE], iof[0:1, 0:NE]))
                v(dve.tensor_reduce(tabf[:, NE:NE + 8], b2, AX.X, ALU.add))
                v(ts(half_, iof[0:1, 0:4], 2.0, 1.0, ALU.mult, ALU.add))
                v(tt(half_, cum[0:1, NE * NX - 1:NE * NX].broadcast_to([1, 4]), half_, ALU.is_ge))
                v(dve.tensor_reduce(tabf[:, 60:61], half_, AX.X, ALU.add))
                v(ts(tabf[:, 60:61], tabf[:, 60:61], float(NE // 2 - 1), None, ALU.add))
                v(dve.tensor_copy(tab[0:1, :], tabf))
                dve.nop().then_inc(m["table_ready"], 1)
                ga = vec["norm_ffn_g"][0] + 8 * l

                def turn(q, par):
                    for b in range(2):
                        dve.wait_ge(m["xt_filled"], q * 4 + (2 * par + b + 1))
                        tt(xgT[par][:, 4 * b:4 * b + 4, :], banks[b][:, :].rearrange("p (k t) -> p k t", k=4),
                           last(cols[:, ga + 4 * b:ga + 4 * b + 4], P), ALU.mult).then_inc(m["xt_ready"], 1)

                def hidden(q, par):
                    dve.wait_ge(m["silu_ready"], q * 2 + (par + 1))
                    tt(hid[par], silu[par], banks[2 + par][:, FF:2 * FF], ALU.mult).then_inc(m["hid_ready"], 1)

                def output(q, par):
                    if not isinstance(q, int):
                        dve.wait_ge(m[f"y_stored{par}"], q * 16)
                    dve.wait_ge(m["y_filled0"], q * 2 + (par + 1))
                    dve.tensor_copy(yo[par][:, 0:512], banks[5][:, :]).then_inc(m["y_ready0"], 1)

                turn(0, 0)
                turn(0, 1)
                for par in range(2):
                    hidden(0, par)
                    turn(1, par)
                    output(0, par)
                last_pair = dve.value_load(tab[0:1, 60:61], min_val=NE // 2 - 1, max_val=NI // 2 - 1)
                with dve.Fori(1, last_pair) as q:
                    for par in range(2):
                        hidden(q, par)
                        turn(q + 1, par)
                        output(q, par)
                for par in range(2):
                    hidden(last_pair, par)
                    output(last_pair, par)
                for t in range(TT):
                    dve.wait_ge(m[f"y_gathered{t}"], 32)
                    for j in range(2):
                        if j:
                            dve.wait_ge(m["h_half"], t + 1)
                        stt(h[:, t, :], Yg[j][:, t, :], gate[:, j, t:t + 1], h[:, t, :], ALU.mult, ALU.add)\
                            .then_inc(m["h_combined" if j else "h_half"], 1)

            def finish():
                dve.nop().then_inc(S["final"], 4)

            if stage == 0:
                taken_all(dve, "out0", 8)
                finish()
                return
            attention(0)
            if stage == 1:
                taken_all(dve, "wo0", 8)
                finish()
                return
            experts(0)
            if stage == 2:
                dve.wait_ge(M[0]["h_combined"], 4)
                finish()
                return

            norm("mix_norm1")
            v(dve.memset(VML[:, :, :, P:P + 1], 1.0))
            taken_all(dve, "dq", 4)
            taken_all(dve, "dk", 4)
            dve.wait_ge(S["rope_in"], 16 * len(rope_loads))
            for n, d in enumerate((E[1][:, 0:2048], E[1][:, 2048:4096])):
                v(tt(E[4][:, 0:2048], d, d, ALU.mult))
                v(dve.tensor_reduce(dsq[:, 16 * n:16 * n + 16], v3(E[4], 16, 0, 2048), AX.X, ALU.add))
            rstd_of(dsq, dstd, drec, HD, "hmean_ready", "hstd_ready")
            def rotate(n):
                d = E[1][:, 2048 * n:2048 * n + 2048]
                dd = v3(d, 16)
                v(tt(dd, dd, last(drec[:, 16 * n:16 * n + 16], P), ALU.mult))
                v(tt(dd, dd, mid(dgain[n], 16), ALU.mult))
                x4 = d.rearrange("p (t h d) -> p t h d", t=4, h=4)
                x1, x2 = x4[:, :, :, 0:64], x4[:, :, :, 64:128]
                ca = ropec.unsqueeze(2).broadcast_to([P, 4, 4, 64])
                sa = ropes.unsqueeze(2).broadcast_to([P, 4, 4, 64])
                r = [E[4][:, 1024 * i:1024 * i + 1024].rearrange("p (t h d) -> p t h d", t=4, h=4) for i in range(4)]
                tt(r[0], x1, ca, ALU.mult)
                tt(r[1], x2, sa, ALU.mult)
                tt(r[2], x1, sa, ALU.mult)
                v(tt(r[3], x2, ca, ALU.mult))
                tt(x1, r[0], r[1], ALU.subtract)
                v(tt(x2, r[2], r[3], ALU.add))

            def convolve(c0, c1):
                for ct in range(c0, c1):
                    u = first["qk"] + ct
                    dve.wait_ge(S["conv_in"], ct + 1)
                    for k in range(1, 4):
                        o = QKT[:, ct, k:T]
                        ins = stt(o, bank(u)[:, 0:T - k], col("ml_conv_w", 8 * (3 - k) + ct), o, ALU.mult, ALU.add)
                        if k < 3:
                            v(ins)
                    evac(ins, u)

            convolve(0, 4)
            rotate(0)
            convolve(4, 8)
            rotate(1)
            dve.nop().then_inc(S["d_norm"], 1)
            u = first["if"]
            await_filled(dve, u)
            evac(tt(ifg, bank(u)[:, 0:32].rearrange("p (t n) -> p t n", t=4), mid(ifb[:, :], 4), ALU.add), u)
            copies("dT", 1, 8, lambda n: (qdT if n < 4 else kdT)[:, n % 4, :], 2)
            for n, r in enumerate((Irow, Frow)):
                u = first["ifT"] + n
                await_filled(dve, u)
                evac(dve.tensor_copy(r, bank(u)[0:4, :]), u)
                taken(dve, u)
            v(stt(lrow, Frow, -1.0, Frow, ALU.mult, ALU.max), "ml_args")
            v(ts(Frow, Frow, 0.0, None, ALU.min))
            dve.wait_ge(S["ml_act"], 2)
            v(tt(Frow, Frow, lrow, ALU.subtract))
            v(dve.memset(erow, 0.0))
            v(dve.tensor_tensor_scan(Brow, Frow, erow, 0.0, ALU.add, ALU.add))
            v(tt(arow, Irow, Brow, ALU.subtract))
            v(dve.tensor_tensor_scan(Mrow, arow, arow, 0.0, ALU.max, ALU.max))
            v(ts(nMrow, Mrow, -1.0, None, ALU.mult))
            v(tt(enrow, Brow, Mrow, ALU.add), "ml_args")
            u = first["col"]
            await_filled(dve, u)
            evac(dve.tensor_copy(mlc, bank(u)[:, 0:32]), u)
            taken(dve, u)
            for n in range(H):
                u = first[f"mlh{n}"]
                await_filled(dve, u)
                if n:
                    dve.wait_ge(S["dt_ready"], 4 * n)
                v(tt(v3(sdiag, 4), bank(u)[:, :].rearrange("p (s t) -> p s t", s=4), mid(after[:], 4), ALU.add),
                  "diag_ready")
                if n == 2:
                    for t in range(TT):
                        await_filled(dve, first["num0"] + t)
                for s_ in range(TT):
                    u = first[f"mlh{n}"] + 1 + s_
                    await_filled(dve, u)
                    dve.wait_ge(S["dt_ready"], 4 * n + s_ + 1)
                    evac(stt(wts(n, s_), bank(u)[:, 0:T - P * s_], HD_SCALE, dts(4 * n + s_)[:, 0:T - P * s_],
                             ALU.mult, ALU.mult), u)
                if n % 2 == 0:
                    continue
                for t in range(TT):
                    u = first[f"num{n // 2}"] + t
                    await_filled(dve, u)
                    b = bank(u)[:, :].rearrange("p (a c) -> p a c", a=2)
                    dn = st[:, 228:230]
                    v(stt(dn, b[:, :, P], -1.0, mlc[:, 16 + 4 * t + n - 1:16 + 4 * t + n + 1], ALU.mult, ALU.max))
                    v(tt(dn, b[:, :, P], dn, ALU.max))
                    v(dve.reciprocal(st[:, 230:232], dn))
                    for a in range(2):
                        ins = ts(hh[:, t, (n - 1 + a) * P:(n + a) * P], b[:, a, 0:P], st[:, 230 + a:231 + a], None, ALU.mult)
                    evac(ins, u)
                    taken(dve, u)
            h16 = E[1][:, 0:2048].rearrange("p (n d) -> p n d", n=16)
            v(tt(E[1][:, 2048:4096], E[1][:, 0:2048], E[1][:, 0:2048], ALU.mult))
            v(dve.tensor_reduce(dsq[:, 0:16], v3(E[1], 16, 2048, 4096), AX.X, ALU.add))
            rstd_of(dsq[:, 0:16], dstd[:, 0:16], drec[:, 0:16], HD, "hmean_ready", "hstd_ready")
            v(tt(h16, h16, last(drec[:, 0:16], P), ALU.mult))
            dve.wait_ge(S["wide_in"], 48)
            v(tt(hh, hh, mid(hngain, 4), ALU.mult))
            taken_all(dve, "og", 4)
            v(tt(hh, hh, SO, ALU.mult), "hh_ready")

            def moba_max(n):
                for t in range(TT):
                    u = first[f"ms{n}"] + t
                    await_filled(dve, u)
                    c = 4 * n + t
                    v(tt(bank(u)[:, P * t:P * (t + 1)], bank(u)[:, P * t:P * (t + 1)], before[:], ALU.add))
                    v(dve.tensor_reduce(xmx[:, c:c + 1], bank(u)[:, 0:P * (t + 1)], AX.X, ALU.max))
                    v(ts(xnm[:, c:c + 1], xmx[:, c:c + 1], -HD_SCALE, None, ALU.mult), "max_ready")

            def moba_probs(n):
                for t in range(TT):
                    taken(dve, first[f"ms{n}"] + t)
                    c = 4 * n + t
                    v(dve.reciprocal(xrec[:, c:c + 1], xsum[:, c:c + 1]))
                    ts(pm(n, t), pm(n, t), xrec[:, c:c + 1], None, ALU.mult).then_inc(S["mo_probs"], 1)

            def moba_turn(n):
                u = first[f"mp{n}"] + 1
                await_filled(dve, u)
                o = (n % 2) * 1280 + 512
                evac(dve.tensor_copy(E[4][:, o:o + 512], bank(u)[:, :]), u)
                low_part(first[f"mp{n}"] + 3, xhi[:, 4 + n, :], xlo["out1"][:, 4 + n, :])

            moba_max(0)
            for n in range(1, H):
                moba_probs(n - 1)
                moba_max(n)
                moba_turn(n - 1)
            moba_probs(H - 1)
            moba_turn(H - 1)
            for n in range(4):
                low_part(first["ycT"] + n, xhi[:, n, :], xlo["out1"][:, n, :])
            add_to_h("out1")
            if stage == 3:
                taken_all(dve, "out1", 8)
                finish()
                return
            attention(1)
            if stage == 4:
                taken_all(dve, "wo1", 8)
                finish()
                return
            experts(1)
            dve.wait_ge(M[1]["h_combined"], 4)
            finish()


_INS = ["x", "mem", "mem_norm_g", "w_mem_kv", "norm_mix_g", "norm_xa_g", "norm_ffn_g", "xa_wq", "xa_wo", "xa_qn_g",
        "xa_kn_g", "moe_w_grp", "moe_b_grp", "moe_w_exp", "moe_b_exp", "moe_w1", "moe_w3", "moe_w2", "ev_w_in",
        "ev_w_out", "gm_ws", "gm_bs", "gm_ln_g", "s5_lam_re", "s5_lam_im", "s5_b_re", "s5_b_im", "s5_c_re", "s5_c_im",
        "s5_d", "s5_log_step", "s5_w_glu", "s5_b_glu", "od_w_in", "od_w_out", "ml_conv_w", "ml_conv_b", "ml_b_if",
        "ml_hn_g", "mb_qn_g", "mb_kn_g"]


def rope_tables(tokens, half, theta=10000.0):
    freq = np.float32(theta) ** (-np.arange(half, dtype=np.float32) / np.float32(half))
    angle = np.arange(tokens, dtype=np.float32)[:, None] * freq[None, :].astype(np.float32)
    return np.cos(angle).astype(np.float32), np.sin(angle).astype(np.float32)


def kernel(**inputs):
    import concourse.bacc as bacc
    from concourse.bass_utils import run_bass_kernel_spmd

    nc = bacc.Bacc("TRN2", target_bir_lowering=False, num_devices=1)
    arrays, args = {}, {}
    for name in _INS:
        arrays[f"in_{name}"] = np.ascontiguousarray(inputs[name])
    arrays["in_rope_cos"], arrays["in_rope_sin"] = rope_tables(512, 64)
    for name, a in arrays.items():
        args[name[3:]] = nc.dram_tensor(name, a.shape, mybir.dt.from_np(a.dtype), kind="ExternalInput").ap()
    out = nc.dram_tensor("out_h", (1, 512, 1024), F32, kind="ExternalOutput").ap()
    program(nc, args, out)
    r = run_bass_kernel_spmd(nc, [arrays], core_ids=[0])
    return r.results[0]["out_h"]
```

```python
from contextlib import ExitStack

import concourse.bass as bass
import numpy as np
from concourse import mybir

F32 = mybir.dt.float32
F32R = mybir.dt.float32r
BF16 = mybir.dt.bfloat16
I32 = mybir.dt.int32
U32 = mybir.dt.uint32
ACT = mybir.ActivationFunctionType
ALU = mybir.AluOpType
AX = mybir.AxisListType

P = 128
BIG = 1.0e30
TWO_PI = 6.283185
ROUND = 1.5 * 2.0 ** 23
EPS = 1e-6


def uses_of_banks(layers):
    steps = [("cols", 1), ("memT", 4), ("kv0", 2), ("ct", 2), ("kv1", 6), ("bT", 8), ("w", 8), ("memKT", 4)]

    def attention(l):
        return [(f"xa_norm{l}", 8), (f"q{l}", 8), (f"qT{l}", 8), (f"sc{l}", 8), (f"pT{l}", 8), (f"o{l}", 8),
                (f"wo{l}", 8)]

    def moe(l):
        return [(f"ffn_norm{l}", 8), (f"route{l}", 1), (f"rank{l}", 1), (f"idx{l}", 1)]

    steps += [("mix_norm0", 8), ("uv", 8), ("s5u", 4), ("ws", 1), ("mixed", 4), ("yaT", 4), ("uj", 8), ("ucT", 4), ("V", 4),
              ("Vsw", 4), ("Xp", 4), ("y", 8), ("yT", 4), ("glu", 4), ("out0", 8)]
    steps += attention(0) + moe(0)
    steps += [("mix_norm1", 8), ("dq", 4), ("if", 1), ("dk", 4), ("ifT", 2), ("qk", 8), ("col", 1),
              ("v", 4), ("og", 4), ("dv", 4), ("dT", 8), ("mlh0", 5), ("mlh1", 5), ("num0", 4), ("mlh2", 5), ("mlh3", 5),
              ("num1", 4), ("ms0", 4), ("ms1", 4), ("mp0", 4), ("ms2", 4), ("mp1", 4), ("ms3", 4), ("mp2", 4),
              ("mp3", 4), ("ycT", 4), ("out1", 8)]
    steps += attention(1) + moe(1)
    first, n = {}, 0
    for name, k in steps:
        first[name] = n
        n += k
    return first


def program(nc, A, out):
    T, D = A["x"].shape[1:]
    MIX = D // 2
    TT, KT = T // P, D // P
    NM = A["mem"].shape[1]
    MT = NM // P
    H, HD = 4, 128
    XD = D // 4
    G, GI, NS = A["s5_b_re"].shape[1], A["s5_b_re"].shape[3], A["s5_b_re"].shape[2]
    LC = P // GI
    NC = T // LC
    NE, FF = A["moe_w1"].shape[1], A["moe_w1"].shape[3]
    NX = T // P - 1
    NI = NE + 2 * T // P
    XA_SCALE = float(XD) ** -0.5
    HD_SCALE = float(HD) ** -0.5
    first = uses_of_banks(2)
    RING = 4

    ctx = ExitStack()
    with ctx:
        def sb(name, shape, dt=F32):
            return ctx.enter_context(nc.sbuf_tensor(name, shape, dt))

        def sem(name):
            return ctx.enter_context(nc.semaphore(name))

        banks = [ctx.enter_context(nc.psum_tensor(f"bank{i}", [P, 512], F32)) for i in range(8)]
        filled = [sem(f"filled{i}") for i in range(8)]
        evacuated = [sem(f"evacuated{i}") for i in range(8)]

        with ExitStack() as shared:
            xTr, E0r, E1r, E2r, E4r, E5r, E3r = [
                shared.enter_context(nc.sbuf_tensor(f"{n}r", [P, w], F32R))
                for n, w in (("xT", KT * T), ("E0", 4096), ("E1", 4096), ("E2", 4096), ("E4", 4096),
                             ("E5", G * (LC + 1) * GI), ("E3", 4096))]
        xT = sb("xT", [P, KT, T])
        E = {i: sb(f"E{i}", [P, 4096]) for i in (0, 1, 2, 4)}
        E5 = sb("E5", [P, G * (LC + 1) * GI])
        E[3] = sb("E3", [P, 4096])
        h = sb("h", [P, TT, D])
        W = [sb(f"W{i}", [P, KT, 512]) for i in range(2)]
        whi = [sb(f"whi{i}", [P, 512], F32R) for i in range(RING)]
        wlo = [sb(f"wlo{i}", [P, 512], F32R) for i in range(RING)]
        memKT = sb("memKT", [P, KT, NM])
        memV = sb("memV", [P, MT, D])
        ident = sb("ident", [P, P])
        perm = sb("perm", [P, P])
        after = sb("after", [P, P])
        before = sb("before", [P, P])
        strict = E[0][:, P:2 * P]
        ones = sb("ones", [P, P])
        strict16 = sb("strict16", [P, P], BF16)
        ones16 = sb("ones16", [P, P], BF16)
        msum = sb("msum", [P, TT, NE], BF16)
        wsT = sb("wsT", [P, 4 * P])
        sgn = sb("sgn", [P, 1])
        nsgn = sb("nsgn", [P, 1])
        halfpi = sb("halfpi", [P, 1])
        cols = sb("cols", [P, P])
        spare = sb("spare", [P, 1])
        ssq = sb("ssq", [P, 7, 4])
        std = sb("std", [P, 7, 4])
        rstd = sb("rstd", [P, 7, 4])
        rw = sb("rw", [P, 2, KT, 20])
        rbias = sb("rbias", [P, 2, 20])
        ifw = sb("ifw", [P, KT, 8])
        ifb = sb("ifb", [P, 8])
        gbs = sb("gbs", [P, 4])
        sm = sb("sm", [P, 640])
        st = sb("st", [P, 256])
        junk = sb("junk", [P, 256])
        rows = junk[:, 0:P]
        iot = E[0][:, 0:P].bitcast(I32)
        iof = sb("iof", [P, P])
        tab = sb("tab", [P, 64], I32)
        toki = sb("toki", [P, 2 * TT], I32)
        tokf = sb("tokf", [P, 2 * TT])
        pos = sb("pos", [P, 2, 4], U32)
        itemi = sb("itemi", [P, 8], U32)
        gate = sb("gate", [P, 2, 4])
        slots = sb("slots", [P, NI], U32)
        idx = sb("idx", [P, 2], U32)

        xs = [nc.dram_tensor(f"xs{l}", [T, D], F32).ap() for l in range(2)]
        ybuf = [nc.dram_tensor(f"ybuf{l}", [NI * P, D], F32).ap() for l in range(2)]

        names = """x_in rows_in small_in lngain_in s5_in lam_in zeros_ready s5_b2 rstd_ready consts_ready wide_in rope_in mem_in panel0 panel1 x_hi w_hi w_lo w_used
        stat_ready hmean_ready hstd_ready mean_ready std_ready xn_ready s5_args s5_exp s5_sin s5_bb s5_pp s5_w s5_t memk_norm
        ln_mean ln_sq vh_ready ws_masked s5_scan s5_x ya_hi gated ya_lo hd_sq max_ready probs mo_probs
        a_step d_step p_step qk_ready d_norm ml_args ml_act ml_rows diag_ready dt_ready conv_in hh_sq hh_rstd hh_ready
        spare_rows out_stored""".split()
        S = {n: sem(n) for n in names}
        per_layer = """xs_stored onehots_ready slots_ready table_ready gate_args gate_exp pos_ready msum_ready w13a w13b w2a w2b w2_hi w2_lo ht_hi
        idx_ready pool_waited xg_in0 xg_in1 xt_filled xt_ready hid_filled silu_ready hid_ready ht_filled ht_ready
        y_filled0 y_filled1 y_ready0 y_ready1 y_stored0 y_stored1 y_gathered0 y_gathered1 y_gathered2 y_gathered3
        h_half h_combined""".split()
        M = [{n: sem(f"{n}_{l}") for n in per_layer} for l in range(2)]

        block = ctx.enter_context(nc.Block())

        def bank(u):
            return banks[u % 8]

        def claim(pe, u):
            if u >= 8:
                pe.wait_ge(evacuated[u % 8], u // 8)

        def fill(ins, u):
            ins.then_inc(filled[u % 8], 1)

        def await_filled(eng, u):
            eng.wait_ge(filled[u % 8], u // 8 + 1)

        def evac(ins, u):
            ins.then_inc(evacuated[u % 8], 1)

        def taken(eng, u):
            eng.wait_ge(evacuated[u % 8], u // 8 + 1)

        def taken_all(eng, name, n):
            for u in range(first[name] + max(0, n - 8), first[name] + n):
                taken(eng, u)

        class Chain:

            def __init__(self, eng, own):
                self.eng, self.own, self.n = eng, own, {}

            def __call__(self, ins, s=None):
                s = s or self.own
                self.n[s] = self.n.get(s, 0) + 1
                ins.then_inc(S[s], 1)
                self.eng.wait_ge(S[s], self.n[s])

        vec, at = {}, 0
        for name, n in (("mem_norm_g", 8), ("norm_mix_g", 16), ("norm_xa_g", 16), ("norm_ffn_g", 16),
                        ("xa_qn_g", 4), ("xa_kn_g", 4), ("ml_conv_w", 32), ("ml_conv_b", 8), ("s5_b_glu", 4)):
            vec[name] = (at, n)
            at += n
        NROWS = at

        def col(name, i):
            return cols[:, vec[name][0] + i:vec[name][0] + i + 1]

        w_kv = A["w_mem_kv"].rearrange("(k p) n -> p k n", p=P)
        w_ev = A["ev_w_in"][0].rearrange("(k p) n -> p k n", p=P)
        w_evo = A["ev_w_out"][0].rearrange("(k p) n -> p k n", p=P)
        w_glu = A["s5_w_glu"][0].rearrange("(k p) n -> p k n", p=P)
        w_od = A["od_w_in"][0].rearrange("(k p) n -> p k n", p=P)
        w_odo = A["od_w_out"][0].rearrange("(k p) n -> p k n", p=P)
        w_q = [A["xa_wq"][l].rearrange("(k p) n -> p k n", p=P) for l in range(2)]
        w_o = [A["xa_wo"][l].rearrange("(k p) n -> p k n", p=P) for l in range(2)]
        panels, pnum = [], {}

        def panel(name, src, last):
            pnum[name] = len(panels)
            panels.append((src, last))

        for n in range(4):
            panel(f"kv{n}", w_kv[:, :, n * 512:(n + 1) * 512], first["kv0"] + 1 if n == 0 else first["kv1"] + 2 * n - 1)
        for n, (s, k) in enumerate((("uv", 3), ("uv", 7), ("s5u", 3))):
            panel(f"ev{n}", w_ev[:, :, n * 512:(n + 1) * 512], first[s] + k)
        panel("glu", w_glu, first["glu"] + 3)
        for n in range(2):
            panel(f"out0{n}", w_evo[:, :, n * 512:(n + 1) * 512], first["out0"] + 4 * n + 3)
        for l in range(2):
            if l == 1:
                q0 = 4 * MIX + 8
                for n, (s, k, c) in enumerate((("dq", 3, q0), ("dk", 3, q0 + 512), ("qk", 3, 0), ("qk", 7, 512),
                                               ("v", 3, 1024), ("og", 3, 1536), ("dv", 3, q0 + 1024))):
                    panel(f"od{n}", w_od[:, :, c:c + 512], first[s] + k)
                for n in range(2):
                    panel(f"out1{n}", w_odo[:, :, n * 512:(n + 1) * 512], first["out1"] + 4 * n + 3)
            for n in range(2):
                panel(f"wq{l}{n}", w_q[l][:, :, n * 512:(n + 1) * 512], first[f"q{l}"] + 4 * n + 3)
            for n in range(2):
                panel(f"wo{l}{n}", w_o[l][:, :, n * 512:(n + 1) * 512], first[f"wo{l}"] + 4 * n + 3)
        first_of_layer1 = pnum["od0"]
        landed = [S["panel0"], S["panel1"]]

        def slot(name):
            return W[pnum[name] % 2]

        def panel_in(pe, name):
            p = pnum[name]
            pe.wait_ge(landed[p % 2], 16 * (p // 2 + 1))

        split_panels = [f"ev{n}" for n in range(3)] + ["out00", "out01"] + \
                       [f"{w}0{n}" for w in ("wq", "wo") for n in range(2)] + [f"od{n}" for n in range(7)] + \
                       [f"{w}1{n}" for w in ("out", "wq", "wo") for n in range(2)]

        def step(name, k):
            return split_panels.index(name) * KT + k

        def await_ring(eng, s_):
            i, k = divmod(s_ - RING, KT)
            if i >= 0:
                if k < KT - 1:
                    eng.wait_ge(S["w_used"], (KT - 1) * i + k + 1)
                else:
                    await_filled(eng, panels[pnum[split_panels[i]]][1])

        two_parts = [first["mix_norm0"] + k for k in range(8)] + \
                    [first["xa_norm0"] + k for k in range(8)] + [first["o0"] + k for k in range(8)] + \
                    [first["mix_norm1"] + k for k in range(8)] + [first[f"mp{n}"] + 3 for n in range(4)] + \
                    [first["ycT"] + k for k in range(4)] + [first["xa_norm1"] + k for k in range(8)] + \
                    [first["o1"] + k for k in range(8)]

        rope_c = A["rope_cos"].rearrange("(a p) d -> p a d", p=P)
        rope_s = A["rope_sin"].rearrange("(a p) d -> p a d", p=P)
        w1 = A["moe_w1"].rearrange("l e (k p) f -> (l e) p k f", p=P)
        w3 = A["moe_w3"].rearrange("l e (k p) f -> (l e) p k f", p=P)
        w2 = A["moe_w2"].rearrange("l e (k p) d -> (l e) p k d", p=P)

        def v3(buf, a, lo=0, hi=None):
            hi = buf.shape[1] if hi is None else hi
            return buf[:, lo:hi].rearrange("p (a b) -> p a b", a=a)

        xn = v3(E[0], 4)
        s5T = v3(E[0], G)
        s5Q = v3(E[1], G)
        s5cos = v3(E[2], G, 0, G * NC)
        s5sin = v3(E[2], G, G * NC, 2 * G * NC)
        s5PP = E5[:, :].rearrange("p (g k i) -> p g k i", g=G, k=LC + 1)
        s5Qn = E[3][:, :].rearrange("p (g j i) -> p g j i", g=G, j=LC)
        s5Wst = v3(E[3], G)
        xnE = v3(E[4], 4)
        Gu = v3(E[4], 4, 0, 2048)
        Gv = v3(E[4], 4, 2048, 4096)
        U = E[4][0:NC, :].rearrange("c (g j i) -> c g j i", g=G, j=LC)
        Uc = v3(E[3], G, 2048, 4096)
        Vc = v3(E[3], G, 0, 2048)
        Vs = v3(E[4], G, 0, 2048)
        Sc = v3(E[4], G, 2048, 4096)
        Y = E[2][0:NC, :].rearrange("c (j n) -> c j n", j=LC)
        uT = xT[:, 4:8, :]
        yT = v3(E[4], 4, 0, 2048)
        sg = v3(E[3], 4, 0, 2048)
        QKT = v3(E[0], 8)
        VML = E5[:, 0:16 * 129].rearrange("p (t h d) -> p t h d", t=4, h=4)
        SO = v3(E5, 4, 2112, 2112 + 2048)
        Dq = v3(E[1], 4, 0, 2048)
        Dk = v3(E[1], 4, 2048, 4096)
        qdT = v3(E[2], 4, 0, 2048)
        kdT = v3(E[2], 4, 2048, 4096)
        Dv = v3(E[3], 4, 0, 2048)
        hh = v3(E[1], 4, 0, 2048)
        hsq = v3(E[1], 4, 2048, 4096)

        WOFF = [0, 512, 896, 1152]

        def wts(hh_, s):
            o = (hh_ % 2) * 1280 + WOFF[s]
            return E[4][:, o:o + T - P * s]

        def dts(n):
            return E[4][:, 2560 + 512 * (n % 2):3072 + 512 * (n % 2)]

        sdiag = E[4][:, 3584:4096]
        POFF = [0, 128, 384, 768]

        def pm(hh_, t):
            o = (hh_ % 2) * 1280 + POFF[t]
            return E[0][:, o:o + P * (t + 1)]

        TOFF = [0, 512, 1024, 896]

        def ptm(hh_, k):
            o = (hh_ % 2) * 1280 + TOFF[k]
            return E[4][:, o:o + T - P * k]

        def row(name):
            return rows[vec[name][0]:vec[name][0] + vec[name][1], :]

        rows_loads = [(row("mem_norm_g"), A["mem_norm_g"].rearrange("(r c) -> r c", c=P))]
        for name in ("norm_mix_g", "norm_xa_g", "norm_ffn_g", "xa_qn_g", "xa_kn_g"):
            rows_loads.append((row(name), A[name].rearrange("l (r c) -> (l r) c", c=P)))
        rows_loads += [(row("ml_conv_w"), A["ml_conv_w"][0].rearrange("w (r c) -> (w r) c", c=P)),
                  (row("ml_conv_b"), A["ml_conv_b"][0].rearrange("(r c) -> r c", c=P)),
                  (row("s5_b_glu"), A["s5_b_glu"][0].rearrange("(r c) -> r c", c=P))]
        small = []
        for l in range(2):
            small += [(rw[:, l, :, 0:4], A["moe_w_grp"][l].rearrange("(k p) n -> p k n", p=P)),
                      (rw[:, l, :, 4:20], A["moe_w_exp"][l].rearrange("(k p) n -> p k n", p=P)),
                      (rbias[:, l, 0:4], A["moe_b_grp"][l].partition_broadcast(P)),
                      (rbias[:, l, 4:20], A["moe_b_exp"][l].partition_broadcast(P))]
        small += [(ifw[:, :, :], w_od[:, :, 4 * MIX:4 * MIX + 8]),
                  (ifb[:, :], A["ml_b_if"][0].partition_broadcast(P)),
                  (gbs[:, :], A["gm_bs"][0].rearrange("h t -> t h"))]
        lamr, lami, lstep = sm[:, 0:32], sm[:, 32:64], sm[:, 64:96]
        dT = sm[0:GI, 96:128]
        Cst1, Cst2 = v3(E[4], 4, 0, 512), v3(E[4], 4, 512, 1024)
        B1, B2, BB1, BB2, C1, C2 = [v3(E[4], G, 1024 + 512 * n, 1536 + 512 * n) for n in range(6)]
        lam_rows, lam_loads = junk[:, P:2 * P], []
        for lo in (0, NS):
            lam_loads += [(lam_rows[0:G, lo:lo + NS], A["s5_lam_re"][0]), (lam_rows[G:2 * G, lo:lo + NS], A["s5_lam_im"][0])]
        lam_loads.append((lam_rows[2 * G:3 * G, 0:GI], A["s5_d"][0].rearrange("(g i) -> g i", i=GI)))
        s5_loads = [(lstep, A["s5_log_step"][0].partition_broadcast(P))]
        for lo, b1, b2, c1, c2 in ((0, "s5_b_re", "s5_b_im", "s5_c_re", "s5_c_im"),
                                   (NS, "s5_b_im", "s5_b_re", "s5_c_im", "s5_c_re")):
            s5_loads += [(B1[lo:lo + NS], A[b1][0].rearrange("g p i -> p g i")),
                         (Cst1[:, :, lo:lo + NS], A[c1][0].rearrange("(a g) i p -> (g i) a p", a=4)),
                         (Cst2[:, :, lo:lo + NS], A[c2][0].rearrange("(a g) i p -> (g i) a p", a=4))]
        xTf = xT[:, :, :].rearrange("p a b -> p (a b)")
        memtok = v3(xTf, 2, 2048, 4096)
        memnT = v3(xTf, 8, 0, 2048)
        headsel = wsT[0:4, :].rearrange("p (h m) -> p h m", h=4)
        xg = [E[1][:, 1024 * n:1024 * n + 1024] for n in range(2)]
        xgT = [v3(E[1], KT, 2048 + 1024 * n, 3072 + 1024 * n) for n in range(2)]
        yo = [E[2][:, 1024 * n:1024 * n + 1024] for n in range(2)]
        silu = [E[2][:, 2048 + FF * n:2048 + FF * n + FF] for n in range(2)]
        hid = [E[2][:, 2560 + FF * n:2560 + FF * n + FF] for n in range(2)]
        hThi, hTlo = [[E2r[:, lo + FF * n:lo + FF * n + FF] for n in range(2)] for lo in (3072, 3072 + 2 * FF)]
        w2s = [v3(E[3], 2, 2048 * n, 2048 * n + 2048) for n in range(2)]
        Yg = [v3(E[3 + n], TT) for n in range(2)]
        qtok = v3(E[1], TT)
        qT = v3(E[2], KT)
        prob = E[3][:, :].rearrange("p (t h m) -> p t h m", t=TT, h=4)
        pT = E[4][:, :].rearrange("p (h k q) -> p h k q", h=4, k=2)
        xlo = {"ev": v3(E3r, KT), "q": v3(E4r, KT), "o": v3(E1r, KT), "od": v3(E2r, KT), "out1": v3(E5r, KT, 0, KT * T)}
        xhi, ohi = v3(xTr, KT), v3(E0r, KT)

        def by_k(buf):
            return [buf[:, k, :] for k in range(KT)]

        out0_hi = [v3(E1r, KT)[:, 4 + k, :] for k in range(4)] + [v3(E0r, KT)[:, k, :] for k in range(4)]
        gated = v3(E[2], KT)
        xmx, xnm, xsum, xrec = st[:, 0:16], st[:, 16:32], st[:, 32:48], st[:, 48:64]
        wsN = v3(wsT, 4)
        Frow, lrow, erow, Brow = [E[3][0:4, 512 * n:512 * n + 512] for n in range(4)]
        Irow, arow, enrow = E[3][0:4, 2816:3328], E5[0:4, 2112:2624], E5[0:4, 2624:3136]
        Mrow = E[3][0:4, 3328:3840]
        nMrow = Irow
        ifg = st[:, 64:96].rearrange("p (t n) -> p t n", t=4)
        mlc = st[:, 96:128]
        g2 = st[:, 128:132]
        hngain = sm[:, 0:512]
        lngain = slot("glu")[:, KT - 1, :]
        ropec, ropes = v3(E[3], 4, 2048, 2304), v3(E[3], 4, 2304, 2560)
        rope_loads = [(ropec, rope_c), (ropes, rope_s), (E[3][:, 2560:2688], A["mb_qn_g"][0].partition_broadcast(P)),
                      (E[3][:, 2688:2816], A["mb_kn_g"][0].partition_broadcast(P))]
        dsq, dstd, drec = st[:, 132:164], st[:, 164:196], st[:, 196:228]
        step_, are, th, turn, t8, rho8, Fr, Fi, nr, n1, n2 = [sm[:, 128 + 32 * n:160 + 32 * n] for n in range(11)]
        mag, Lr, Li, Lt = [v3(E[1], G, 288 * n, 288 * n + 288) for n in range(4)]
        def t4(lo, k):
            return sm[:, lo:lo + 4 * k].rearrange("p (t k) -> p t k", t=4)

        lg, gsub, gexp, gmax, gs, gp, geq, gf = (t4(0, 20), t4(80, 4), t4(96, 4), sm[:, 112:116], sm[:, 116:120],
                                                 sm[:, 120:124], t4(124, 4), t4(140, 4))
        sel16, sel, m1, m2, f1, f2 = t4(160, 16), t4(224, 4), sm[:, 240:244], sm[:, 244:248], t4(248, 4), t4(264, 4)
        sel2, dsub, dexp, tmp4, RB = t4(280, 4), sm[:, 296:300], sm[:, 300:304], t4(304, 4), t4(448, 16)
        M12 = [t4(320, 16), t4(384, 16)]
        posf, rev4 = sm[:, 576:584], sm[:, 584:588]
        def c3(ap):
            return ap.rearrange("p (e j) -> p e j", e=NE)

        E4 = E[4]
        rank, full, more, cum, zero, base, xbase, slotf, itemf = [
            E4[:, lo:lo + n] for lo, n in ((0, 5 * NE), (80, NX), (96, NE * NX), (144, NE * NX), (192, NE * NX),
                                           (240, NE), (256, NE), (272, 8), (280, 8))]
        slot1h, item1h = v3(E4r, 8, 512, 512 + 8 * P), v3(E4r, 8, 1536, 1536 + 8 * NI)
        epx, nth, tabf, half_, big1, big2 = [
            E4[0:1, lo:lo + n] for lo, n in ((1792, NE * NX), (1840, 8), (1856, 64), (1920, 4), (2048, 8 * NE * NX),
                                             (2048 + 8 * NE * NX, 8 * NE * NX))]
        dgain = [E[3][:, 2560:2688], E[3][:, 2688:2816]]

        NORMS = {"mem": 0, "mix_norm0": 1, "xa_norm0": 2, "ffn_norm0": 3, "mix_norm1": 4, "xa_norm1": 5, "ffn_norm1": 6}
        @block.sync
        def _(sp):
            def load_panel(p, slot_is_free=False):
                src, _ = panels[p]
                if p >= 2 and not slot_is_free:
                    await_filled(sp, panels[p - 2][1])
                sp.dma_start(W[p % 2][:, 0:src.shape[1], :], src).then_inc(landed[p % 2], 16)

            def experts(l):
                m = M[l]
                for p in range(first_of_layer1 if l == 0 else len(panels))[-2:]:
                    await_filled(sp, panels[p][1])
                await_filled(sp, first[f"pT{l}"] + 7)

                def load_up(e, par):
                    for n, w in enumerate((w1, w3)):
                        sp.dma_start(W[par][:, :, n * FF:(n + 1) * FF], w[e]).then_inc(m["w13a" if par == 0 else "w13b"], 16)

                def load_down(e, par):
                    sp.dma_start(w2s[par], w2[e])\
                      .then_inc(m["w2a" if par == 0 else "w2b"], 16)

                def store(q, par):
                    for half in range(2):
                        sp.wait_ge(m[f"y_ready{half}"], q * 2 + (par + 1))
                    sp.dma_start(ybuf[l][bass.ds(q * (2 * P) + par * P, P), :], yo[par]).then_inc(m[f"y_stored{par}"], 16)

                sp.wait_ge(S["spare_rows"], 16 * 2 * (NI - NE) * P // NM)
                for par in range(2):
                    load_up(NE * l + par, par)
                    load_down(NE * l + par, par)
                sp.wait_ge(m["table_ready"], 1)
                last_pair = sp.value_load(tab[0:1, 60:61], min_val=NE // 2 - 1, max_val=NI // 2 - 1)
                with sp.Fori(1, last_pair + 1) as q:
                    for par in range(2):
                        e = sp.value_load(tab[0:1, bass.ds(q * 2 + par, 1)], min_val=0, max_val=NE - 1)
                        sp.wait_ge(m["hid_filled"], q * 2 + (par - 1))
                        load_up(e + NE * l, par)
                        sp.wait_ge(m["y_filled1"], q * 2 + (par - 1))
                        load_down(e + NE * l, par)
                        store(q - 1, par)
                for par in range(2):
                    store(last_pair, par)

            sp.dma_start(memtok, A["mem"][0].rearrange("(a p) d -> p a d", p=P)).then_inc(S["mem_in"], 16)
            for dst, src in s5_loads:
                sp.dma_start(dst, src, allow_slow_non_contiguous=True).then_inc(S["s5_in"], 16)
            load_panel(0)
            load_panel(1)
            for k in range(TT):
                sp.dma_start(h[:, k, :], A["x"][0, k * P:(k + 1) * P, :]).then_inc(S["x_in"], 16)
            sp.wait_ge(S["s5_in"], 16 * len(s5_loads))
            for lo in (0, NS):
                sp.dma_start(B2[lo:lo + NS], B1[NS - lo:2 * NS - lo]).then_inc(S["s5_b2"], 16)
            for dst, src in small:
                sp.dma_start(dst, src, allow_slow_non_contiguous=True).then_inc(S["small_in"], 16)
            sp.dma_start(wsN, A["gm_ws"][0].rearrange("h t s -> t h s")).then_inc(S["wide_in"], 16)
            for p in range(2, first_of_layer1):
                load_panel(p)
                if p == pnum["glu"]:
                    sp.dma_start(lngain, A["gm_ln_g"][0].partition_broadcast(P)).then_inc(S["lngain_in"], 16)
            experts(0)
            sp.wait_ge(M[0]["y_gathered2"], 32)
            for p in range(first_of_layer1, len(panels)):
                load_panel(p, slot_is_free=p < first_of_layer1 + 2)
            experts(1)
            for t in range(TT):
                sp.wait_ge(M[1]["h_combined"], t + 1)
                sp.dma_start(out[0, t * P:(t + 1) * P, :], h[:, t, :]).then_inc(S["out_stored"], 16)
            sp.wait_ge(S["out_stored"], 16 * TT)

        @block.gpsimd
        def _(pool):
            p_ = Chain(pool, "p_step")

            def select(t, base, pattern, mult, op, fill):
                p_(pool.affine_select(out=t, in_=t, compare_op=op, fill=fill, base=base, pattern=pattern,
                                      channel_multiplier=mult))

            for dst, src in lam_loads:
                pool.dma_start(dst, src).then_inc(S["lam_in"], 16)
            for t, value in ((ident, 0.0), (perm, 0.0), (after, 0.0), (before, 0.0), (strict, 1.0), (ones, 1.0),
                             (halfpi, TWO_PI / 4), (sgn, 1.0), (nsgn, -1.0)):
                p_(pool.memset(t[:], value))
            select(ident[:], 0, [[-1, P]], 1, ALU.not_equal, 1.0)
            select(perm[:], -NS, [[-1, P]], 1, ALU.not_equal, 1.0)
            select(perm[:], NS, [[-1, P]], 1, ALU.not_equal, -1.0)
            select(after[:], 0, [[1, P]], -1, ALU.is_ge, -BIG)
            select(before[:], 0, [[-1, P]], 1, ALU.is_ge, -BIG)
            select(strict[:], 0, [[1, P]], -1, ALU.is_gt, 0.0)
            select(sgn[:], NS - 1, [[0, 1]], -1, ALU.is_ge, -1.0)
            select(nsgn[:], NS - 1, [[0, 1]], -1, ALU.is_ge, 1.0)
            p_(pool.tensor_copy(strict16[:], strict[:]))
            p_(pool.tensor_copy(ones16[:], ones[:]))
            p_(pool.iota(iot[:], pattern=[[1, P]], base=0, channel_multiplier=0))
            p_(pool.iota(toki[:], pattern=[[0, 2], [P, TT]], base=0, channel_multiplier=1))
            p_(pool.tensor_copy(tokf[:], toki[:]))
            p_(pool.tensor_copy(iof[:], iot[:]))
            pool.sem_inc(S["consts_ready"], 1)
            pool.memset(E[0][:], 0.0).then_inc(S["zeros_ready"], 1)

            def low_parts(*names, k0=0, k1=KT):
                for name in names:
                    for k in range(k0, k1):
                        s_ = step(name, k)
                        pool.wait_ge(S["w_hi"], s_ + 1)
                        pool.tensor_tensor(wlo[s_ % RING][:, :], slot(name)[:, k, :], whi[s_ % RING][:, :].bitcast(F32),
                                           ALU.subtract).then_inc(S["w_lo"], 1)

            low_parts("ev0", "ev1", "ev2")

            taken(pool, first["ws"])
            wsv = v3(wsT, 4)
            p_(pool.affine_select(out=wsv, in_=wsv, compare_op=ALU.is_ge, fill=0.0, base=0, pattern=[[0, 4], [1, P]],
                                  channel_multiplier=-1), "ws_masked")
            await_filled(pool, first["mixed"] + 3)
            p_(pool.memset(headsel, 0.0))
            p_(pool.affine_select(out=headsel, in_=headsel, compare_op=ALU.not_equal, fill=1.0, base=0,
                                  pattern=[[-1, 4], [0, P]], channel_multiplier=1), "ws_masked")

            def experts(l):
                m = M[l]

                def wait_alone(semaphore, value):
                    pool.wait_ge(semaphore, value)
                    pool.sem_inc(m["pool_waited"], 1)

                def gather(q, par):
                    if not isinstance(q, int):
                        wait_alone(m["xt_filled"], q * 4 + (2 * par - 2))
                    pool.tensor_copy(idx[:, par:par + 1], slots[:, bass.ds(q * 2 + par, 1)]).then_inc(m["idx_ready"], 1)
                    wait_alone(m["idx_ready"], q * 2 + (par + 1))
                    pool.indirect_dma_start(xg[par], None, xs[l],
                                            bass.IndirectOffsetOnAxis(ap=idx[:, par:par + 1], axis=0))\
                        .then_inc(m[f"xg_in{par}"], 16)

                pool.wait_ge(S["rstd_ready"], 2 * l + 2)
                for t in range(TT):
                    p_(pool.tensor_scalar(xn[:, t, :], h[:, t, :], rstd[:, NORMS[f"ffn_norm{l}"], t:t + 1], None, ALU.mult))
                    pool.dma_start(xs[l][t * P:(t + 1) * P, :], xn[:, t, :]).then_inc(m["xs_stored"], 16)
                pool.wait_ge(m["slots_ready"], 1)
                pool.wait_ge(m["xs_stored"], 16 * TT)
                gather(0, 0)
                gather(0, 1)
                pool.wait_ge(m["table_ready"], 1)
                last_pair = pool.value_load(tab[0:1, 60:61], min_val=NE // 2 - 1, max_val=NI // 2 - 1)
                with pool.Fori(1, last_pair + 1) as q:
                    gather(q, 0)
                    gather(q, 1)
                pool.wait_ge(m["pos_ready"], 1)
                for par in range(2):
                    wait_alone(m[f"y_stored{par}"], last_pair * 16 + 16)
                for t in range(TT):
                    for j in range(2):
                        pool.indirect_dma_start(Yg[j][:, t, :], None, ybuf[l],
                                                bass.IndirectOffsetOnAxis(ap=pos[:, j, t:t + 1], axis=0))\
                            .then_inc(m[f"y_gathered{t}"], 16)
            low_parts("out00", "out01")
            taken_all(pool, "kv1", 6)
            for l in range(2):
                for n in range(NE * P // NM, NI * P // NM):
                    pool.dma_start(ybuf[l][n * NM:(n + 1) * NM, :].rearrange("(k p) d -> p k d", p=P), memV[:, :, :])\
                        .then_inc(S["spare_rows"], 16)
            low_parts("wq00", "wq01", "wo00", "wo01")
            experts(0)
            low_parts(*[f"od{n}" for n in range(7)])
            taken_all(pool, "og", 4)
            pool.wait_ge(S["wide_in"], 32)
            p_(pool.tensor_tensor(SO, SO, hngain.unsqueeze(1).broadcast_to([P, TT, MIX]), ALU.mult))
            low_parts("out10", k1=RING)
            taken_all(pool, "num0", 4)
            taken_all(pool, "num1", 4)
            p_(pool.tensor_tensor(hsq, hh, hh, ALU.mult), "hh_sq")
            pool.wait_ge(S["hh_rstd"], 1)
            h16 = E[1][:, 0:2048].rearrange("p (n d) -> p n d", n=16)
            p_(pool.tensor_tensor(h16, h16, drec[:, 0:16].unsqueeze(2).broadcast_to([P, 16, P]), ALU.mult))
            p_(pool.tensor_tensor(hh, hh, SO, ALU.mult), "hh_ready")
            low_parts("out10", k0=RING)
            low_parts("out11")
            low_parts("wq10", "wq11", "wo10", "wo11")
            experts(1)

        LAST_ADD = {"xa_norm0": "out0", "ffn_norm0": "wo0", "xa_norm1": "out1", "ffn_norm1": "wo1"}

        @block.tensor
        def _(pe):
            def transpose_gain_norm(name):
                u0 = first[name]
                src = {"mix_norm0": xnE, "mix_norm1": xn}.get(name, h)
                for k in range(KT):
                    claim(pe, u0 + k)
                    for t in range(TT):
                        if name in LAST_ADD:
                            if k % 4 == 0:
                                taken(pe, first[LAST_ADD[name]] + k + t)
                        elif k == 0:
                            pe.wait_ge(S["xn_ready"], MT + TT * (name == "mix_norm1") + t + 1)
                        ins = pe.transpose(bank(u0 + k)[:, t * P:(t + 1) * P], src[:, t, k * P:(k + 1) * P], ident[:])
                    fill(ins, u0 + k)

            def split_gemm(u, panel_name, hi, lo, x_ready=None, weights_first=False):
                for t in range(TT):
                    claim(pe, u + t)
                for k in range(KT):
                    s_ = step(panel_name, k)
                    if x_ready:
                        x_ready(k)
                    pe.wait_ge(S["w_lo"], s_ + 1)
                    wh, wl = whi[s_ % RING], wlo[s_ % RING]
                    xh, xl = hi[k], lo[k]
                    for t in range(TT):
                        c = slice(t * P, (t + 1) * P)
                        if weights_first:
                            passes = ((wh[:, c], xh), (wh[:, c], xl), (wl[:, c], xh))
                        else:
                            passes = ((xh[:, c], wh[:, :]), (xh[:, c], wl[:, :]), (xl[:, c], wh[:, :]))
                        for n, (a, b) in enumerate(passes):
                            ins = pe.matmul(bank(u + t)[:, :], a, b, start=(k == 0 and n == 0),
                                            stop=(k == KT - 1 and n == 2))
                        if k == KT - 1:
                            fill(ins, u + t)
                    if k < KT - 1:
                        ins.then_inc(S["w_used"], 1)

            pe.wait_ge(S["consts_ready"], 1)
            u = first["cols"]
            pe.wait_ge(S["rows_in"], 16 * len(rows_loads))
            pe.wait_ge(S["lam_in"], 16 * len(lam_loads))
            pe.transpose(bank(u)[:, 0:NROWS], rows[0:NROWS, :], ident[0:NROWS, 0:NROWS])
            pe.transpose(bank(u)[:, P:P + 2 * G], lam_rows[0:2 * G, :], ident[0:2 * G, 0:2 * G])
            fill(pe.transpose(bank(u)[0:GI, 2 * P:2 * P + G], lam_rows[2 * G:3 * G, 0:GI],
                              ident[2 * G:3 * G, 2 * G:3 * G]), u)
            u = first["memT"]
            for t in range(MT):
                pe.wait_ge(S["xn_ready"], t + 1)
            for k in range(0, KT, 2):
                for kk in range(2):
                    for t in range(MT):
                        ins = pe.transpose(bank(u)[:, kk * NM + t * P:kk * NM + (t + 1) * P],
                                           memtok[:, t, (k + kk) * P:(k + kk + 1) * P], ident[:])
                fill(ins, u)
                u += 1
            taken_all(pe, "memT", 4)
            def memory_gemm(name, ns):
                u = first[name]
                for n in ns:
                    panel_in(pe, f"kv{n}")
                    for t in range(MT):
                        claim(pe, u)
                        for k in range(KT):
                            ins = pe.matmul(bank(u)[:, :], memnT[:, k, t * P:(t + 1) * P], slot(f"kv{n}")[:, k, :],
                                            start=(k == 0), stop=(k == KT - 1))
                        fill(ins, u)
                        u += 1

            memory_gemm("kv0", (0,))
            pe.wait_ge(S["s5_in"], 16 * len(s5_loads))
            for n, c in enumerate((Cst1, Cst2)):
                u = first["ct"] + n
                claim(pe, u)
                for a in range(4):
                    ins = pe.transpose(bank(u)[:, a * P:(a + 1) * P], c[:, a, :], ident[:])
                fill(ins, u)
            memory_gemm("kv1", (1, 2, 3))
            pe.wait_ge(S["s5_bb"], 1)
            for n in range(8):
                u = first["bT"] + n
                claim(pe, u)
                for g in range(4 * n, 4 * n + 4):
                    ins = pe.transpose(bank(u)[:, (g % 4) * P:(g % 4 + 1) * P],
                                       s5Qn[:, g].rearrange("p j i -> p (j i)"), ident[:])
                fill(ins, u)
            pe.wait_ge(S["s5_pp"], 1)
            for n in range(8):
                u = first["w"] + n
                claim(pe, u)
                for g in range(4 * n, 4 * n + 4):
                    ins = pe.matmul(bank(u)[0:GI, (g % 4) * P:(g % 4 + 1) * P], BB1[:, g, :], s5PP[:, g, 0:LC, :]
                                    .rearrange("p k i -> p (k i)"), start=(g % 4 == 0), stop=(g % 4 == 3),
                                    skip_group_check=True)
                fill(ins, u)
            u = first["memKT"]
            pe.wait_ge(S["memk_norm"], 1)
            for k in range(0, KT, 2):
                claim(pe, u)
                for kk in range(2):
                    for t in range(MT):
                        ins = pe.transpose(bank(u)[:, kk * NM + t * P:kk * NM + (t + 1) * P],
                                           memtok[:, t, (k + kk) * P:(k + kk + 1) * P], ident[:])
                fill(ins, u)
                u += 1

            transpose_gain_norm("mix_norm0")
            for n in range(2):
                split_gemm(first["uv"] + 4 * n, f"ev{n}", by_k(xhi), by_k(xlo["ev"]), lambda k: taken(pe, first["mix_norm0"] + k))
            split_gemm(first["s5u"], "ev2", by_k(xhi), by_k(xlo["ev"]), weights_first=True)
            u = first["ws"]
            claim(pe, u)
            pe.wait_ge(S["wide_in"], 16)
            for n in range(H):
                ins = pe.transpose(bank(u)[:, n * P:(n + 1) * P], wsN[:, n, :], ident[:])
            fill(ins, u)
            pe.wait_ge(S["ws_masked"], 1)
            pe.wait_ge(S["vh_ready"], 1)
            for n in range(H):
                u = first["mixed"] + n
                claim(pe, u)
                fill(pe.matmul(bank(u)[:, :], wsT[:, n * P:(n + 1) * P], Gv[:, :, n * P:(n + 1) * P], start=True,
                               stop=True), u)
            taken_all(pe, "mixed", 4)
            for n in range(4):
                u = first["yaT"] + n
                claim(pe, u)
                for t in range(TT):
                    ins = pe.transpose(bank(u)[:, t * P:(t + 1) * P], Gu[:, t, n * P:(n + 1) * P], ident[:])
                fill(ins, u)
            taken_all(pe, "s5u", 4)
            for j in range(LC):
                u = first["uj"] + j
                claim(pe, u)
                for n in range(4):
                    ins = pe.transpose(bank(u)[0:NC, n * P:(n + 1) * P],
                                       uT[:, n, :].rearrange("p (c j) -> p j c", j=LC)[:, j, :], ident[:])
                fill(ins, u)
            taken_all(pe, "uj", 8)
            for n in range(4):
                u = first["ucT"] + n
                claim(pe, u)
                for g in range(8):
                    ins = pe.transpose(bank(u)[:, g * NC:(g + 1) * NC], U[:, 8 * n + g].rearrange("c j i -> c (j i)"),
                                       ident[0:NC, 0:NC])
                fill(ins, u)
            taken_all(pe, "ucT", 4)
            taken_all(pe, "bT", 8)
            for n in range(4):
                u = first["V"] + n
                claim(pe, u)
                for g in range(8):
                    ins = pe.matmul(bank(u)[:, g * NC:(g + 1) * NC], s5Q[:, 8 * n + g, :], Uc[:, 8 * n + g, :],
                                    start=(g == 0), stop=(g == 7), skip_group_check=True)
                fill(ins, u)
            for n in range(4):
                u = first["Vsw"] + n
                claim(pe, u)
                taken(pe, first["V"] + n)
                fill(pe.matmul(bank(u)[:, :], perm[:], Vc[:, 8 * n:8 * n + 8, :].rearrange("p g c -> p (g c)"),
                               start=True, stop=True), u)
            pe.wait_ge(S["s5_scan"], 1)
            for n in range(4):
                u = first["Xp"] + n
                claim(pe, u)
                fill(pe.matmul(bank(u)[:, :], perm[:], Vs[:, 8 * n:8 * n + 8, :].rearrange("p g c -> p (g c)"),
                               start=True, stop=True), u)
            pe.wait_ge(S["s5_x"], 1)
            pe.wait_ge(S["s5_t"], 16 * LC)
            for n in range(8):
                u = first["y"] + n
                claim(pe, u)
                for g in range(4 * n, 4 * n + 4):
                    o = bank(u)[0:NC, (g % 4) * P:(g % 4 + 1) * P]
                    pe.matmul(o, Uc[:, g, :], s5T[:, g, :], start=(g % 4 == 0), stop=False, skip_group_check=True)
                    ins = pe.matmul(o, Sc[:, g, :], s5PP[:, g, 1:LC + 1, :].rearrange("p k i -> p (k i)"),
                                    start=False, stop=(g % 4 == 3), skip_group_check=True)
                fill(ins, u)
            taken_all(pe, "y", 8)
            for n in range(4):
                u = first["yT"] + n
                claim(pe, u)
                for j in range(LC):
                    ins = pe.transpose(bank(u)[:, j * NC:(j + 1) * NC], Y[:, j, n * P:(n + 1) * P],
                                       ident[0:NC, 0:NC])
                fill(ins, u)
            taken_all(pe, "yT", 4)
            panel_in(pe, "glu")
            for n in range(4):
                u = first["glu"] + n
                claim(pe, u)
                for k in range(4):
                    ins = pe.matmul(bank(u)[:, :], slot("glu")[:, k, n * P:(n + 1) * P], yT[:, k, :], start=(k == 0),
                                    stop=(k == 3))
                fill(ins, u)
            for n in range(2):
                split_gemm(first["out0"] + 4 * n, f"out0{n}", out0_hi, by_k(xhi), lambda k: pe.wait_ge(S["ya_lo"], k + 1))
            def attention(l):
                transpose_gain_norm(f"xa_norm{l}")
                for n in range(2):
                    split_gemm(first[f"q{l}"] + 4 * n, f"wq{l}{n}", by_k(xhi), by_k(xlo["q"]), lambda k: taken(pe, first[f"xa_norm{l}"] + k))
                for k in range(KT):
                    u = first[f"qT{l}"] + k
                    claim(pe, u)
                    for t in range(TT):
                        if k % 4 == 0:
                            taken(pe, first[f"q{l}"] + k + t)
                        ins = pe.transpose(bank(u)[:, t * P:(t + 1) * P], qtok[:, t, k * P:(k + 1) * P], ident[:])
                    fill(ins, u)
                taken_all(pe, f"qT{l}", 8)
                for t in range(TT):
                    for hp in range(2):
                        u = first[f"sc{l}"] + 2 * t + hp
                        claim(pe, u)
                        for n in range(2):
                            for kk in range(2):
                                k = 2 * (2 * hp + n) + kk
                                ins = pe.matmul(bank(u)[:, n * NM:(n + 1) * NM], qT[:, k, t * P:(t + 1) * P],
                                                memKT[:, k, :], start=(kk == 0), stop=(kk == 1))
                        fill(ins, u)
                for n in range(8):
                    claim(pe, first[f"pT{l}"] + n)
                for t in range(TT):
                    pe.wait_ge(S["probs"], 8 * l + 2 * (t + 1))
                    for n in range(4):
                        for k in range(2):
                            u = first[f"pT{l}"] + 2 * n + k
                            ins = pe.transpose(bank(u)[:, t * P:(t + 1) * P], prob[:, t, n, k * P:(k + 1) * P], ident[:])
                            if t == TT - 1:
                                fill(ins, u)
                for n in range(4):
                    for d in range(2):
                        u = first[f"o{l}"] + 2 * n + d
                        claim(pe, u)
                        for k in range(2):
                            taken(pe, first[f"pT{l}"] + 2 * n + k)
                            ins = pe.matmul(bank(u)[:, :], memV[:, k, n * XD + d * P:n * XD + (d + 1) * P],
                                            pT[:, n, k, :], start=(k == 0), stop=(k == 1))
                        fill(ins, u)
                for n in range(2):
                    split_gemm(first[f"wo{l}"] + 4 * n, f"wo{l}{n}", by_k(ohi), by_k(xlo["o"]), lambda k: taken(pe, first[f"o{l}"] + k))

            def experts(l):
                m = M[l]
                transpose_gain_norm(f"ffn_norm{l}")
                taken_all(pe, f"ffn_norm{l}", 8)
                u = first[f"route{l}"]
                claim(pe, u)
                pe.wait_ge(S["small_in"], 16 * len(small))
                for t in range(TT):
                    for k in range(KT):
                        ins = pe.matmul(bank(u)[:, 20 * t:20 * t + 20], xT[:, k, t * P:(t + 1) * P], rw[:, l, k, :],
                                        start=(k == 0), stop=(k == KT - 1), skip_group_check=True)
                fill(ins, u)
                u = first[f"rank{l}"]
                claim(pe, u)
                pe.wait_ge(m["msum_ready"], 1)
                for t in range(TT + 1):
                    for s_ in range(min(t + 1, TT)):
                        ins = pe.matmul(bank(u)[:, NE * t:NE * (t + 1)], strict16[:] if s_ == t else ones16[:],
                                        msum[:, s_, :], start=(s_ == 0), stop=(s_ == min(t, TT - 1)),
                                        skip_group_check=True)
                fill(ins, u)
                u = first[f"idx{l}"]
                claim(pe, u)
                pe.wait_ge(m["onehots_ready"], 1)
                for n in range(2 * TT):
                    ins = pe.matmul(bank(u)[:, 0:NI], slot1h[:, n, :], item1h[:, n, :], start=(n == 0),
                                    stop=(n == 2 * TT - 1))
                fill(ins, u)
                for v in range(u - 7, u + 1):
                    taken(pe, v)

                def later(semaphore, value):
                    if not isinstance(value, int) or value > 0:
                        pe.wait_ge(semaphore, value)

                def turn(q, par):
                    pe.wait_ge(m[f"xg_in{par}"], q * 16 + 16)
                    later(m["xt_ready"], q * 4 + 2 * par)
                    for b in range(2):
                        for k in range(4):
                            ins = pe.transpose(banks[b][:, k * P:(k + 1) * P],
                                               xg[par][:, (4 * b + k) * P:(4 * b + k + 1) * P], ident[:])
                        ins.then_inc(m["xt_filled"], 1)

                def up(q, par):
                    pe.wait_ge(m["xt_ready"], q * 4 + (2 * par + 2))
                    pe.wait_ge(m["w13a" if par == 0 else "w13b"], q * 32 + 32)
                    later(m["hid_ready"], q * 2 + (par - 1))
                    for k in range(KT):
                        ins = pe.matmul(banks[2 + par][:, :], xgT[par][:, k, :], W[par][:, k, :], start=(k == 0),
                                        stop=(k == KT - 1))
                    ins.then_inc(m["hid_filled"], 1)

                def turn_hidden(q, par):
                    pe.wait_ge(m["hid_ready"], q * 2 + (par + 1))
                    later(m["ht_ready"], q * 2 + par)
                    for k in range(2):
                        ins = pe.transpose(banks[4][:, k * P:(k + 1) * P], hid[par][:, k * P:(k + 1) * P], ident[:])
                    ins.then_inc(m["ht_filled"], 1)

                def down(q, par):
                    pe.wait_ge(m["ht_ready"], q * 2 + (par + 1))
                    pe.wait_ge(m["w2_lo"], q * 8 + (4 * par + 4))
                    for half in range(2):
                        later(m[f"y_ready{half}"], q * 2 + par)
                        for k in range(2):
                            xh, xl = hThi[par][:, k * P:(k + 1) * P], hTlo[par][:, k * P:(k + 1) * P]
                            wh, wl = whi[2 * half + k], wlo[2 * half + k]
                            for n, (a, b) in enumerate(((xh, wh), (xh, wl), (xl, wh))):
                                ins = pe.matmul(banks[5 + half][:, :], a, b[:, :], start=(k == 0 and n == 0),
                                                stop=(k == 1 and n == 2))
                        ins.then_inc(m[f"y_filled{half}"], 1)

                def pair(q):
                    up(q, 1)
                    turn_hidden(q, 0)
                    turn(q + 1, 0)
                    down(q, 0)
                    up(q + 1, 0)
                    turn_hidden(q, 1)
                    turn(q + 1, 1)
                    down(q, 1)

                turn(0, 0)
                up(0, 0)
                turn(0, 1)
                pe.wait_ge(m["table_ready"], 1)
                last_pair = pe.value_load(tab[0:1, 60:61], min_val=NE // 2 - 1, max_val=NI // 2 - 1)
                pair(0)
                with pe.Fori(1, last_pair) as q:
                    pair(q)
                up(last_pair, 1)
                turn_hidden(last_pair, 0)
                down(last_pair, 0)
                turn_hidden(last_pair, 1)
                down(last_pair, 1)

            attention(0)
            experts(0)
            transpose_gain_norm("mix_norm1")
            split_gemm(first["dq"], "od0", by_k(xhi), by_k(xlo["od"]), lambda k: taken(pe, first["mix_norm1"] + k))
            u = first["if"]
            claim(pe, u)
            for t in range(TT):
                for n, x_ in enumerate((xhi, xlo["od"])):
                    for k in range(KT):
                        ins = pe.matmul(bank(u)[:, 8 * t:8 * t + 8], x_[:, k, t * P:(t + 1) * P].bitcast(F32), ifw[:, k, :],
                                        start=(k == 0 and n == 0), stop=(k == KT - 1 and n == 1), skip_group_check=True)
            fill(ins, u)
            split_gemm(first["dk"], "od1", by_k(xhi), by_k(xlo["od"]))
            taken(pe, first["if"])
            for n in range(2):
                u = first["ifT"] + n
                claim(pe, u)
                for t in range(TT):
                    ins = pe.transpose(bank(u)[0:4, t * P:(t + 1) * P], ifg[:, t, 4 * n:4 * n + 4], ident[:])
                fill(ins, u)
            for n in range(2):
                split_gemm(first["qk"] + 4 * n, f"od{2 + n}", by_k(xhi), by_k(xlo["od"]), weights_first=True)
            u = first["col"]
            claim(pe, u)
            pe.wait_ge(S["ml_rows"], 1)
            for n, r in enumerate((arow, enrow)):
                for t in range(TT):
                    ins = pe.transpose(bank(u)[:, 16 * n + 4 * t:16 * n + 4 * t + 4], r[:, t * P:(t + 1) * P],
                                       ident[0:4, 0:4])
            fill(ins, u)
            split_gemm(first["v"], "od4", by_k(xhi), by_k(xlo["od"]))
            split_gemm(first["og"], "od5", by_k(xhi), by_k(xlo["od"]))
            split_gemm(first["dv"], "od6", by_k(xhi), by_k(xlo["od"]))
            pe.wait_ge(S["d_norm"], 1)
            for n in range(8):
                u = first["dT"] + n
                claim(pe, u)
                src = Dq if n < 4 else Dk
                for t in range(TT):
                    ins = pe.transpose(bank(u)[:, t * P:(t + 1) * P], src[:, t, (n % 4) * P:(n % 4 + 1) * P], ident[:])
                fill(ins, u)
            pe.wait_ge(S["ws_masked"], 2)
            pe.wait_ge(S["qk_ready"], 8)
            taken_all(pe, "v", 4)
            for n in range(H):
                u = first[f"mlh{n}"]
                claim(pe, u)
                fill(pe.matmul(bank(u)[:, :], headsel[:, n, :], nMrow, start=True, stop=True), u)
                for s_ in range(TT):
                    u = first[f"mlh{n}"] + 1 + s_
                    claim(pe, u)
                    fill(pe.matmul(bank(u)[:, 0:T - P * s_], QKT[:, 4 + n, s_ * P:(s_ + 1) * P],
                                   QKT[:, n, s_ * P:T], start=True, stop=True), u)
                if n % 2 == 0:
                    continue
                for t in range(TT):
                    u = first[f"num{n // 2}"] + t
                    claim(pe, u)
                    for n2 in (n - 1, n):
                        for s_ in range(t + 1):
                            taken(pe, first[f"mlh{n2}"] + 1 + s_)
                            ins = pe.matmul(bank(u)[:, 256 * (n2 % 2):256 * (n2 % 2) + 129],
                                            wts(n2, s_)[:, P * (t - s_):P * (t - s_ + 1)], VML[:, s_, n2, :],
                                            start=(s_ == 0), stop=(s_ == t))
                    fill(ins, u)
            taken_all(pe, "dT", 8)

            def moba_scores(n):
                for t in range(TT):
                    u = first[f"ms{n}"] + t
                    claim(pe, u)
                    fill(pe.matmul(bank(u)[:, 0:P * (t + 1)], qdT[:, n, t * P:(t + 1) * P],
                                   kdT[:, n, 0:P * (t + 1)], start=True, stop=True), u)

            def moba_out(n):
                pe.wait_ge(S["mo_probs"], 4 * (n + 1))
                for b, ks in enumerate(((0,), (1, 3), (2,))):
                    u = first[f"mp{n}"] + b
                    claim(pe, u)
                    o = 0
                    for k in ks:
                        for t in range(k, TT):
                            ins = pe.transpose(bank(u)[:, o:o + P], pm(n, t)[:, k * P:(k + 1) * P], ident[:])
                            o += P
                    fill(ins, u)
                u = first[f"mp{n}"] + 3
                claim(pe, u)
                for b in range(3):
                    taken(pe, first[f"mp{n}"] + b)
                for k in range(TT):
                    ins = pe.matmul(bank(u)[:, k * P:T], Dv[:, k, n * P:(n + 1) * P], ptm(n, k), start=(k == 0),
                                    stop=(k == TT - 1), skip_group_check=True)
                fill(ins, u)

            moba_scores(0)
            for n in range(1, H):
                moba_scores(n)
                moba_out(n - 1)
            moba_out(H - 1)
            pe.wait_ge(S["hh_ready"], 1)
            for n in range(4):
                u = first["ycT"] + n
                claim(pe, u)
                for t in range(TT):
                    ins = pe.transpose(bank(u)[:, t * P:(t + 1) * P], hh[:, t, n * P:(n + 1) * P], ident[:])
                fill(ins, u)
            for n in range(2):
                split_gemm(first["out1"] + 4 * n, f"out1{n}", by_k(xhi),
                           by_k(xlo["out1"])[4:] + by_k(xlo["out1"])[:4],
                           lambda k: taken(pe, first["ycT"] + k if k < 4 else first[f"mp{k - 4}"] + 3))
            attention(1)
            experts(1)

        @block.scalar
        def _(act):
            a_ = Chain(act, "a_step")

            def h_is_ready(name, t):
                if name == "mix_norm0":
                    act.wait_ge(S["x_in"], 16 * TT)
                elif name == "mix_norm1":
                    act.wait_ge(M[0]["h_combined"], t + 1)
                else:
                    taken(act, first[LAST_ADD[name]] + 4 + t)

            def high_part(u, dst, scale=1.0):
                await_filled(act, u)
                act.activation(dst, bank(u)[:, :], ACT.Copy, scale=scale).then_inc(S["x_hi"], 1)

            def weights(name, k0, k1):
                p = pnum[name]
                act.wait_ge(landed[p % 2], 16 * (p // 2 + 1))
                for k in range(k0, k1):
                    s_ = step(name, k)
                    await_ring(act, s_)
                    act.activation(whi[s_ % RING][:, :], slot(name)[:, k, :], ACT.Copy).then_inc(S["w_hi"], 1)

            def weights_between(a, b):
                weights(a, RING, KT)
                if b:
                    weights(b, 0, RING)

            def table(func):
                a_(act.activation(spare[:, 0:1], ones[:, 0:1], func))

            def squares(name):
                n = NORMS[name]
                for t in range(TT):
                    h_is_ready(name, t)
                    if name == "mix_norm0":
                        dst = memV[:, t % MT, :]
                        if t >= MT:
                            act.wait_ge(S["stat_ready"], MT + 4 * (n - 1) + t - MT + 1)
                    else:
                        dst = E[1][:, t * D:(t + 1) * D]
                    act.activation(dst, h[:, t, :], ACT.Square, accum_out=ssq[:, n, t:t + 1]).then_inc(S["stat_ready"], 1)

            def root(name):
                n = NORMS[name]
                act.wait_ge(S["mean_ready"], n + 1)
                act.activation(std[:, n, :], ssq[:, n, :], ACT.Sqrt).then_inc(S["std_ready"], 1)

            def norm(name, between=None):
                if name != "mix_norm0" and "xa" not in name:
                    table(ACT.Sqrt)
                    squares(name)
                if between:
                    between()
                if name != "mix_norm0" and "xa" not in name:
                    root(name)
                gain, lo = {"mix": ("norm_mix_g", 0), "xa_": ("norm_xa_g", 0), "ffn": ("norm_ffn_g", 0)}[name[0:3]]
                lo = 8 * int(name[-1])
                if first[name] in two_parts:
                    for k in range(KT):
                        high_part(first[name] + k, xhi[:, k, :], col(gain, lo + k))
                    if "xa" in name:
                        squares(name)
                        root(name)
                    return
                for k in range(0, KT, 2):
                    u = first[name] + k
                    await_filled(act, u)
                    evac(act.activation(xT[:, k, :], bank(u)[:, :], ACT.Copy, scale=col(gain, lo + k)), u)

            def copies(name, n0, n1, dst, step=1):
                for n in range(n0, n1, step):
                    u = first[name] + n
                    await_filled(act, u)
                    evac(act.activation(dst(n), bank(u)[:, :], ACT.Copy), u)

            for dst, src in rows_loads:
                act.dma_start(dst, src).then_inc(S["rows_in"], 16)
            act.wait_ge(S["mem_in"], 16)
            for t in range(MT):
                act.activation(memnT[:, 4 * t:4 * t + 4, :].rearrange("p a b -> p (a b)"), memtok[:, t, :], ACT.Square,
                               accum_out=ssq[:, 0, t:t + 1]).then_inc(S["stat_ready"], 1)
            act.wait_ge(S["mean_ready"], 1)
            act.activation(std[:, 0, 0:MT], ssq[:, 0, 0:MT], ACT.Sqrt).then_inc(S["std_ready"], 1)
            act.wait_ge(S["s5_in"], 16 * len(s5_loads))
            act.activation(step_, lstep, ACT.Exp).then_inc(S["s5_exp"], 1)
            act.wait_ge(S["s5_args"], 1)
            act.activation(mag, mag, ACT.Exp).then_inc(S["s5_exp"], 1)
            act.activation(rho8, are, ACT.Exp, scale=float(LC)).then_inc(S["s5_exp"], 1)
            act.wait_ge(S["s5_args"], 2)
            act.wait_ge(S["consts_ready"], 1)
            act.activation(Li, Li, ACT.Sin, scale=TWO_PI).then_inc(S["s5_sin"], 1)
            act.activation(Lr, Lr, ACT.Sin, bias=halfpi[:, 0:1], scale=-TWO_PI).then_inc(S["s5_sin"], 1)
            act.activation(s5sin, s5sin, ACT.Sin, scale=TWO_PI).then_inc(S["s5_sin"], 1)
            act.activation(s5cos, s5cos, ACT.Sin, bias=halfpi[:, 0:1], scale=-TWO_PI).then_inc(S["s5_sin"], 1)
            squares("mix_norm0")
            root("mix_norm0")
            copies("kv0", 0, 2, lambda n: memtok[:, n, 0:512])
            copies("kv1", 0, 6, lambda n: (memtok if n < 2 else memV)[:, n % 2, ((n // 2 + 1) % 2) * 512:((n // 2 + 1) % 2 + 1) * 512])
            taken(act, first["kv1"] + 1)
            for t in range(MT):
                for n in range(4):
                    a_(act.activation(junk[:, 0:XD], memtok[:, t, n * XD:(n + 1) * XD], ACT.Square,
                                      accum_out=xmx[:, 4 * t + n:4 * t + n + 1]), "hd_sq")
            act.wait_ge(S["hmean_ready"], 1)
            act.activation(xnm[:, 0:8], xmx[:, 0:8], ACT.Sqrt).then_inc(S["hstd_ready"], 1)
            for n in range(8):
                u = first["bT"] + n
                await_filled(act, u)
                if n == 0:
                    act.wait_ge(S["s5_pp"], 1)
                evac(act.activation(E[1][:, 512 * n:512 * n + 512], bank(u)[:, :], ACT.Copy), u)
            for n in range(8):
                u = first["w"] + n
                await_filled(act, u)
                evac(act.activation(E[3][0:GI, 512 * n:512 * n + 512], bank(u)[0:GI, :], ACT.Copy), u)
            act.wait_ge(S["s5_w"], 1)
            act.wait_ge(S["zeros_ready"], 1)
            for j in range(LC):
                act.dma_start(s5T[GI * j:GI * (j + 1), :, GI * j:P], s5Wst[0:GI, :, 0:P - GI * j]).then_inc(S["s5_t"], 16)
            for n in range(4):
                u = first["memKT"] + n
                await_filled(act, u)
                evac(act.activation(memKT[:, 2 * n:2 * n + 2, :].rearrange("p a b -> p (a b)"), bank(u)[:, :], ACT.Copy), u)
            weights("ev0", 0, RING)
            norm("mix_norm0")
            weights_between("ev0", "ev1")
            for n in range(8):
                if n == 4:
                    weights_between("ev1", "ev2")
                u = first["uv"] + n
                await_filled(act, u)
                dst = (Gu if n < 4 else Gv)[:, n % 4, :]
                evac(act.activation(dst, bank(u)[:, :], ACT.Gelu_apprx_tanh), u)
            for n in range(16):
                if n % 4 == 0:
                    weights("ev2", RING + n // 4, RING + n // 4 + 1)
                if n == 0:
                    act.wait_ge(S["ln_mean"], 1)
                a_(act.activation(junk[:, 0:P], Gv[:, n // 4, (n % 4) * P:(n % 4 + 1) * P], ACT.Square,
                                  bias=xnm[:, n:n + 1], accum_out=xsum[:, n:n + 1]), "ln_sq")
            act.wait_ge(S["ln_mean"], 2)
            act.activation(xrec, xsum, ACT.Sqrt).then_inc(S["ln_sq"], 1)
            a_.n["ln_sq"] += 1
            await_filled(act, first["s5u"] + 3)
            copies("yaT", 0, 4, lambda n: xT[:, n, :])
            copies("ucT", 0, 4, lambda n: Uc[:, 8 * n:8 * n + 8, :].rearrange("p g c -> p (g c)"))
            copies("V", 0, 4, lambda n: Vc[:, 8 * n:8 * n + 8, :].rearrange("p g c -> p (g c)"))
            for k in range(4):
                taken(act, first["yaT"] + k)
                act.activation(out0_hi[k], xT[:, k, :], ACT.Copy).then_inc(S["ya_hi"], 1)
            weights("out00", 0, RING)
            act.wait_ge(S["s5_x"], 1)
            for n in range(8):
                u = first["y"] + n
                await_filled(act, u)
                evac(act.activation(Y[:, :, 64 * n:64 * n + 64].rearrange("c j (g i) -> c g j i", g=4),
                                    bank(u)[0:NC, :].rearrange("c (g j i) -> c g j i", g=4, j=LC),
                                    ACT.Gelu_apprx_tanh), u)
            for n in range(4):
                u = first["yT"] + n
                await_filled(act, u)
                evac(act.activation(yT[:, n, :].rearrange("p (c j) -> p j c", j=LC),
                                    bank(u)[:, :].rearrange("p (j c) -> p j c", j=LC), ACT.Copy), u)
            for n in range(4):
                u = first["glu"] + n
                await_filled(act, u)
                evac(act.activation(sg[:, n, :], bank(u)[:, :], ACT.Sigmoid, bias=col("s5_b_glu", n)), u)
            for k in range(4):
                act.wait_ge(S["gated"], k + 1)
                act.activation(out0_hi[4 + k], gated[:, k, :], ACT.Copy).then_inc(S["ya_hi"], 1)
            weights_between("out00", "out01")
            weights_between("out01", None)
            def queries(l, half):
                n = NORMS[f"xa_norm{l}"]
                if half == 0:
                    act.wait_ge(S["rstd_ready"], 2 * l + 1)
                for t in range(TT):
                    u = first[f"q{l}"] + 4 * half + t
                    await_filled(act, u)
                    evac(act.activation(qtok[:, t, half * 512:(half + 1) * 512], bank(u)[:, :], ACT.Copy,
                                        scale=rstd[:, n, t:t + 1]), u)

            def head_squares(l, half):
                for t in range(TT):
                    taken(act, first[f"q{l}"] + 4 * half + t)
                    for n in range(2 * half, 2 * half + 2):
                        a_(act.activation(junk[:, 0:XD], qtok[:, t, n * XD:(n + 1) * XD], ACT.Square,
                                          accum_out=dsq[:, 4 * t + n:4 * t + n + 1]), "hd_sq")

            def attention(l):
                weights(f"wq{l}0", 0, RING)
                norm(f"xa_norm{l}")
                weights_between(f"wq{l}0", f"wq{l}1")
                queries(l, 0)
                head_squares(l, 0)
                weights_between(f"wq{l}1", f"wo{l}0")
                queries(l, 1)
                for k in range(0, KT, 2):
                    u = first[f"qT{l}"] + k
                    await_filled(act, u)
                    evac(act.activation(qT[:, k, :], bank(u)[:, :], ACT.Copy, scale=g2[:, 2 * l:2 * l + 1]), u)
                head_squares(l, 1)
                act.wait_ge(S["hmean_ready"], (2, 5)[l])
                act.activation(dstd[:, 0:16], dsq[:, 0:16], ACT.Sqrt).then_inc(S["hstd_ready"], 1)
                table(ACT.Exp)
                for t in range(TT):
                    for hp in range(2):
                        u = first[f"sc{l}"] + 2 * t + hp
                        act.wait_ge(S["max_ready"], (0, 24)[l] + 2 * t + hp + 1)
                        for n in range(2):
                            c = 4 * t + 2 * hp + n
                            ins = act.activation(prob[:, t, 2 * hp + n, :], bank(u)[:, n * NM:(n + 1) * NM], ACT.Exp,
                                                 bias=xnm[:, c:c + 1], scale=drec[:, c:c + 1], accum_out=xsum[:, c:c + 1])
                        evac(ins, u)
                copies(f"pT{l}", 0, 8, lambda n: pT[:, n // 2, n % 2, :], 2)
                for n in range(8):
                    high_part(first[f"o{l}"] + n, ohi[:, n, :])
                weights_between(f"wo{l}0", f"wo{l}1")
                weights_between(f"wo{l}1", None)

            def experts(l):
                m = M[l]
                norm(f"ffn_norm{l}")
                act.wait_ge(m["gate_args"], 1)
                act.activation(gexp, gsub, ACT.Exp).then_inc(m["gate_exp"], 1)
                act.wait_ge(m["gate_args"], 2)
                act.activation(dexp, dsub, ACT.Exp).then_inc(m["gate_exp"], 1)

                def item(q, par):
                    act.wait_ge(m["hid_filled"], q * 2 + (par + 1))
                    act.activation(silu[par], banks[2 + par][:, 0:FF], ACT.Silu).then_inc(m["silu_ready"], 1)
                    act.wait_ge(m["w2a" if par == 0 else "w2b"], q * 16 + 16)
                    for half in range(2):
                        for k in range(2):
                            act.activation(whi[2 * half + k][:, :], w2s[par][:, k, half * 512:(half + 1) * 512], ACT.Copy)\
                               .then_inc(m["w2_hi"], 1)
                    act.wait_ge(m["ht_filled"], q * 2 + (par + 1))
                    act.activation(hThi[par], banks[4][:, 0:2 * P], ACT.Copy).then_inc(m["ht_hi"], 1)
                    if not isinstance(q, int):
                        act.wait_ge(m[f"y_stored{par}"], q * 16)
                    act.wait_ge(m["y_filled1"], q * 2 + (par + 1))
                    act.activation(yo[par][:, 512:1024], banks[6][:, :], ACT.Copy).then_inc(m["y_ready1"], 1)

                item(0, 0)
                item(0, 1)
                act.wait_ge(m["table_ready"], 1)
                last_pair = act.value_load(tab[0:1, 60:61], min_val=NE // 2 - 1, max_val=NI // 2 - 1)
                with act.Fori(1, last_pair + 1) as q:
                    item(q, 0)
                    item(q, 1)

            attention(0)
            experts(0)
            norm("mix_norm1", lambda: weights("od0", 0, RING))
            act.dma_start(hngain, A["ml_hn_g"][0].partition_broadcast(P)).then_inc(S["wide_in"], 16)
            for dst, src in rope_loads:
                act.dma_start(dst, src).then_inc(S["rope_in"], 16)
            weights_between("od0", "od1")
            copies("dq", 0, 4, lambda n: Dq[:, n, :])
            weights_between("od1", "od2")
            copies("dk", 0, 4, lambda n: Dk[:, n, :])
            weights_between("od2", "od3")
            act.wait_ge(S["hmean_ready"], 3)
            act.activation(dstd, dsq, ACT.Sqrt).then_inc(S["hstd_ready"], 1)

            def taps(c0, c1):
                for ct in range(c0, c1):
                    u = first["qk"] + ct
                    await_filled(act, u)
                    act.activation(QKT[:, ct, :], bank(u)[:, :], ACT.Identity, bias=col("ml_conv_b", ct),
                                   scale=col("ml_conv_w", 24 + ct)).then_inc(S["conv_in"], 1)

            taps(0, 4)
            act.wait_ge(S["ml_args"], 1)
            a_(act.activation(erow, lrow, ACT.Exp, scale=-1.0), "ml_act")
            a_(act.activation(lrow, erow, ACT.Ln, bias=ones[0:4, 0:1]), "ml_act")
            weights_between("od3", "od4")
            act.wait_ge(S["ml_args"], 2)
            act.activation(enrow, enrow, ACT.Exp, scale=-1.0).then_inc(S["ml_rows"], 1)
            taps(4, 8)
            weights_between("od4", "od5")
            for ct in range(8):
                taken(act, first["qk"] + ct)
                act.activation(QKT[:, ct, :], QKT[:, ct, :], ACT.Silu).then_inc(S["qk_ready"], 1)
            for n in range(TT):
                u = first["v"] + n
                await_filled(act, u)
                evac(act.activation(VML[:, n, :, 0:P], bank(u)[:, :].rearrange("p (h d) -> p h d", h=4), ACT.Copy), u)
            weights_between("od5", "od6")
            for n in range(TT):
                u = first["og"] + n
                await_filled(act, u)
                evac(act.activation(SO[:, n, :], bank(u)[:, :], ACT.Sigmoid), u)
            weights_between("od6", "out10")
            copies("dv", 0, 4, lambda n: Dv[:, n, :])
            copies("dT", 0, 8, lambda n: (qdT if n < 4 else kdT)[:, n % 4, :], 2)
            taken(act, first["col"])
            for n in range(H):
                u = first[f"mlh{n}"]
                act.wait_ge(S["diag_ready"], n + 1)
                for s_ in range(TT):
                    i = 4 * n + s_
                    if i >= 2:
                        taken(act, first[f"mlh{(i - 2) // 4}"] + 1 + (i - 2) % 4)
                    d = dts(i)
                    bias = mlc[:, 4 * s_ + n:4 * s_ + n + 1]
                    if s_ < 3:
                        ins = act.activation(d[:, P:T - P * s_], bank(u)[:, P * (s_ + 1):T], ACT.Exp, bias=bias)
                        if s_ == 2:
                            evac(ins, u)
                    act.activation(d[:, 0:P], sdiag[:, P * s_:P * (s_ + 1)], ACT.Exp, bias=bias)\
                       .then_inc(S["dt_ready"], 1)
            def moba_exp(n):
                for t in range(TT):
                    u = first[f"ms{n}"] + t
                    act.wait_ge(S["max_ready"], 8 + 4 * n + t + 1)
                    if n >= 2:
                        for b in range(3):
                            await_filled(act, first[f"mp{n - 2}"] + b)
                    c = 4 * n + t
                    evac(act.activation(pm(n, t), bank(u)[:, 0:P * (t + 1)], ACT.Exp, bias=xnm[:, c:c + 1],
                                        scale=HD_SCALE, accum_out=xsum[:, c:c + 1]), u)

            def moba_turn(n):
                for b, o in ((0, 0), (2, 1024)):
                    u = first[f"mp{n}"] + b
                    w = (512, 512, 256)[b]
                    await_filled(act, u)
                    evac(act.activation(E[4][:, (n % 2) * 1280 + o:(n % 2) * 1280 + o + w], bank(u)[:, 0:w], ACT.Copy), u)
                high_part(first[f"mp{n}"] + 3, xhi[:, 4 + n, :])

            moba_exp(0)
            for n in range(1, H):
                moba_exp(n)
                if n == 1:
                    act.wait_ge(S["hmean_ready"], 4)
                    act.activation(dstd[:, 0:16], dsq[:, 0:16], ACT.Sqrt).then_inc(S["hstd_ready"], 1)
                moba_turn(n - 1)
            moba_turn(H - 1)
            for n in range(4):
                high_part(first["ycT"] + n, xhi[:, n, :])
            weights_between("out10", "out11")
            weights_between("out11", None)
            attention(1)
            experts(1)

        @block.vector
        def _(dve):
            v = Chain(dve, "d_step")
            tt, ts, stt = dve.tensor_tensor, dve.tensor_scalar, dve.scalar_tensor_tensor

            def last(ap, n):
                return ap.unsqueeze(len(ap.shape)).broadcast_to(list(ap.shape) + [n])

            def mid(ap, n):
                return ap.unsqueeze(1).broadcast_to([ap.shape[0], n] + list(ap.shape[1:]))

            def rstd_of(sq, std_, rec, width, s_in, s_out, s_rec=None):
                v(ts(sq, sq, 1.0 / width, EPS, ALU.mult, ALU.add), s_in)
                dve.wait_ge(S[s_out], v.n[s_in])
                v(dve.reciprocal(rec, std_), s_rec)

            def low_part(u, hi, lo, scale=1.0):
                dve.wait_ge(S["x_hi"], two_parts.index(u) + 1)
                evac(stt(lo, bank(u)[:, :], scale, hi.bitcast(F32), ALU.mult, ALU.subtract), u)

            def rstd_of_tokens(name):
                n = NORMS[name]
                dve.wait_ge(S["stat_ready"], 2 + 4 * n)
                rstd_of(ssq[:, n, :], std[:, n, :], rstd[:, n, :], D, "mean_ready", "std_ready",
                        "rstd_ready" if name in LAST_ADD else None)

            def norm(name):
                n = NORMS[name]
                dst = xnE if name == "mix_norm0" else xn
                if name != "mix_norm0" and "xa" not in name:
                    rstd_of_tokens(name)
                if name not in LAST_ADD:
                    for t in range(TT):
                        ts(dst[:, t, :], h[:, t, :], rstd[:, n, t:t + 1], None, ALU.mult).then_inc(S["xn_ready"], 1)
                gain = {"mix": "norm_mix_g", "xa_": "norm_xa_g", "ffn": "norm_ffn_g"}[name[0:3]]
                lo = 8 * int(name[-1])
                if name == "mix_norm0":
                    dve.wait_ge(S["s5_t"], 16 * LC)
                if first[name] in two_parts:
                    for k in range(KT):
                        low_part(first[name] + k, xhi[:, k, :], xlo[{"mix_norm0": "ev", "mix_norm1": "od"}.get(name, "q")][:, k, :],
                                 col(gain, lo + k))
                    if "xa" in name:
                        rstd_of_tokens(name)
                    return
                for k in range(1, KT, 2):
                    u = first[name] + k
                    await_filled(dve, u)
                    evac(ts(xT[:, k, :], bank(u)[:, :], col(gain, lo + k), None, ALU.mult), u)

            def copies(name, n0, n1, dst, step=1):
                for n in range(n0, n1, step):
                    u = first[name] + n
                    await_filled(dve, u)
                    evac(dve.tensor_copy(dst(n), bank(u)[:, :]), u)

            def add_to_h(name):
                for n in range(2):
                    for t in range(TT):
                        u = first[name] + 4 * n + t
                        await_filled(dve, u)
                        hs = h[:, t, n * 512:(n + 1) * 512]
                        evac(tt(hs, bank(u)[:, :], hs, ALU.add), u)

            dve.wait_ge(S["consts_ready"], 1)
            u = first["cols"]
            await_filled(dve, u)
            v(dve.tensor_copy(sm[:, 0:2 * G], bank(u)[:, P:P + 2 * G]))
            v(dve.tensor_copy(dT, bank(u)[0:GI, 2 * P:2 * P + G]))
            evac(dve.tensor_copy(cols[:, 0:NROWS], bank(u)[:, 0:NROWS]), u)
            dve.wait_ge(S["stat_ready"], 2)
            rstd_of(ssq[:, 0, 0:MT], std[:, 0, 0:MT], rstd[:, 0, 0:MT], D, "mean_ready", "std_ready")
            for t in range(MT):
                ts(memtok[:, t, :], memtok[:, t, :], rstd[:, 0, t:t + 1], None, ALU.mult).then_inc(S["xn_ready"], 1)
            taken(dve, u)
            for k in range(0, KT, 2):
                u = first["memT"] + k // 2
                await_filled(dve, u)
                v(ts(memnT[:, k, :], bank(u)[:, 0:NM], col("mem_norm_g", k), None, ALU.mult))
                evac(ts(memnT[:, k + 1, :], bank(u)[:, NM:2 * NM], col("mem_norm_g", k + 1), None, ALU.mult), u)
            for l in range(2):
                v(tt(g2[:, 2 * l:2 * l + 2], cols[:, vec["xa_qn_g"][0] + 2 * l:vec["xa_qn_g"][0] + 2 * l + 2],
                     cols[:, vec["xa_kn_g"][0] + 2 * l:vec["xa_kn_g"][0] + 2 * l + 2], ALU.mult))

            dve.wait_ge(S["s5_in"], 16 * len(s5_loads))
            dve.wait_ge(S["s5_exp"], 1)
            v(tt(are, lamr, step_, ALU.mult))
            v(tt(th, lami, step_, ALU.mult))
            v(ts(turn, th, 1.0 / (2.0 * np.pi), None, ALU.mult))

            def fraction(x, tmp):
                v(ts(tmp, x, ROUND, ROUND, ALU.add, ALU.subtract))
                v(tt(x, x, tmp, ALU.subtract))

            fraction(turn, n1)
            v(ts(t8, turn, float(LC), None, ALU.mult))
            fraction(t8, n1)
            K9 = mid(iof[:, 0:LC + 1], G)
            v(tt(mag, last(are, LC + 1), K9, ALU.mult), "s5_args")
            v(tt(Li, last(turn, LC + 1), K9, ALU.mult))
            fraction(Li, Lt)
            v(stt(Lr, Li, -1.0, Li, ALU.mult, ALU.max))
            v(tt(s5sin, last(t8, NC), mid(iof[:, 0:NC], G), ALU.mult))
            fraction(s5sin, s5cos)
            v(stt(s5cos, s5sin, -1.0, s5sin, ALU.mult, ALU.max), "s5_args")
            dve.wait_ge(S["s5_exp"], 3)
            dve.wait_ge(S["s5_sin"], 2)
            v(tt(Lr, Lr, mag, ALU.mult))
            v(tt(Li, Li, mag, ALU.mult))
            lr1, li1 = Lr[:, :, 1], Li[:, :, 1]
            v(ts(nr, lr1, -1.0, None, ALU.add))
            v(tt(n1, lamr, lamr, ALU.mult))
            v(tt(n2, lami, lami, ALU.mult))
            v(tt(n1, n1, n2, ALU.add))
            v(dve.reciprocal(th, n1))
            for dst, a, b, op in ((Fr, nr, li1, ALU.add), (Fi, li1, nr, ALU.subtract)):
                v(tt(n1, a, lamr, ALU.mult))
                v(tt(n2, b, lami, ALU.mult))
                v(tt(n1, n1, n2, op))
                v(tt(dst, n1, th, ALU.mult))
            dve.wait_ge(S["s5_b2"], 32)
            v(ts(B2, B2, nsgn[:, 0:1], None, ALU.mult))
            for n, (c, sc) in enumerate(((C1, sgn[:, 0:1]), (C2, -1.0))):
                u = first["ct"] + n
                await_filled(dve, u)
                evac(ts(c, bank(u)[:, :].rearrange("p (g i) -> p g i", g=G), sc, None, ALU.mult), u)
                taken(dve, u)
            tA, tB = v3(E[4], G, 0, 512), v3(E[4], G, 512, 1024)

            def combine(dst, p, a, q, b, op=ALU.add):
                tt(tA, last(p, GI), a, ALU.mult)
                v(tt(tB, last(q, GI), b, ALU.mult))
                v(tt(dst, tA, tB, op))

            rstd_of_tokens("mix_norm0")
            combine(BB1, Fr, B1, Fi, B2)
            combine(BB2, Fr, B2, Fi, B1, ALU.subtract)
            for j in range(LC):
                combine(s5Qn[:, :, j, :], Lr[:, :, LC - 1 - j], BB1, Li[:, :, LC - 1 - j], BB2)
            dve.nop().then_inc(S["s5_bb"], 1)
            for k in range(LC + 1):
                combine(s5PP[:, :, k, :], Lr[:, :, k], C1, Li[:, :, k], C2)
            dve.nop().then_inc(S["s5_pp"], 1)
            dve.wait_ge(S["hd_sq"], 8)
            rstd_of(xmx[:, 0:8], xnm[:, 0:8], xrec[:, 0:8], XD, "hmean_ready", "hstd_ready")
            for n in range(8):
                k = memtok[:, n // 4, (n % 4) * XD:(n % 4 + 1) * XD]
                ins = ts(k, k, xrec[:, n:n + 1], None, ALU.mult)
            ins.then_inc(S["memk_norm"], 1)
            taken_all(dve, "w", 8)
            dI = v3(E[4], G, 0, 512)[0:GI]
            v(tt(dI, mid(ident[0:GI, 0:GI], G), last(dT, GI), ALU.mult))
            W0 = s5Wst[0:GI, :, 0:GI]
            v(tt(W0, W0, dI, ALU.add), "s5_w")

            norm("mix_norm0")
            G16 = E[4][:, 2048:4096].rearrange("p (n d) -> p n d", n=16)
            taken_all(dve, "uv", 8)
            v(dve.tensor_reduce(xmx, G16, AX.X, ALU.add))
            v(ts(xnm, xmx, -1.0 / HD, None, ALU.mult), "ln_mean")
            dve.wait_ge(S["ln_sq"], 16)
            v(ts(xsum, xsum, 1.0 / HD, EPS, ALU.mult, ALU.add), "ln_mean")
            dve.wait_ge(S["ln_sq"], 17)
            v(dve.reciprocal(xmx, xrec))
            for n in range(16):
                ins = ts(G16[:, n, :], G16[:, n, :], xnm[:, n:n + 1], xmx[:, n:n + 1], ALU.add, ALU.mult)
            v(ins)
            dve.wait_ge(S["lngain_in"], 16)
            tt(Gv, Gv, mid(lngain, 4), ALU.mult).then_inc(S["vh_ready"], 1)
            await_filled(dve, first["s5u"] + 3)
            copies("s5u", 0, 4, lambda n: uT[:, n, :])
            copies("ws", 0, 1, lambda n: wsT[:, :])
            dve.wait_ge(S["small_in"], 16 * len(small))
            for n in range(H):
                u = first["mixed"] + n
                await_filled(dve, u)
                g = Gu[:, :, n * P:(n + 1) * P]
                evac(stt(g, bank(u)[:, :].rearrange("p (c d) -> p c d", c=4), gbs[:, n:n + 1], g, ALU.add, ALU.mult), u)
            for j in range(LC):
                u = first["uj"] + j
                await_filled(dve, u)
                evac(dve.tensor_copy(U[:, :, j, :], bank(u)[0:NC, :].rearrange("c (g i) -> c g i", g=G)), u)
            dve.wait_ge(S["s5_sin"], 4)
            for n in range(4):
                u = first["Vsw"] + n
                await_filled(dve, u)
                evac(tt(Vs[:, 8 * n:8 * n + 8, :], bank(u)[:, :].rearrange("p (g c) -> p g c", g=8),
                        s5sin[:, 8 * n:8 * n + 8, :], ALU.mult), u)
            taken_all(dve, "Vsw", 4)
            v(tt(Vc, Vc, s5cos, ALU.mult))
            v(tt(Vs, Vs, Vc, ALU.add))
            rho = v3(E[1], G, 0, 2048)
            v(dve.tensor_copy(rho, last(rho8, NC)))
            v(dve.memset(rho[:, :, 0:1], 0.0))
            v(dve.tensor_tensor_scan(E[4][:, 2048:4096], E[1][:, 0:2048], E[4][:, 0:2048], 0.0, ALU.mult, ALU.add))
            v(tt(Vs, Sc, s5sin, ALU.mult), "s5_scan")
            v(tt(Vc, Sc, s5cos, ALU.mult))
            v(dve.memset(Sc[:, :, 0:1], 0.0))
            for n in range(4):
                u = first["Xp"] + n
                await_filled(dve, u)
                r = slice(8 * n, 8 * n + 8)
                evac(tt(Sc[:, r, 1:NC], Vc[:, r, 0:NC - 1],
                        bank(u)[:, :].rearrange("p (g c) -> p g c", g=8)[:, :, 0:NC - 1], ALU.subtract), u)
            taken_all(dve, "Xp", 4)
            dve.nop().then_inc(S["s5_x"], 1)
            for k in range(4):
                dve.wait_ge(S["ya_hi"], k + 1)
                tt(xhi[:, k, :], xT[:, k, :], out0_hi[k].bitcast(F32), ALU.subtract).then_inc(S["ya_lo"], 1)
            for n in range(4):
                taken(dve, first["glu"] + n)
                tt(gated[:, n, :], sg[:, n, :], yT[:, n, :], ALU.mult).then_inc(S["gated"], 1)
            for k in range(4):
                dve.wait_ge(S["ya_hi"], 4 + k + 1)
                tt(xhi[:, 4 + k, :], gated[:, k, :], out0_hi[4 + k].bitcast(F32), ALU.subtract).then_inc(S["ya_lo"], 1)
            add_to_h("out0")

            def attention(l):
                norm(f"xa_norm{l}")
                for k in range(1, KT, 2):
                    u = first[f"qT{l}"] + k
                    await_filled(dve, u)
                    evac(ts(qT[:, k, :], bank(u)[:, :], g2[:, 2 * l + 1:2 * l + 2], None, ALU.mult), u)

                dve.wait_ge(S["hd_sq"], 8 + 16 * l + 16)
                rstd_of(dsq[:, 0:16], dstd[:, 0:16], drec[:, 0:16], XD, "hmean_ready", "hstd_ready")
                v(ts(drec[:, 0:16], drec[:, 0:16], XA_SCALE, None, ALU.mult))

                def maxima(n):
                    u = first[f"sc{l}"] + n
                    await_filled(dve, u)
                    v(dve.tensor_reduce(xmx[:, 2 * n:2 * n + 2], bank(u)[:, :].rearrange("p (a m) -> p a m", a=2),
                                        AX.X, ALU.max))
                    v(stt(xnm[:, 2 * n:2 * n + 2], xmx[:, 2 * n:2 * n + 2], -1.0, drec[:, 2 * n:2 * n + 2], ALU.mult,
                          ALU.mult), "max_ready")

                def normalise(n):
                    taken(dve, first[f"sc{l}"] + n)
                    v(dve.reciprocal(xrec[:, 2 * n:2 * n + 2], xsum[:, 2 * n:2 * n + 2]))
                    for a in range(2):
                        p_ = prob[:, n // 2, 2 * (n % 2) + a, :]
                        ins = ts(p_, p_, xrec[:, 2 * n + a:2 * n + a + 1], None, ALU.mult)
                    ins.then_inc(S["probs"], 1)

                maxima(0)
                for n in range(1, 8):
                    maxima(n)
                    normalise(n - 1)
                normalise(7)
                copies(f"pT{l}", 1, 8, lambda n: pT[:, n // 2, n % 2, :], 2)
                for n in range(8):
                    low_part(first[f"o{l}"] + n, ohi[:, n, :], xlo["o"][:, n, :])
                add_to_h(f"wo{l}")

            def first_max(x, mx, eq, onehot):
                v(dve.tensor_reduce(mx, x, AX.X, ALU.max))
                v(tt(eq, x, last(mx, 4), ALU.is_equal))
                v(tt(eq, eq, mid(rev4, 4), ALU.mult))
                v(dve.tensor_reduce(posf[:, 0:4], eq, AX.X, ALU.max))
                v(tt(onehot, eq, last(posf[:, 0:4], 4), ALU.is_equal))

            def experts(l):
                m = M[l]
                norm(f"ffn_norm{l}")
                v(ts(rev4, iof[:, 0:4], -1.0, 4.0, ALU.mult, ALU.add))
                v(ts(full, iof[:, 0:NX], float(P), float(P), ALU.mult, ALU.add))
                v(ts(base, iof[:, 0:NE], float(P), None, ALU.mult))
                v(dve.memset(zero, 0.0))
                u = first[f"route{l}"]
                await_filled(dve, u)
                dve.wait_ge(S["small_in"], 16 * len(small))
                evac(tt(lg, bank(u)[:, 0:80].rearrange("p (t n) -> p t n", t=4), last(rstd[:, NORMS[f"ffn_norm{l}"], :], 20),
                        ALU.mult), u)
                taken(dve, u)
                v(tt(lg, lg, mid(rbias[:, l, :], 4), ALU.add))
                gl = lg[:, :, 0:4]
                first_max(gl, gmax, geq, gf)
                v(tt(gsub, gl, last(gmax, 4), ALU.subtract))
                dve.nop().then_inc(m["gate_args"], 1)
                el = lg[:, :, 4:20].rearrange("p t (g e) -> p t g e", g=4)
                s16 = sel16.rearrange("p t (g e) -> p t g e", g=4)
                v(tt(s16, el, last(gf, 4), ALU.mult))
                v(dve.tensor_reduce(sel, sel16.rearrange("p t (g e) -> p t e g", g=4), AX.X, ALU.add))
                first_max(sel, m1, tmp4, f1)
                v(stt(sel2, f1, -BIG, sel, ALU.mult, ALU.add))
                first_max(sel2, m2, tmp4, f2)
                v(tt(dsub, m2, m1, ALU.subtract))
                dve.nop().then_inc(m["gate_args"], 1)
                for mm, f in zip(M12, (f1, f2)):
                    v(tt(mm.rearrange("p t (g e) -> p t g e", g=4), last(gf, 4),
                         f.unsqueeze(2).broadcast_to([P, 4, 4, 4]), ALU.mult))
                tt(msum[:, :, :], M12[0], M12[1], ALU.add).then_inc(m["msum_ready"], 1)
                dve.wait_ge(m["gate_exp"], 2)
                v(dve.tensor_reduce(gs, gexp, AX.X, ALU.add))
                v(dve.reciprocal(gp, gs))
                v(ts(gs, dexp, 1.0, None, ALU.add))
                v(dve.reciprocal(gmax, gs))
                v(tt(gate[:, 0, :], gmax, gp, ALU.mult))
                v(tt(gate[:, 1, :], gate[:, 0, :], dexp, ALU.mult))
                u = first[f"rank{l}"]
                await_filled(dve, u)
                evac(dve.tensor_copy(rank[:, :], bank(u)[:, 0:5 * NE]), u)
                taken(dve, u)
                R, cnt = rank[:, 0:4 * NE].rearrange("p (t e) -> p t e", t=4), rank[:, 4 * NE:5 * NE]
                v(tt(c3(more), last(cnt, NX), mid(full, NE), ALU.is_gt))
                v(dve.tensor_tensor_scan(cum, more, zero, 0.0, ALU.add, ALU.add))
                v(tt(xbase, c3(cum)[:, :, 0], c3(more)[:, :, 0], ALU.subtract))
                v(ts(xbase, xbase, float(P), float((NE - 1) * P), ALU.mult, ALU.add))
                v(tt(base, base, xbase, ALU.subtract))
                v(ts(RB, R, float(P), None, ALU.is_lt))
                v(tt(RB, RB, mid(base, 4), ALU.mult))
                v(tt(RB, RB, R, ALU.add))
                v(tt(RB, RB, mid(xbase, 4), ALU.add))
                for j in range(2):
                    v(tt(sel16, M12[j], RB, ALU.mult))
                    v(dve.tensor_reduce(posf[:, 4 * j:4 * j + 4], sel16, AX.X, ALU.add))
                v(dve.tensor_copy(pos[:, :, :], posf.rearrange("p (j t) -> p j t", j=2)))
                posw = pos[:, :, :].rearrange("p j t -> p (j t)")
                v(ts(itemi[:, :], posw, P.bit_length() - 1, None, ALU.logical_shift_right))
                v(dve.tensor_copy(itemf, itemi[:, :]))
                v(stt(slotf, itemf, -float(P), posf, ALU.mult, ALU.add))
                v(tt(slot1h, mid(iof[:, :], 8), last(slotf, P), ALU.is_equal))
                v(tt(item1h, mid(iof[:, 0:NI], 8), last(itemf, NI), ALU.is_equal))
                tt(item1h, item1h.bitcast(F32), last(tokf[:, :], NI), ALU.mult).then_inc(m["onehots_ready"], 1)
                u = first[f"idx{l}"]
                await_filled(dve, u)
                evac(dve.tensor_copy(slots[:, :], bank(u)[:, 0:NI]), u)
                taken(dve, u)
                dve.nop().then_inc(m["slots_ready"], 1)
                dve.nop().then_inc(m["pos_ready"], 1)
                v(dve.tensor_copy(c3(epx), last(iof[0:1, 0:NE], NX)))
                v(ts(nth, iof[0:1, 0:8], 1.0, None, ALU.add))
                b1, b2 = v3(big1, 8), v3(big2, 8)
                v(tt(b1, mid(cum[0:1, :], 8), last(nth, NE * NX), ALU.is_equal))
                v(tt(b1, b1, mid(more[0:1, :], 8), ALU.mult))
                v(tt(b2, b1, mid(epx, 8), ALU.mult))
                v(dve.memset(tabf, 0.0))
                v(dve.tensor_copy(tabf[:, 0:NE], iof[0:1, 0:NE]))
                v(dve.tensor_reduce(tabf[:, NE:NE + 8], b2, AX.X, ALU.add))
                v(ts(half_, iof[0:1, 0:4], 2.0, 1.0, ALU.mult, ALU.add))
                v(tt(half_, cum[0:1, NE * NX - 1:NE * NX].broadcast_to([1, 4]), half_, ALU.is_ge))
                v(dve.tensor_reduce(tabf[:, 60:61], half_, AX.X, ALU.add))
                v(ts(tabf[:, 60:61], tabf[:, 60:61], float(NE // 2 - 1), None, ALU.add))
                v(dve.tensor_copy(tab[0:1, :], tabf))
                dve.nop().then_inc(m["table_ready"], 1)
                ga = vec["norm_ffn_g"][0] + 8 * l

                def turn(q, par):
                    for b in range(2):
                        dve.wait_ge(m["xt_filled"], q * 4 + (2 * par + b + 1))
                        tt(xgT[par][:, 4 * b:4 * b + 4, :], banks[b][:, :].rearrange("p (k t) -> p k t", k=4),
                           last(cols[:, ga + 4 * b:ga + 4 * b + 4], P), ALU.mult).then_inc(m["xt_ready"], 1)

                def hidden(q, par):
                    dve.wait_ge(m["silu_ready"], q * 2 + (par + 1))
                    tt(hid[par], silu[par], banks[2 + par][:, FF:2 * FF], ALU.mult).then_inc(m["hid_ready"], 1)

                def low_parts(q, par):
                    for half in range(2):
                        for k in range(2):
                            c = 2 * half + k
                            dve.wait_ge(m["w2_hi"], q * 8 + (4 * par + c + 1))
                            tt(wlo[c][:, :], w2s[par][:, k, half * 512:(half + 1) * 512], whi[c][:, :].bitcast(F32),
                               ALU.subtract).then_inc(m["w2_lo"], 1)
                    dve.wait_ge(m["ht_hi"], q * 2 + (par + 1))
                    tt(hTlo[par], banks[4][:, 0:2 * P], hThi[par].bitcast(F32), ALU.subtract).then_inc(m["ht_ready"], 1)

                def output(q, par):
                    if not isinstance(q, int):
                        dve.wait_ge(m[f"y_stored{par}"], q * 16)
                    dve.wait_ge(m["y_filled0"], q * 2 + (par + 1))
                    dve.tensor_copy(yo[par][:, 0:512], banks[5][:, :]).then_inc(m["y_ready0"], 1)

                turn(0, 0)
                turn(0, 1)
                for par in range(2):
                    hidden(0, par)
                    low_parts(0, par)
                    turn(1, par)
                    output(0, par)
                last_pair = dve.value_load(tab[0:1, 60:61], min_val=NE // 2 - 1, max_val=NI // 2 - 1)
                with dve.Fori(1, last_pair) as q:
                    for par in range(2):
                        hidden(q, par)
                        low_parts(q, par)
                        turn(q + 1, par)
                        output(q, par)
                for par in range(2):
                    hidden(last_pair, par)
                    low_parts(last_pair, par)
                    output(last_pair, par)
                for t in range(TT):
                    dve.wait_ge(m[f"y_gathered{t}"], 32)
                    for j in range(2):
                        if j:
                            dve.wait_ge(m["h_half"], t + 1)
                        stt(h[:, t, :], Yg[j][:, t, :], gate[:, j, t:t + 1], h[:, t, :], ALU.mult, ALU.add)\
                            .then_inc(m["h_combined" if j else "h_half"], 1)

            attention(0)
            experts(0)
            norm("mix_norm1")
            v(dve.memset(VML[:, :, :, P:P + 1], 1.0))
            u = first["if"]
            await_filled(dve, u)
            evac(tt(ifg, bank(u)[:, 0:32].rearrange("p (t n) -> p t n", t=4), mid(ifb[:, :], 4), ALU.add), u)
            taken_all(dve, "dq", 4)
            taken_all(dve, "dk", 4)
            dve.wait_ge(S["rope_in"], 16 * len(rope_loads))
            for n, d in enumerate((E[1][:, 0:2048], E[1][:, 2048:4096])):
                v(tt(E[4][:, 0:2048], d, d, ALU.mult))
                v(dve.tensor_reduce(dsq[:, 16 * n:16 * n + 16], v3(E[4], 16, 0, 2048), AX.X, ALU.add))
            rstd_of(dsq, dstd, drec, HD, "hmean_ready", "hstd_ready")
            def rotate(n):
                d = E[1][:, 2048 * n:2048 * n + 2048]
                dd = v3(d, 16)
                v(tt(dd, dd, last(drec[:, 16 * n:16 * n + 16], P), ALU.mult))
                v(tt(dd, dd, mid(dgain[n], 16), ALU.mult))
                x4 = d.rearrange("p (t h d) -> p t h d", t=4, h=4)
                x1, x2 = x4[:, :, :, 0:64], x4[:, :, :, 64:128]
                ca = ropec.unsqueeze(2).broadcast_to([P, 4, 4, 64])
                sa = ropes.unsqueeze(2).broadcast_to([P, 4, 4, 64])
                r = [E[4][:, 1024 * i:1024 * i + 1024].rearrange("p (t h d) -> p t h d", t=4, h=4) for i in range(4)]
                tt(r[0], x1, ca, ALU.mult)
                tt(r[1], x2, sa, ALU.mult)
                tt(r[2], x1, sa, ALU.mult)
                v(tt(r[3], x2, ca, ALU.mult))
                tt(x1, r[0], r[1], ALU.subtract)
                v(tt(x2, r[2], r[3], ALU.add))

            def convolve(c0, c1):
                for ct in range(c0, c1):
                    u = first["qk"] + ct
                    dve.wait_ge(S["conv_in"], ct + 1)
                    for k in range(1, 4):
                        o = QKT[:, ct, k:T]
                        ins = stt(o, bank(u)[:, 0:T - k], col("ml_conv_w", 8 * (3 - k) + ct), o, ALU.mult, ALU.add)
                        if k < 3:
                            v(ins)
                    evac(ins, u)

            for n, r in enumerate((Irow, Frow)):
                u = first["ifT"] + n
                await_filled(dve, u)
                evac(dve.tensor_copy(r, bank(u)[0:4, :]), u)
                taken(dve, u)
            v(stt(lrow, Frow, -1.0, Frow, ALU.mult, ALU.max), "ml_args")
            v(ts(Frow, Frow, 0.0, None, ALU.min))
            convolve(0, 4)
            dve.wait_ge(S["ml_act"], 2)
            v(tt(Frow, Frow, lrow, ALU.subtract))
            v(dve.memset(erow, 0.0))
            v(dve.tensor_tensor_scan(Brow, Frow, erow, 0.0, ALU.add, ALU.add))
            v(tt(arow, Irow, Brow, ALU.subtract))
            v(dve.tensor_tensor_scan(Mrow, arow, arow, 0.0, ALU.max, ALU.max))
            v(ts(nMrow, Mrow, -1.0, None, ALU.mult))
            v(tt(enrow, Brow, Mrow, ALU.add), "ml_args")
            rotate(0)
            convolve(4, 8)
            u = first["col"]
            await_filled(dve, u)
            evac(dve.tensor_copy(mlc, bank(u)[:, 0:32]), u)
            taken(dve, u)
            rotate(1)
            dve.nop().then_inc(S["d_norm"], 1)
            copies("dT", 1, 8, lambda n: (qdT if n < 4 else kdT)[:, n % 4, :], 2)
            for n in range(H):
                u = first[f"mlh{n}"]
                await_filled(dve, u)
                if n:
                    dve.wait_ge(S["dt_ready"], 4 * n)
                v(tt(v3(sdiag, 4), bank(u)[:, :].rearrange("p (s t) -> p s t", s=4), mid(after[:], 4), ALU.add),
                  "diag_ready")
                if n == 2:
                    for t in range(TT):
                        await_filled(dve, first["num0"] + t)
                for s_ in range(TT):
                    u = first[f"mlh{n}"] + 1 + s_
                    await_filled(dve, u)
                    dve.wait_ge(S["dt_ready"], 4 * n + s_ + 1)
                    evac(stt(wts(n, s_), bank(u)[:, 0:T - P * s_], HD_SCALE, dts(4 * n + s_)[:, 0:T - P * s_],
                             ALU.mult, ALU.mult), u)
                if n % 2 == 0:
                    continue
                for t in range(TT):
                    u = first[f"num{n // 2}"] + t
                    await_filled(dve, u)
                    b = bank(u)[:, :].rearrange("p (a c) -> p a c", a=2)
                    dn = st[:, 228:230]
                    v(stt(dn, b[:, :, P], -1.0, mlc[:, 16 + 4 * t + n - 1:16 + 4 * t + n + 1], ALU.mult, ALU.max))
                    v(tt(dn, b[:, :, P], dn, ALU.max))
                    v(dve.reciprocal(st[:, 230:232], dn))
                    for a in range(2):
                        ins = ts(hh[:, t, (n - 1 + a) * P:(n + a) * P], b[:, a, 0:P], st[:, 230 + a:231 + a], None, ALU.mult)
                    evac(ins, u)
                    taken(dve, u)
            def moba_max(n):
                for t in range(TT):
                    u = first[f"ms{n}"] + t
                    await_filled(dve, u)
                    c = 4 * n + t
                    v(tt(bank(u)[:, P * t:P * (t + 1)], bank(u)[:, P * t:P * (t + 1)], before[:], ALU.add))
                    v(dve.tensor_reduce(xmx[:, c:c + 1], bank(u)[:, 0:P * (t + 1)], AX.X, ALU.max))
                    v(ts(xnm[:, c:c + 1], xmx[:, c:c + 1], -HD_SCALE, None, ALU.mult), "max_ready")

            def moba_probs(n):
                for t in range(TT):
                    taken(dve, first[f"ms{n}"] + t)
                    c = 4 * n + t
                    v(dve.reciprocal(xrec[:, c:c + 1], xsum[:, c:c + 1]))
                    ts(pm(n, t), pm(n, t), xrec[:, c:c + 1], None, ALU.mult).then_inc(S["mo_probs"], 1)

            def moba_turn(n):
                u = first[f"mp{n}"] + 1
                await_filled(dve, u)
                o = (n % 2) * 1280 + 512
                evac(dve.tensor_copy(E[4][:, o:o + 512], bank(u)[:, :]), u)
                low_part(first[f"mp{n}"] + 3, xhi[:, 4 + n, :], xlo["out1"][:, n, :])

            moba_max(0)
            for n in range(1, H):
                moba_probs(n - 1)
                if n == 2:
                    dve.wait_ge(S["hstd_ready"], 4)
                    dve.reciprocal(drec[:, 0:16], dstd[:, 0:16]).then_inc(S["hh_rstd"], 1)
                moba_max(n)
                if n == 1:
                    dve.wait_ge(S["hh_sq"], 1)
                    v(dve.tensor_reduce(dsq[:, 0:16], v3(E[1], 16, 2048, 4096), AX.X, ALU.add))
                    v(ts(dsq[:, 0:16], dsq[:, 0:16], 1.0 / HD, EPS, ALU.mult, ALU.add), "hmean_ready")
                moba_turn(n - 1)
            moba_probs(H - 1)
            moba_turn(H - 1)
            for n in range(4):
                low_part(first["ycT"] + n, xhi[:, n, :], xlo["out1"][:, 4 + n, :])
            add_to_h("out1")
            attention(1)
            experts(1)


_INS = ["x", "mem", "mem_norm_g", "w_mem_kv", "norm_mix_g", "norm_xa_g", "norm_ffn_g", "xa_wq", "xa_wo", "xa_qn_g",
        "xa_kn_g", "moe_w_grp", "moe_b_grp", "moe_w_exp", "moe_b_exp", "moe_w1", "moe_w3", "moe_w2", "ev_w_in",
        "ev_w_out", "gm_ws", "gm_bs", "gm_ln_g", "s5_lam_re", "s5_lam_im", "s5_b_re", "s5_b_im", "s5_c_re", "s5_c_im",
        "s5_d", "s5_log_step", "s5_w_glu", "s5_b_glu", "od_w_in", "od_w_out", "ml_conv_w", "ml_conv_b", "ml_b_if",
        "ml_hn_g", "mb_qn_g", "mb_kn_g"]


def rope_tables(tokens, half, theta=10000.0):
    freq = np.float32(theta) ** (-np.arange(half, dtype=np.float32) / np.float32(half))
    angle = np.arange(tokens, dtype=np.float32)[:, None] * freq[None, :].astype(np.float32)
    return np.cos(angle).astype(np.float32), np.sin(angle).astype(np.float32)


def kernel(**inputs):
    import concourse.bacc as bacc
    from concourse.bass_utils import run_bass_kernel_spmd

    nc = bacc.Bacc("TRN2", target_bir_lowering=False, num_devices=1)
    arrays, args = {}, {}
    for name in _INS:
        arrays[f"in_{name}"] = np.ascontiguousarray(inputs[name])
    arrays["in_rope_cos"], arrays["in_rope_sin"] = rope_tables(512, 64)
    for name, a in arrays.items():
        args[name[3:]] = nc.dram_tensor(name, a.shape, mybir.dt.from_np(a.dtype), kind="ExternalInput").ap()
    out = nc.dram_tensor("out_h", (1, 512, 1024), F32, kind="ExternalOutput").ap()
    program(nc, args, out)
    r = run_bass_kernel_spmd(nc, [arrays], core_ids=[0])
    return r.results[0]["out_h"]
```
